# Optimizing a Trainium2 kernel written in Bass

```python
import math
import jax, jax.numpy as jnp
from jax import lax
import numpy as np

D_MODEL = 1024
BATCH = 1
SEQ = 512
DEPTH = 2

N_MIXERS = 2
N_SSD_LAYERS = (DEPTH + N_MIXERS - 1) // N_MIXERS
N_LRU_LAYERS = DEPTH // N_MIXERS
SSD_EXPAND = 2
SSD_D_INNER = SSD_EXPAND * D_MODEL
SSD_HEADDIM = 64
SSD_HEADS = SSD_D_INNER // SSD_HEADDIM
SSD_GROUPS = 4
SSD_HPG = SSD_HEADS // SSD_GROUPS
SSD_D_STATE = 128
SSD_CONV = 4
SSD_CHUNK = 128
SSD_CONV_DIM = SSD_D_INNER + 2 * SSD_GROUPS * SSD_D_STATE
SSD_IN_DIM = SSD_D_INNER + SSD_CONV_DIM + SSD_HEADS
LRU_WIDTH = 1280
LRU_HEADS = 10
LRU_BLOCK = LRU_WIDTH // LRU_HEADS
LRU_CONV = 4
LRU_C = 8.0
D_FF = 4 * D_MODEL
FFN_CONV = 3
EPS = 1e-6


def rmsnorm(x, w):
    xf = x.astype(jnp.float32)
    y = xf * lax.rsqrt(jnp.mean(xf * xf, axis=-1, keepdims=True) + EPS)
    return (y * w.astype(jnp.float32)).astype(x.dtype)

def causal_dwconv(x, w, b):
    k = w.shape[0]
    s = x.shape[1]
    xp = jnp.pad(x, ((0, 0), (k - 1, 0), (0, 0)))
    y = b
    for j in range(k):
        y = y + xp[:, j:j + s, :] * w[j]
    return y

def ssd_chunked_scan(xh, dt, a, bm, cm):
    bsz, s, h, p = xh.shape
    nc = s // SSD_CHUNK
    xdt = (xh * dt[..., None]).reshape(bsz, nc, SSD_CHUNK, SSD_GROUPS, SSD_HPG, p)
    da = (dt * a).reshape(bsz, nc, SSD_CHUNK, SSD_GROUPS, SSD_HPG)
    bc = bm.reshape(bsz, nc, SSD_CHUNK, SSD_GROUPS, SSD_D_STATE)
    cc = cm.reshape(bsz, nc, SSD_CHUNK, SSD_GROUPS, SSD_D_STATE)
    cs = jnp.moveaxis(jnp.cumsum(da, axis=2), 2, -1)
    tri = jnp.tril(jnp.ones((SSD_CHUNK, SSD_CHUNK), dtype=bool))
    decay_in = jnp.exp(jnp.where(tri, cs[..., :, None] - cs[..., None, :], -jnp.inf))
    cb = jnp.einsum('bclgn,bcsgn->bcgls', cc, bc)
    scores = cb[:, :, :, None] * decay_in
    y_diag = jnp.einsum('bcgels,bcsgep->bclgep', scores, xdt)
    decay_out = jnp.moveaxis(jnp.exp(cs[..., -1:] - cs), -1, 2)
    states = jnp.einsum('bclgn,bclgep->bcgepn', bc, xdt * decay_out[..., None])
    tot = cs[..., -1]
    inc = jnp.moveaxis(jnp.cumsum(tot, axis=1), 1, -1)
    exc = inc - jnp.moveaxis(tot, 1, -1)
    stri = jnp.tril(jnp.ones((nc, nc), dtype=bool), -1)
    decay_chunk = jnp.exp(jnp.where(stri, exc[..., :, None] - inc[..., None, :], -jnp.inf))
    entering = jnp.einsum('bgezc,bcgepn->bzgepn', decay_chunk, states)
    state_decay = jnp.moveaxis(jnp.exp(cs), -1, 2)
    y_off = jnp.einsum('bclgn,bcgepn->bclgep', cc, entering) * state_decay[..., None]
    return (y_diag + y_off).reshape(bsz, s, h, p)

def gated_group_rmsnorm(y, z, w):
    bsz, s, d = y.shape
    g = (y * jax.nn.silu(z.astype(jnp.float32))).reshape(bsz, s, SSD_GROUPS, d // SSD_GROUPS)
    g = g * lax.rsqrt(jnp.mean(g * g, axis=-1, keepdims=True) + EPS)
    return g.reshape(bsz, s, d) * w.astype(jnp.float32)

def ssd_mixer(u, w_in, conv_w, conv_b, dt_bias, a_log, d_skip, norm_w, w_out):
    bsz, s, _ = u.shape
    proj = u @ w_in
    z = proj[..., :SSD_D_INNER]
    xbc = proj[..., SSD_D_INNER:SSD_D_INNER + SSD_CONV_DIM]
    dt_raw = proj[..., SSD_D_INNER + SSD_CONV_DIM:]
    xbc = jax.nn.silu(causal_dwconv(xbc, conv_w, conv_b)).astype(jnp.float32)
    xs = xbc[..., :SSD_D_INNER].reshape(bsz, s, SSD_HEADS, SSD_HEADDIM)
    bm = xbc[..., SSD_D_INNER:SSD_D_INNER + SSD_GROUPS * SSD_D_STATE].reshape(bsz, s, SSD_GROUPS, SSD_D_STATE)
    cm = xbc[..., SSD_D_INNER + SSD_GROUPS * SSD_D_STATE:].reshape(bsz, s, SSD_GROUPS, SSD_D_STATE)
    dt = jax.nn.softplus(dt_raw.astype(jnp.float32) + dt_bias.astype(jnp.float32))
    a = -jnp.exp(a_log.astype(jnp.float32))
    y = ssd_chunked_scan(xs, dt, a, bm, cm)
    y = y + d_skip.astype(jnp.float32)[:, None] * xs
    y = gated_group_rmsnorm(y.reshape(bsz, s, SSD_D_INNER), z, norm_w)
    return (y.astype(u.dtype) @ w_out).astype(u.dtype)

def _linear_combine(c1, c2):
    a1, b1 = c1
    a2, b2 = c2
    return a1 * a2, a2 * b1 + b2

def rglru_mixer(u, w_in, b_in, conv_w, conv_b, w_gx, b_gx, w_ga, b_ga, lam, w_out, b_out):
    bsz, s, _ = u.shape
    proj = u @ w_in + b_in
    ybr = jax.nn.gelu(proj[..., :LRU_WIDTH].astype(jnp.float32))
    xbr = causal_dwconv(proj[..., LRU_WIDTH:], conv_w, conv_b)
    xh = xbr.reshape(bsz, s, LRU_HEADS, LRU_BLOCK)
    gx = jax.nn.sigmoid((jnp.einsum('bshi,hij->bshj', xh, w_gx).reshape(bsz, s, LRU_WIDTH) + b_gx).astype(jnp.float32))
    ga = jax.nn.sigmoid((jnp.einsum('bshi,hij->bshj', xh, w_ga).reshape(bsz, s, LRU_WIDTH) + b_ga).astype(jnp.float32))
    log_a = LRU_C * ga * jax.nn.log_sigmoid(lam.astype(jnp.float32))
    a_t = jnp.exp(log_a)
    mult = jnp.sqrt(-jnp.expm1(2.0 * log_a))
    b_t = mult * gx * xbr.astype(jnp.float32)
    _, h = lax.associative_scan(_linear_combine, (a_t, b_t), axis=1)
    out = (h * ybr).astype(u.dtype) @ w_out + b_out
    return out.astype(u.dtype)

def conv_ffn(u, w_up, conv_w, conv_b, w_down):
    hcv = causal_dwconv(u @ w_up, conv_w, conv_b)
    g = hcv[..., :D_FF]
    v = hcv[..., D_FF:]
    return ((jax.nn.gelu(g.astype(jnp.float32)) * v.astype(jnp.float32)).astype(u.dtype) @ w_down).astype(u.dtype)

def first_inputs(seed: int = 0) -> dict:
    key = jax.random.key(seed)
    ks = jax.random.split(key, 32)
    f32 = jnp.float32

    def nrm(k, shape, scale):
        return scale * jax.random.normal(k, shape, f32)

    def gain(k, shape):
        return 1.0 + 0.1 * jax.random.normal(k, shape, f32)

    na, nb = N_SSD_LAYERS, N_LRU_LAYERS
    dt0 = jnp.exp(jax.random.uniform(ks[9], (na, SSD_HEADS), f32, math.log(1e-3), math.log(1e-1)))
    lam_u = jax.random.uniform(ks[20], (nb, LRU_WIDTH), f32, 0.9, 0.999)
    return {
        'x': jax.random.normal(ks[0], (BATCH, SEQ, D_MODEL), f32),
        'norm_mix_pre': gain(ks[1], (DEPTH, D_MODEL)),
        'norm_mix_post': gain(ks[2], (DEPTH, D_MODEL)),
        'norm_ffn_pre': gain(ks[3], (DEPTH, D_MODEL)),
        'norm_ffn_post': gain(ks[4], (DEPTH, D_MODEL)),
        'ssd_w_in': nrm(ks[5], (na, D_MODEL, SSD_IN_DIM), D_MODEL ** -0.5),
        'ssd_conv_w': nrm(ks[6], (na, SSD_CONV, SSD_CONV_DIM), SSD_CONV ** -0.5),
        'ssd_conv_b': nrm(ks[7], (na, SSD_CONV_DIM), 0.01),
        'ssd_dt_bias': dt0 + jnp.log(-jnp.expm1(-dt0)),
        'ssd_a_log': jnp.log(jax.random.uniform(ks[10], (na, SSD_HEADS), f32, 1.0, 16.0)),
        'ssd_d': gain(ks[11], (na, SSD_HEADS)),
        'ssd_norm': gain(ks[12], (na, SSD_D_INNER)),
        'ssd_w_out': nrm(ks[13], (na, SSD_D_INNER, D_MODEL), SSD_D_INNER ** -0.5),
        'lru_w_in': nrm(ks[14], (nb, D_MODEL, 2 * LRU_WIDTH), D_MODEL ** -0.5),
        'lru_b_in': nrm(ks[15], (nb, 2 * LRU_WIDTH), 0.01),
        'lru_conv_w': nrm(ks[16], (nb, LRU_CONV, LRU_WIDTH), LRU_CONV ** -0.5),
        'lru_conv_b': nrm(ks[17], (nb, LRU_WIDTH), 0.01),
        'lru_w_gx': nrm(ks[18], (nb, LRU_HEADS, LRU_BLOCK, LRU_BLOCK), LRU_BLOCK ** -0.5),
        'lru_b_gx': nrm(ks[19], (nb, LRU_WIDTH), 0.01),
        'lru_w_ga': nrm(ks[21], (nb, LRU_HEADS, LRU_BLOCK, LRU_BLOCK), LRU_BLOCK ** -0.5),
        'lru_b_ga': nrm(ks[22], (nb, LRU_WIDTH), 0.01),
        'lru_lambda': jnp.log(lam_u) - jnp.log1p(-lam_u),
        'lru_w_out': nrm(ks[23], (nb, LRU_WIDTH, D_MODEL), LRU_WIDTH ** -0.5),
        'lru_b_out': nrm(ks[24], (nb, D_MODEL), 0.01),
        'ffn_w_up': nrm(ks[25], (DEPTH, D_MODEL, 2 * D_FF), D_MODEL ** -0.5),
        'ffn_conv_w': nrm(ks[26], (DEPTH, FFN_CONV, 2 * D_FF), FFN_CONV ** -0.5),
        'ffn_conv_b': nrm(ks[27], (DEPTH, 2 * D_FF), 0.01),
        'ffn_w_down': nrm(ks[28], (DEPTH, D_FF, D_MODEL), D_FF ** -0.5),
    }

def first_block(x, norm_mix_pre, norm_mix_post, norm_ffn_pre, norm_ffn_post,
              ssd_w_in, ssd_conv_w, ssd_conv_b, ssd_dt_bias, ssd_a_log, ssd_d, ssd_norm, ssd_w_out,
              lru_w_in, lru_b_in, lru_conv_w, lru_conv_b, lru_w_gx, lru_b_gx, lru_w_ga, lru_b_ga,
              lru_lambda, lru_w_out, lru_b_out,
              ffn_w_up, ffn_conv_w, ffn_conv_b, ffn_w_down):
    for i in range(DEPTH):
        h = rmsnorm(x, norm_mix_pre[i])
        j = i // N_MIXERS
        if i % N_MIXERS == 0:
            m = ssd_mixer(h, ssd_w_in[j], ssd_conv_w[j], ssd_conv_b[j], ssd_dt_bias[j],
                          ssd_a_log[j], ssd_d[j], ssd_norm[j], ssd_w_out[j])
        else:
            m = rglru_mixer(h, lru_w_in[j], lru_b_in[j], lru_conv_w[j], lru_conv_b[j],
                            lru_w_gx[j], lru_b_gx[j], lru_w_ga[j], lru_b_ga[j],
                            lru_lambda[j], lru_w_out[j], lru_b_out[j])
        x = x + rmsnorm(m, norm_mix_post[i])
        h = rmsnorm(x, norm_ffn_pre[i])
        f = conv_ffn(h, ffn_w_up[i], ffn_conv_w[i], ffn_conv_b[i], ffn_w_down[i])
        x = x + rmsnorm(f, norm_ffn_post[i])
    return x


N_EVEN = (DEPTH + 1) // 2
N_ODD = DEPTH // 2

HGRN_DIM = D_MODEL // 2
HGRN_HEAD_DIM = 128
HGRN_HEADS = HGRN_DIM // HGRN_HEAD_DIM
HGRN_CHUNK = 64

S5_DIM = D_MODEL - HGRN_DIM
S5_GROUP = 16
S5_GROUPS = S5_DIM // S5_GROUP
S5_STATE = 64
S5_DT_MIN = 1e-3
S5_DT_MAX = 1e-1

EVEN_IN = 4 * HGRN_DIM + S5_DIM

MLA_HEADS = 8
MLA_Q_RANK = 384
MLA_KV_RANK = 256
MLA_NOPE = 128
MLA_ROPE = 64
MLA_V = 128
MLA_QK = MLA_NOPE + MLA_ROPE
ODD_IN = MLA_Q_RANK + MLA_KV_RANK + MLA_ROPE
ROPE_THETA = 10000.0
Q_BLOCK = 128

D_FF_2 = 2816
CONV_W = 3


def rmsnorm_2(x, g):
    xf = x.astype(jnp.float32)
    y = xf * lax.rsqrt(jnp.mean(xf * xf, axis=-1, keepdims=True) + EPS)
    return (y * g.astype(jnp.float32)).astype(x.dtype)

def hgrn2(q, f, i, g, lb, norm_g):
    f32 = jnp.float32
    B_, S_, _ = q.shape
    H, Dh, C = HGRN_HEADS, HGRN_HEAD_DIM, HGRN_CHUNK
    N = S_ // C
    lb = lb.astype(f32)
    forget = lb + (1.0 - lb) * jax.nn.sigmoid(f.astype(f32))
    key_in = 1.0 - forget

    def heads(t):
        return t.astype(f32).reshape(B_, N, C, H, Dh).transpose(0, 3, 1, 2, 4)

    qh, kh, vh = heads(q), heads(key_in), heads(i)
    b = jnp.cumsum(heads(jnp.log(forget)), axis=3)
    b_last = b[:, :, :, -1:, :]
    qd = qh * jnp.exp(b)
    kd = kh * jnp.exp(-b)
    causal = jnp.tril(jnp.ones((C, C), dtype=bool))
    att = jnp.where(causal, jnp.einsum('bhntd,bhnsd->bhnts', qd, kd), 0.0)
    o_intra = jnp.einsum('bhnts,bhnsv->bhntv', att, vh)
    d_state = jnp.einsum('bhnsd,bhnsv->bhndv', kh * jnp.exp(b_last - b), vh)
    decay = jnp.exp(b_last[:, :, :, 0, :])

    def step(state, inp):
        ds_n, dec_n = inp
        return dec_n[..., None] * state + ds_n, state

    s0 = jnp.zeros((B_, H, Dh, Dh), f32)
    _, s_start = lax.scan(step, s0, (d_state.transpose(2, 0, 1, 3, 4), decay.transpose(2, 0, 1, 3)))
    s_start = s_start.transpose(1, 2, 0, 3, 4)
    o = o_intra + jnp.einsum('bhntd,bhndv->bhntv', qd, s_start)
    o = o.transpose(0, 2, 3, 1, 4).reshape(B_, S_, H, Dh)
    o = o * lax.rsqrt(jnp.mean(o * o, axis=-1, keepdims=True) + EPS) * norm_g.astype(f32).reshape(H, Dh)
    return o.reshape(B_, S_, HGRN_DIM) * jax.nn.silu(g.astype(f32))

def s5(u, a_re, a_im, log_dt, b_re, b_im, c_re, c_im, d_skip, w_glu, b_glu):
    f32 = jnp.float32
    B_, S_, _ = u.shape
    G, P, Hc = S5_GROUPS, S5_STATE, S5_GROUP
    uf = u.astype(f32).reshape(B_, S_, G, Hc)
    ar, ai = a_re.astype(f32), a_im.astype(f32)
    dt = jnp.exp(log_dt.astype(f32))[:, None]
    mag = jnp.exp(ar * dt)
    abar_re, abar_im = mag * jnp.cos(ai * dt), mag * jnp.sin(ai * dt)
    den = ar * ar + ai * ai
    xr, xi = abar_re - 1.0, abar_im
    coef_re = ((xr * ar + xi * ai) / den)[..., None]
    coef_im = ((xi * ar - xr * ai) / den)[..., None]
    br, bi = b_re.astype(f32), b_im.astype(f32)
    bb_re = coef_re * br - coef_im * bi
    bb_im = coef_re * bi + coef_im * br
    bu_re = jnp.einsum('bsgh,gph->bsgp', uf, bb_re)
    bu_im = jnp.einsum('bsgh,gph->bsgp', uf, bb_im)
    a_seq_re = jnp.broadcast_to(abar_re, (1, S_, G, P))
    a_seq_im = jnp.broadcast_to(abar_im, (1, S_, G, P))

    def combine(left, right):
        a1r, a1i, b1r, b1i = left
        a2r, a2i, b2r, b2i = right
        return (a2r * a1r - a2i * a1i, a2r * a1i + a2i * a1r,
                a2r * b1r - a2i * b1i + b2r, a2r * b1i + a2i * b1r + b2i)

    _, _, s_re, s_im = lax.associative_scan(combine, (a_seq_re, a_seq_im, bu_re, bu_im), axis=1)
    y = (jnp.einsum('bsgp,ghp->bsgh', s_re, c_re.astype(f32))
         - jnp.einsum('bsgp,ghp->bsgh', s_im, c_im.astype(f32))
         + d_skip.astype(f32).reshape(G, Hc) * uf)
    z = jax.nn.gelu(y.reshape(B_, S_, S5_DIM))
    return z * jax.nn.sigmoid(z @ w_glu.astype(f32) + b_glu.astype(f32))

def even_mixer(hn, w_in, lb, hgrn_norm_g, a_re, a_im, log_dt, b_re, b_im, c_re, c_im,
               d_skip, w_glu, b_glu, w_out):
    proj = hn @ w_in
    q, f, i, g, u = jnp.split(proj, [HGRN_DIM, 2 * HGRN_DIM, 3 * HGRN_DIM, 4 * HGRN_DIM], axis=-1)
    y_a = hgrn2(q, f, i, g, lb, hgrn_norm_g).astype(hn.dtype)
    y_b = s5(u, a_re, a_im, log_dt, b_re, b_im, c_re, c_im, d_skip, w_glu, b_glu).astype(hn.dtype)
    return jnp.concatenate([y_a, y_b], axis=-1) @ w_out

def rotate(x, cos, sin):
    x1, x2 = jnp.split(x, 2, axis=-1)
    return jnp.concatenate([x1 * cos - x2 * sin, x1 * sin + x2 * cos], axis=-1)

def mla(hn, positions, w_in, q_norm_g, w_uq, kv_norm_g, w_ukv, w_out):
    B_, S_, _ = hn.shape
    H = MLA_HEADS
    proj = hn @ w_in
    cq, ckv, k_rope = jnp.split(proj, [MLA_Q_RANK, MLA_Q_RANK + MLA_KV_RANK], axis=-1)
    q = (rmsnorm_2(cq, q_norm_g) @ w_uq).reshape(B_, S_, H, MLA_QK)
    kv = (rmsnorm_2(ckv, kv_norm_g) @ w_ukv).reshape(B_, S_, H, MLA_NOPE + MLA_V)
    q_nope, q_rope = jnp.split(q, [MLA_NOPE], axis=-1)
    k_nope, v = jnp.split(kv, [MLA_NOPE], axis=-1)
    freqs = ROPE_THETA ** (-jnp.arange(0, MLA_ROPE, 2, dtype=jnp.float32) / MLA_ROPE)
    ang = positions.astype(jnp.float32)[..., None] * freqs
    cos = jnp.cos(ang)[:, :, None, :].astype(hn.dtype)
    sin = jnp.sin(ang)[:, :, None, :].astype(hn.dtype)
    q_rope = rotate(q_rope, cos, sin)
    k_rope = rotate(k_rope[:, :, None, :], cos, sin)
    q = jnp.concatenate([q_nope, q_rope], axis=-1)
    k = jnp.concatenate([k_nope, jnp.broadcast_to(k_rope, (B_, S_, H, MLA_ROPE))], axis=-1)
    scale = MLA_QK ** -0.5
    nb = S_ // Q_BLOCK
    qb = q.reshape(B_, nb, Q_BLOCK, H, MLA_QK).transpose(1, 0, 2, 3, 4)
    kpos = jnp.arange(S_)

    def attend(args):
        q_blk, blk = args
        s = jnp.einsum('bqhd,bkhd->bhqk', q_blk, k).astype(jnp.float32) * scale
        qpos = blk * Q_BLOCK + jnp.arange(Q_BLOCK)
        s = jnp.where(kpos[None, :] <= qpos[:, None], s, -jnp.inf)
        p = jax.nn.softmax(s, axis=-1).astype(v.dtype)
        return jnp.einsum('bhqk,bkhd->bqhd', p, v)

    o = lax.map(attend, (qb, jnp.arange(nb)))
    o = o.transpose(1, 0, 2, 3, 4).reshape(B_, S_, H * MLA_V)
    return o @ w_out

def conv_ffn_2(hn, w_in, conv_w, conv_b, w_out):
    a, u = jnp.split(hn @ w_in, 2, axis=-1)
    a = lax.conv_general_dilated(a, conv_w[:, None, :], window_strides=(1,),
                                 padding=[(CONV_W - 1, 0)],
                                 dimension_numbers=('NWC', 'WIO', 'NWC'),
                                 feature_group_count=D_FF_2) + conv_b
    return (jax.nn.silu(a) * u) @ w_out

def second_inputs(seed: int = 0) -> dict:
    key = jax.random.key(seed)
    ks = iter(jax.random.split(key, 40))
    nrm = lambda shape, s: jax.random.normal(next(ks), shape, jnp.float32) * s
    D = D_MODEL
    G, P, Hc = S5_GROUPS, S5_STATE, S5_GROUP
    x = nrm((BATCH, SEQ, D), 1.0)
    offset = jax.random.randint(next(ks), (BATCH, 1), 0, SEQ)
    positions = (offset + jnp.arange(SEQ)[None, :]).astype(jnp.int32)
    return {
        "x": x,
        "positions": positions,
        "norm_mix_g": 1.0 + nrm((DEPTH, D), 0.02),
        "norm_ffn_g": 1.0 + nrm((DEPTH, D), 0.02),
        "final_norm_g": 1.0 + nrm((D,), 0.02),
        "even_w_in": nrm((N_EVEN, D, EVEN_IN), D ** -0.5),
        "hgrn_lb_logits": nrm((N_EVEN + 1, HGRN_DIM), 0.1),
        "hgrn_norm_g": 1.0 + nrm((N_EVEN, HGRN_DIM), 0.02),
        "s5_a_re": -0.5 + nrm((N_EVEN, G, P), 0.01),
        "s5_a_im": jnp.pi * jnp.arange(P, dtype=jnp.float32) + nrm((N_EVEN, G, P), 0.01),
        "s5_log_dt": jax.random.uniform(next(ks), (N_EVEN, G), jnp.float32,
                                        math.log(S5_DT_MIN), math.log(S5_DT_MAX)),
        "s5_b_re": nrm((N_EVEN, G, P, Hc), (2 * Hc) ** -0.5),
        "s5_b_im": nrm((N_EVEN, G, P, Hc), (2 * Hc) ** -0.5),
        "s5_c_re": nrm((N_EVEN, G, Hc, P), (2 * P) ** -0.5),
        "s5_c_im": nrm((N_EVEN, G, Hc, P), (2 * P) ** -0.5),
        "s5_d": nrm((N_EVEN, S5_DIM), 1.0),
        "s5_w_glu": nrm((N_EVEN, S5_DIM, S5_DIM), S5_DIM ** -0.5),
        "s5_b_glu": nrm((N_EVEN, S5_DIM), 0.02),
        "even_w_out": nrm((N_EVEN, HGRN_DIM + S5_DIM, D), (HGRN_DIM + S5_DIM) ** -0.5),
        "odd_w_in": nrm((N_ODD, D, ODD_IN), D ** -0.5),
        "mla_q_norm_g": 1.0 + nrm((N_ODD, MLA_Q_RANK), 0.02),
        "mla_w_uq": nrm((N_ODD, MLA_Q_RANK, MLA_HEADS * MLA_QK), MLA_Q_RANK ** -0.5),
        "mla_kv_norm_g": 1.0 + nrm((N_ODD, MLA_KV_RANK), 0.02),
        "mla_w_ukv": nrm((N_ODD, MLA_KV_RANK, MLA_HEADS * (MLA_NOPE + MLA_V)), MLA_KV_RANK ** -0.5),
        "odd_w_out": nrm((N_ODD, MLA_HEADS * MLA_V, D), (MLA_HEADS * MLA_V) ** -0.5),
        "ffn_w_in": nrm((DEPTH, D, 2 * D_FF_2), D ** -0.5),
        "ffn_conv_w": nrm((DEPTH, CONV_W, D_FF_2), CONV_W ** -0.5),
        "ffn_conv_b": nrm((DEPTH, D_FF_2), 0.02),
        "ffn_w_out": nrm((DEPTH, D_FF_2, D), D_FF_2 ** -0.5),
    }

def second_block(x, positions, norm_mix_g, norm_ffn_g, final_norm_g,
              even_w_in, hgrn_lb_logits, hgrn_norm_g,
              s5_a_re, s5_a_im, s5_log_dt, s5_b_re, s5_b_im, s5_c_re, s5_c_im,
              s5_d, s5_w_glu, s5_b_glu, even_w_out,
              odd_w_in, mla_q_norm_g, mla_w_uq, mla_kv_norm_g, mla_w_ukv, odd_w_out,
              ffn_w_in, ffn_conv_w, ffn_conv_b, ffn_w_out):
    lower_bounds = jnp.cumsum(jax.nn.softmax(hgrn_lb_logits.astype(jnp.float32), axis=0), axis=0)
    h = x
    for layer in range(DEPTH):
        j = layer // 2
        hn = rmsnorm_2(h, norm_mix_g[layer])
        if layer % 2 == 0:
            mix = even_mixer(hn, even_w_in[j], lower_bounds[j], hgrn_norm_g[j],
                             s5_a_re[j], s5_a_im[j], s5_log_dt[j], s5_b_re[j], s5_b_im[j],
                             s5_c_re[j], s5_c_im[j], s5_d[j], s5_w_glu[j], s5_b_glu[j],
                             even_w_out[j])
        else:
            mix = mla(hn, positions, odd_w_in[j], mla_q_norm_g[j], mla_w_uq[j],
                      mla_kv_norm_g[j], mla_w_ukv[j], odd_w_out[j])
        h = h + mix
        h = h + conv_ffn_2(rmsnorm_2(h, norm_ffn_g[layer]), ffn_w_in[layer], ffn_conv_w[layer],
                         ffn_conv_b[layer], ffn_w_out[layer])
    return rmsnorm_2(h, final_norm_g)


def setup_inputs(seed=0):
    out = dict(first_inputs(seed))
    for name, value in second_inputs(seed + 1).items():
        if name != "x":
            out[name + "_2"] = value
    return out


def reference(
    x, norm_mix_pre, norm_mix_post, norm_ffn_pre, norm_ffn_post, ssd_w_in, ssd_conv_w,
    ssd_conv_b, ssd_dt_bias, ssd_a_log, ssd_d, ssd_norm, ssd_w_out, lru_w_in, lru_b_in,
    lru_conv_w, lru_conv_b, lru_w_gx, lru_b_gx, lru_w_ga, lru_b_ga, lru_lambda, lru_w_out,
    lru_b_out, ffn_w_up, ffn_conv_w, ffn_conv_b, ffn_w_down, positions_2, norm_mix_g_2,
    norm_ffn_g_2, final_norm_g_2, even_w_in_2, hgrn_lb_logits_2, hgrn_norm_g_2, s5_a_re_2,
    s5_a_im_2, s5_log_dt_2, s5_b_re_2, s5_b_im_2, s5_c_re_2, s5_c_im_2, s5_d_2, s5_w_glu_2,
    s5_b_glu_2, even_w_out_2, odd_w_in_2, mla_q_norm_g_2, mla_w_uq_2, mla_kv_norm_g_2,
    mla_w_ukv_2, odd_w_out_2, ffn_w_in_2, ffn_conv_w_2, ffn_conv_b_2, ffn_w_out_2,
):
    x = first_block(
        x, norm_mix_pre, norm_mix_post, norm_ffn_pre, norm_ffn_post, ssd_w_in, ssd_conv_w,
        ssd_conv_b, ssd_dt_bias, ssd_a_log, ssd_d, ssd_norm, ssd_w_out, lru_w_in, lru_b_in,
        lru_conv_w, lru_conv_b, lru_w_gx, lru_b_gx, lru_w_ga, lru_b_ga, lru_lambda, lru_w_out,
        lru_b_out, ffn_w_up, ffn_conv_w, ffn_conv_b, ffn_w_down,
    )
    return second_block(
        x, positions_2, norm_mix_g_2, norm_ffn_g_2, final_norm_g_2, even_w_in_2,
        hgrn_lb_logits_2, hgrn_norm_g_2, s5_a_re_2, s5_a_im_2, s5_log_dt_2, s5_b_re_2,
        s5_b_im_2, s5_c_re_2, s5_c_im_2, s5_d_2, s5_w_glu_2, s5_b_glu_2, even_w_out_2,
        odd_w_in_2, mla_q_norm_g_2, mla_w_uq_2, mla_kv_norm_g_2, mla_w_ukv_2, odd_w_out_2,
        ffn_w_in_2, ffn_conv_w_2, ffn_conv_b_2, ffn_w_out_2,
    )


_drawn_inputs = setup_inputs


def setup_inputs(seed=0):
    import zlib

    import numpy as np

    out = dict(_drawn_inputs(seed))
    spreads = {}
    factors = {'ssd_conv_b': 3.292,
     'lru_b_gx': 8.0,
     'lru_b_ga': 8.0,
     'lru_b_out': 3.267,
     'ffn_conv_b': 3.815,
     'norm_mix_g_2': 6.161,
     'norm_ffn_g_2': 5.36,
     'final_norm_g_2': 8.309,
     'hgrn_lb_logits_2': 3.295,
     'hgrn_norm_g_2': 8.0,
     's5_a_re_2': 64.0,
     's5_a_im_2': 64.0,
     's5_log_dt_2': 64.0,
     's5_b_re_2': 64.0,
     's5_b_im_2': 64.0,
     's5_c_re_2': 64.0,
     's5_c_im_2': 64.0,
     's5_b_glu_2': 46.584,
     'mla_q_norm_g_2': 8.0,
     'mla_kv_norm_g_2': 8.0,
     'ffn_conv_b_2': 7.817}
    for name, (base, spread) in spreads.items():
        noise = np.random.default_rng([zlib.crc32(name.encode()), seed]).standard_normal(out[name].shape)
        drawn = base * np.exp(spread * noise) if base else spread * noise
        out[name] = __import__('jax').numpy.asarray(drawn.astype(out[name].dtype))
    for name, factor in factors.items():
        out[name] = (out[name] * factor).astype(out[name].dtype)
    return out
```

```python
import math
from contextlib import ExitStack

import numpy as np
import concourse.bass as bass
from concourse import mybir
from concourse.alu_op_type import AluOpType as ALU

ACT = mybir.ActivationFunctionType
F32 = mybir.dt.float32
F32R = mybir.dt.float32r
I32 = mybir.dt.int32
AX = mybir.AxisListType

P = 128
T = 512
D = 1024
KD = D // P
NC = T // P
EPS = 1e-6
SSD_CH = 2048
NX = SSD_CH // P
SSD_H = 32
SSD_G = 4
LRU_W = 1280
NL = LRU_W // P
FF1 = 4096
FF2 = 2816
HG = 4
S5T = 16
MLA_H = 8
RING = 4
BPU = 8
MAGIC = 1.5 * 2.0 ** 23
TWO_PI = (6.28125, 1.93500518798828125e-03, 2 * math.pi - 6.28125 - 1.93500518798828125e-03)
NEG = -3.0e38

COLUMNS = [
    ("mix_pre", 16), ("mix_post", 16), ("ffn_pre", 16), ("ffn_post", 16), ("mix_g2", 16), ("ffn_g2", 16),
    ("final_g", 8), ("ssd_conv", 24 * 5), ("ssd_d", 16), ("ssd_norm", 16), ("dt_bias", 1), ("a_log", 1),
    ("lru_bx", 10), ("lru_by", 10), ("lru_conv", 10 * 5), ("lru_bgx", 10), ("lru_bga", 10), ("lru_lam", 10),
    ("lru_bout", 8), ("ffn1_0", 32 * 8), ("ffn1_1", 32 * 8), ("ffn2_0", 22 * 4), ("ffn2_1", 22 * 4),
    ("lb", 8), ("hgrn_g", 4), ("s5_are", 16), ("s5_aim", 16), ("s5_logdt", 16), ("s5_d", 4), ("b_glu", 4),
    ("q_g", 3), ("kv_g", 2), ("freq", 1),
]
COL, _n = {}, 0
for _name, _w in COLUMNS:
    COL[_name] = _n
    _n += _w
NCOL = _n

SEGMENTS = [
    ("ssd_dt", 1, 1024), ("ssd_xbc", 24, 1024), ("ssd_z", 16, 1024), ("ssd_out", 16, 1024),
    ("f0_up0", 32, 1024), ("f0_dn0", 16, 1024), ("f0_up1", 32, 1024), ("f0_dn1", 16, 1024),
    ("lru_in", 20, 1024), ("lru_gate", 5, 512), ("lru_out", 16, 640),
    ("f1_up0", 32, 1024), ("f1_dn0", 16, 1024), ("f1_up1", 32, 1024), ("f1_dn1", 16, 1024),
    ("ev_in", 20, 1024), ("glu", 2, 1024), ("ev_out", 8, 1024),
    ("f2_up0", 24, 1024), ("f2_dn0", 16, 768), ("f2_up1", 20, 1024), ("f2_dn1", 16, 640),
    ("od_in", 7, 1024), ("uq", 6, 768), ("uk", 2, 1024), ("uv", 2, 1024), ("od_out", 8, 1024),
    ("f3_up0", 24, 1024), ("f3_dn0", 16, 768), ("f3_up1", 20, 1024), ("f3_dn1", 16, 640),
]
UNIT0, _n = {}, 0
for _name, _k, _w in SEGMENTS:
    UNIT0[_name] = _n
    _n += _k
UNITS = _n

TILES = [
    ("ssd_dt", 1), ("ssd_xbc", 24), ("ssd_z", 16), ("ssd_out", 8),
    ("f0_up0", 32), ("f0_dn0", 8), ("f0_up1", 32), ("f0_dn1", 8),
    ("lru_in", 20), ("lru_gate", 20), ("lru_out", 8),
    ("f1_up0", 32), ("f1_dn0", 8), ("f1_up1", 32), ("f1_dn1", 8),
    ("ev_in", 20), ("glu", 4), ("ev_out", 8),
    ("f2_up0", 24), ("f2_dn0", 8), ("f2_up1", 20), ("f2_dn1", 8),
    ("od_in", 7), ("uq", 12), ("uk", 8), ("uv", 8), ("od_out", 8),
    ("f3_up0", 24), ("f3_dn0", 8), ("f3_up1", 20), ("f3_dn1", 8),
]
TILE0, _n = {}, 0
for _name, _k in TILES:
    TILE0[_name] = _n
    _n += _k


def wait(eng, sem, value):
    if not isinstance(value, int) or value > 0:
        eng.wait_ge(sem, value)


def repeat(eng, n, body, peel_last=False):
    body(0)
    if n - peel_last > 1:
        with eng.Fori(1, n - peel_last) as i:
            body(i)
    if peel_last:
        body(n - 1)


class Chain:

    def __init__(self, eng, sem, n=0):
        self.eng, self.sem, self.n = eng, sem, n

    def __call__(self, ins):
        ins.then_inc(self.sem, 1)
        self.n += 1
        return self.n

    def sync(self):
        self.eng.wait_ge(self.sem, self.n)

    def link(self, ins):
        self(ins)
        self.sync()
        return self.n


def build_program(nc, dram, out_dram):
    ctx = ExitStack()
    with ctx:
        KB = 1024
        base = 16512
        place = {}
        for name, size in (("cols", NCOL * 4 + (-NCOL * 4) % 32), ("ident", 512), ("ones", 512), ("causal", 512),
                           ("neg_diag", 512), ("pair_mask", 512), ("eps", 32), ("x", 16 * KB), ("h", 32 * KB),
                           ("m", 16 * KB), ("raw", 16 * KB), ("whi", 16 * KB), ("wlo", 16 * KB), ("big", 88 * KB)):
            place[name] = base
            base += size
        assert base <= nc.sbuf_usable_end, base
        BIG, M_, H_ = place["big"], place["m"], place["h"]

        def at(name, offset, shape, dt=F32):
            return nc.alloc_sbuf_tensor_at(name, list(shape), dt, offset=offset)

        cols = at("cols", place["cols"], [P, NCOL])
        ident = at("ident", place["ident"], [P, P])
        ones = at("ones", place["ones"], [P, P])
        causal = at("causal", place["causal"], [P, P])
        neg_diag = at("neg_diag", place["neg_diag"], [P, P])
        pair_mask = at("pair_mask", place["pair_mask"], [P, P], I32)
        eps = at("eps", place["eps"], [P, 1])
        xT = at("xT", place["x"], [P, KD, T])
        h_hi = at("h_hi", H_, [P, KD, T], F32R)
        h_lo = at("h_lo", H_ + 16 * KB, [P, KD, T], F32R)
        mT = at("mT", M_, [P, KD, T])
        raw = at("raw", place["raw"], [P, RING, 1024])
        whi = at("whi", place["whi"], [P, RING, 1024], F32R)
        wlo = at("wlo", place["wlo"], [P, RING, 1024], F32R)
        SCR = BIG + 76 * KB
        sqb = at("sqb", SCR, [P, 2, T])
        ntmp = at("ntmp", SCR + 4 * KB, [P, 2, T])
        rms = at("rms", SCR + 8 * KB, [P, T])
        inv = at("inv", SCR + 10 * KB, [P, T])
        act_hi = at("act_hi", BIG, [P, 16, T], F32R)
        act_lo = at("act_lo", BIG + 32 * KB, [P, 16, T], F32R)
        tg = at("tg", BIG + 64 * KB, [P, 2, T])
        tv = at("tv", BIG + 68 * KB, [P, 2, T])
        pt = at("pt", BIG + 72 * KB, [P, 2, T])
        zr = at("zr", M_, [P, 2, T])
        g_hi = at("g_hi", BIG, [P, NX, T], F32R)
        xbc = at("xbc", BIG + 32 * KB, [P, 24, T])
        g_lo = at("g_lo", BIG + 32 * KB, [P, NX, T], F32R)
        ctap = at("ctap", BIG + 80 * KB, [P, 2, T])
        t1 = at("t1", BIG + 80 * KB, [P, 2, T])
        ec = at("ec", BIG + 84 * KB, [P, 2, T])
        xdt = at("xdt", BIG, [P, NC, SSD_CH])
        dd = at("dd", M_, [32, 4, T])
        dtT = at("dtT", M_ + 8 * KB, [32, T])
        csT = at("csT", M_ + 10 * KB, [32, T])
        nat = at("nat", M_ + 12 * KB, [P, 3, NC, 32])
        etot = at("etot", M_ + 12 * KB + 1536, [P, 32, NC])
        diag = at("diag", M_ + 14 * KB, [32, 32, NC])
        acol = at("acol", M_ + 14 * KB + 512, [32, 2])
        seg128 = at("seg128", M_ + 15 * KB, [32, 2])
        bn = at("bn", M_, [P, NC, P])
        ent = at("ent", M_ + 2 * KB, [P, 3, 512])
        xdd = at("xdd", M_ + 8 * KB, [P, 512])
        xb_hi = at("xb_hi", BIG, [P, NL, T], F32R)
        xb_lo = at("xb_lo", BIG + 20 * KB, [P, NL, T], F32R)
        ybr = at("ybr", BIG + 40 * KB, [P, NL, T])
        xbr = at("xbr", BIG + 60 * KB, [P, NL, T])
        ltap = at("ltap", BIG + 80 * KB, [P, 2, T])
        lcv = at("lcv", BIG + 84 * KB, [P, 2, T])
        gx = at("gx", H_, [P, NL, T])
        ga = at("ga", H_ + 20 * KB, [P, NL, T])
        lth = at("lth", BIG, [P, NL, T])
        lh = at("lh", BIG + 20 * KB, [P, NL, T])
        lo_hi = at("lo_hi", BIG, [P, NL, T], F32R)
        lo_lo = at("lo_lo", BIG + 40 * KB, [P, NL, T], F32R)
        lam8 = at("lam8", H_ + 40 * KB, [P, 4, NL])
        ev = at("ev", BIG, [P, 20, T])
        lbv = at("lbv", M_ + 15 * KB, [P, 6, 4])
        seg64 = at("seg64", M_ + 12 * KB, [P, T])
        bcum = at("bcum", BIG + 40 * KB, [P, 4, T])
        kd = at("kd", BIG + 48 * KB, [P, 4, T])
        k2 = at("k2", BIG + 56 * KB, [P, 4, T])
        attT = at("attT", BIG + 64 * KB, [P, 2, T])
        vN = at("vN", BIG + 68 * KB, [P, 2, T])
        kN = at("kN", BIG + 72 * KB, [P, 2, T])
        stS = at("stS", M_, [P, 2, 7, P])
        dec = at("dec", M_ + 7 * KB, [P, 4, 8])
        otmp = at("otmp", M_ + 8 * KB, [P, 2, T])
        sbuf = [[[at(f"s5{'ri'[c]}{par}{b}", BIG + 8 * KB + 3 * KB * (4 * par + 2 * b + c), [P, 768])
                  for c in range(2)] for b in range(2)] for par in range(2)]
        zf = at("zf", BIG + 32 * KB, [P, 4, T])
        z_hi = at("z_hi", BIG + 40 * KB, [P, 4, T], F32R)
        z_lo = at("z_lo", BIG + 48 * KB, [P, 4, T], F32R)
        wb = at("wb", BIG + 56 * KB, [P, 2, 4, P])
        cc = at("cc", BIG + 60 * KB, [P, 2, S5T, 32])
        braw = at("braw", M_, [P, 2, S5T, 32])
        bbar = at("bbar", M_ + 4 * KB, [P, 2, S5T, 32])
        btmp = at("btmp", M_ + 8 * KB, [P, S5T, 32])
        s5c = at("s5c", M_ + 10 * KB, [P, 24, S5T])
        apow = at("apow", M_ + 12 * KB, [P, 9, 3, S5T])
        od = at("od", BIG, [P, 7, T])
        cq_hi = at("cq_hi", BIG + 14 * KB, [P, 3, T], F32R)
        cq_lo = at("cq_lo", BIG + 20 * KB, [P, 3, T], F32R)
        ck_hi = at("ck_hi", BIG + 26 * KB, [P, 2, T], F32R)
        ck_lo = at("ck_lo", BIG + 30 * KB, [P, 2, T], F32R)
        qT = at("qT", BIG + 34 * KB, [P, 12, T])
        kT = at("kT", BIG + 60 * KB, [P, 8, T])
        trig = at("trig", H_, [P, 6, T])
        pos_i = at("pos_i", H_ + 12 * KB, [P, T], I32)
        rtmp = at("rtmp", H_ + 14 * KB, [P, 2, T])
        krot = at("krot", H_ + 18 * KB, [P, 2, T])
        kz = at("kz", BIG, [P, 2, 4, T])
        vT = at("vT", M_, [P, NC, 1024])
        prb = at("prb", SCR, [P, 2, T])
        prt = at("prt", SCR + 4 * KB, [P, 2, T])
        stat = at("stat", SCR + 8 * KB, [P, 4, 32])

        bank = [ctx.enter_context(nc.psum_tensor(f"bank{b}", [P, T], F32)) for b in range(8)]

        def sem(name):
            return ctx.enter_context(nc.semaphore(name))

        w_in = [sem(f"w_in{s}") for s in range(RING)]
        hi_done = sem("hi_done")
        split_done = sem("split_done")
        unit_done = sem("unit_done")
        bank_free = sem("bank_free")
        x_in = sem("x_in")
        consts = sem("consts")
        out_sem = sem("out_sem")
        n_sq, n_mm, n_rms, n_inv, n_t, n_hi, n_lo = (sem("n_" + s) for s in ("sq", "mm", "rms", "inv", "t", "hi", "lo"))
        x_new = sem("x_new")
        m_new = sem("m_new")

        def w(eng, s, v):
            wait(eng, s, v)

        def split_hi(i, c):
            act = nc.scalar
            s = c % RING
            u = i * RING + c
            if isinstance(u, int) and u >= UNITS:
                return
            w(act, w_in[s], (i + c // RING + 1) * 16)
            w(act, unit_done, u - RING + 1)
            act.activation(whi[:, s, :], raw[:, s, :], ACT.Copy).then_inc(hi_done, 1)

        class Stage:

            def __init__(self, name, ks=(8,)):
                self.name, self.ks = name, ks
                self.u0, self.t0 = UNIT0[name], TILE0[name]
                self.banks = 4 if len(ks) == 1 else 2

            def split_ahead(self, i, k):
                split_hi(i, self.u0 + k + RING)

            def unit_ready(self, eng, i, k):
                w(eng, unit_done, i * RING + (self.u0 + k + 1))

            def pe_start(self, pe, t):
                if isinstance(t, int) and t < self.banks:
                    if t == 0:
                        w(pe, bank_free, self.t0)
                else:
                    w(pe, bank_free, t + (self.t0 - self.banks + 1))

            def freed(self, eng, t):
                w(eng, bank_free, t + (self.t0 + 1))

            def pe_tile(self, pe, out, i, k, rhs, ready=None):
                kt = 0
                n = sum(self.ks)
                for q, blocks in enumerate(self.ks):
                    s = (self.u0 + k + q) % RING
                    w(pe, split_done, i * RING + (self.u0 + k + q + 1))
                    for b in range(blocks):
                        if ready is not None:
                            ready(kt)
                        hi, lo = rhs(kt)
                        wh, wl = whi[:, s, b * P:b * P + P], wlo[:, s, b * P:b * P + P]
                        pe.matmul(out, wh, hi, start=kt == 0, stop=False)
                        pe.matmul(out, wh, lo, start=False, stop=False)
                        last = pe.matmul(out, wl, hi, start=False, stop=kt == n - 1)
                        kt += 1
                    last.then_inc(unit_done, 1)

        stage = {}
        for name, ks in (("ssd_dt", (8,)), ("ssd_xbc", (8,)), ("ssd_z", (8,)), ("ssd_out", (8, 8)),
                         ("lru_in", (8,)), ("lru_gate", (1,)), ("lru_out", (5, 5)), ("ev_in", (8,)), ("glu", (4,)),
                         ("ev_out", (8,)), ("od_in", (8,)), ("uq", (3,)), ("uk", (2,)), ("uv", (2,)), ("od_out", (8,)),
                         *((f"f{f}_up{a}", (8,)) for f in range(4) for a in range(2)),
                         ("f0_dn0", (8, 8)), ("f0_dn1", (8, 8)), ("f1_dn0", (8, 8)), ("f1_dn1", (8, 8)),
                         ("f2_dn0", (6, 6)), ("f2_dn1", (5, 5)), ("f3_dn0", (6, 6)), ("f3_dn1", (5, 5))):
            stage[name] = Stage(name, ks)

        def col(name, k=0, n=1):
            c = COL[name] + k
            if isinstance(c, int):
                return cols[:, c:c + n]
            return cols[:, bass.ds(c, n)]

        class Norm:
            count = dict(sq=0, rms=0, t=0, hi=0, x=0)

            def __init__(self, K, src, gain, n, mode, hi=None, lo=None, squared=None):
                c = Norm.count
                self.squared = squared or src
                self.K, self.src, self.gain, self.n, self.mode = K, src, gain, n, mode
                self.hi, self.lo = hi, lo
                self.sq0, self.r0, self.t0, self.h0, self.x0 = c["sq"], c["rms"], c["t"], c["hi"], c["x"]
                c["sq"] += K
                c["rms"] += 1
                c["t"] += K
                if mode == "split":
                    c["hi"] += K
                elif mode == "residual":
                    c["x"] += K

            def act(self, act, ready):
                for k in range(self.K):
                    ready(act, k)
                    w(act, n_mm, self.sq0 + k - 1)
                    act.activation(sqb[:, (self.sq0 + k) % 2, :], self.squared(k), ACT.Square).then_inc(n_sq, 1)
                w(act, n_mm, self.sq0 + self.K)
                w(act, n_inv, self.r0)
                act.activation(rms[:], bank[7][:], ACT.Sqrt, bias=eps[:], scale=1.0 / self.n).then_inc(n_rms, 1)
                if self.mode == "split":
                    for k in range(self.K):
                        w(act, n_t, self.t0 + k + 1)
                        act.activation(self.hi(k), ntmp[:, (self.t0 + k) % 2, :], ACT.Copy).then_inc(n_hi, 1)

            def pe(self, pe):
                for k in range(self.K):
                    w(pe, n_sq, self.sq0 + k + 1)
                    pe.matmul(bank[7][:], ones[:], sqb[:, (self.sq0 + k) % 2, :], start=k == 0,
                              stop=k == self.K - 1).then_inc(n_mm, 1)

            def dve(self, dve):
                w(dve, n_rms, self.r0 + 1)
                w(dve, n_t, self.t0)
                dve.reciprocal(inv[:], rms[:]).then_inc(n_inv, 1)
                w(dve, n_inv, self.r0 + 1)

                def low(k):
                    w(dve, n_hi, self.h0 + k + 1)
                    dve.tensor_tensor(self.lo(k), ntmp[:, (self.t0 + k) % 2, :], self.hi(k).bitcast(F32),
                                      ALU.subtract).then_inc(n_lo, 1)

                for k in range(self.K):
                    b = (self.t0 + k) % 2
                    if self.mode == "split" and k >= 2:
                        w(dve, n_lo, self.h0 + k - 1)
                    if self.mode == "split" and k < 2:
                        w(dve, n_lo, self.h0)
                        w(dve, x_new, self.x0)
                    if self.mode == "residual":
                        w(dve, x_new, self.x0 + k - 1 if k >= 2 else self.x0)
                        w(dve, n_lo, self.h0)
                    if self.mode == "final":
                        w(dve, x_new, self.x0)
                    dst = self.src(k) if self.mode == "final" else ntmp[:, b, :]
                    dve.scalar_tensor_tensor(out=dst, in0=self.src(k), scalar=self.gain(k), in1=inv[:],
                                             op0=ALU.mult, op1=ALU.mult).then_inc(n_t, 1)
                    if self.mode == "residual":
                        w(dve, n_t, self.t0 + k + 1)
                        dve.tensor_tensor(xT[:, k, :], xT[:, k, :], ntmp[:, b, :], ALU.add).then_inc(x_new, 1)
                    if self.mode == "split" and k >= 1:
                        low(k - 1)
                if self.mode == "split":
                    low(self.K - 1)

            def lo_ready(self, pe, k):
                w(pe, n_lo, self.h0 + k + 1)

        def in_x(k):
            return xT[:, k, :]

        def in_m(k):
            return mT[:, k, :]

        def out_h(k):
            return h_hi[:, k, :]

        def out_hl(k):
            return h_lo[:, k, :]

        def pre(name, layer):
            return Norm(KD, in_x, lambda k: col(name, layer * KD + k), D, "split", out_h, out_hl)

        def post(name, layer):
            return Norm(KD, in_m, lambda k: col(name, layer * KD + k), D, "residual")

        class FFN:

            def __init__(self, f, pairs, kind, prm, pre_norm):
                self.f, self.pairs, self.kind, self.prm, self.norm = f, pairs, kind, prm, pre_norm
                self.up = [stage[f"f{f}_up{a}"] for a in range(2)]
                self.dn = [stage[f"f{f}_dn{a}"] for a in range(2)]
                self.tap, self.gel, self.prod, self.hi, self.lo, self.c1 = (
                    sem(f"f{f}_{s}") for s in ("tap", "gate", "prod", "hi", "lo", "c1"))
                self.taps = 2 if kind == "gelu" else 1
                self.prev = [0, pairs[0]]
                self.per = 4 * self.taps

            def prm_col(self, j, c):
                return col(self.prm, j * self.per + c)

            def product(self, eng, up, j, prev):
                if self.taps == 2:
                    w(eng, self.prod, j + (prev + 1))
                else:
                    up.freed(eng, j * 2 + 1)

            def pe(self, pe):
                for a in range(2):
                    up, dn, prev = self.up[a], self.dn[a], self.prev[a]

                    def up_body(i):
                        for k in range(4):
                            t = i * 4 + k
                            up.pe_start(pe, t)
                            first = a == 0 and isinstance(t, int) and t == 0
                            ready = (lambda kt: self.norm.lo_ready(pe, kt)) if first else None
                            up.pe_tile(pe, bank[k][:], i, k, lambda kt: (h_hi[:, kt, :], h_lo[:, kt, :]), ready)

                    def dn_body(i):
                        for k in range(2):
                            t = i * 2 + k
                            dn.pe_start(pe, t)
                            first = isinstance(t, int) and t == 0
                            ready = (lambda kt: w(pe, self.lo, prev + kt + 1)) if first else None
                            dn.pe_tile(pe, bank[k][:], i, 2 * k,
                                       lambda kt: (act_hi[:, kt, :], act_lo[:, kt, :]), ready)

                    repeat(pe, self.pairs[a] // 2, up_body)
                    repeat(pe, 4, dn_body)

            def act(self, act):
                func = ACT.Gelu_apprx_tanh if self.kind == "gelu" else ACT.Silu
                for a in range(2):
                    up, dn, prev = self.up[a], self.dn[a], self.prev[a]

                    def high(j, e):
                        self.product(act, up, j, prev)
                        act.activation(act_hi[:, j, :] if isinstance(j, int) else act_hi[:, bass.ds(j, 1), :],
                                       pt[:, e, :], ACT.Copy).then_inc(self.hi, 1)

                    def up_body(i):
                        for e in range(2):
                            j = i * 2 + e
                            t = j * 2
                            for v in range(2):
                                up.unit_ready(act, i, 2 * e + v)
                                if v < self.taps:
                                    if v == 0:
                                        if not isinstance(j, int) or j >= 2:
                                            self.product(act, up, j - 2, prev)
                                    act.activation((tg, tv)[v][:, e, :], bank[2 * e + v][:], ACT.Identity,
                                                   bias=self.prm_col(j + prev, 4 * v + 3),
                                                   scale=self.prm_col(j + prev, 4 * v + 2)).then_inc(self.tap, 1)
                                up.split_ahead(i, 2 * e + v)
                            if not (isinstance(j, int) and j == 0):
                                high(j - 1, 1 - e)
                            up.freed(act, t)
                            act.activation(tg[:, e, :], tg[:, e, :], func).then_inc(self.gel, 1)

                    repeat(act, self.pairs[a] // 2, up_body)
                    high(self.pairs[a] - 1, 1)
                    last = self.f == 3 and a == 1

                    def dn_body(i):
                        for k in range(4):
                            dn.unit_ready(act, i, k)
                            dn.split_ahead(i, k)

                    repeat(act, 4, dn_body, peel_last=last)

            def dve(self, dve):
                for a in range(2):
                    up, dn, prev = self.up[a], self.dn[a], self.prev[a]

                    def low(j, e):
                        w(dve, self.hi, j + (prev + 1))
                        hi = act_hi[:, j, :] if isinstance(j, int) else act_hi[:, bass.ds(j, 1), :]
                        lo = act_lo[:, j, :] if isinstance(j, int) else act_lo[:, bass.ds(j, 1), :]
                        dve.tensor_tensor(lo, pt[:, e, :], hi.bitcast(F32), ALU.subtract).then_inc(self.lo, 1)

                    def up_body(i):
                        for e in range(2):
                            j = i * 2 + e
                            for v in range(self.taps):
                                dst, src = (tg, tv)[v], bank[2 * e + v]
                                n = (j + prev) * self.taps + v
                                w(dve, self.tap, n + 1)
                                dve.scalar_tensor_tensor(
                                    out=dst[:, e, 1:T], in0=src[:, 0:T - 1], scalar=self.prm_col(j + prev, 4 * v + 1),
                                    in1=dst[:, e, 1:T], op0=ALU.mult, op1=ALU.add).then_inc(self.c1, 1)
                                w(dve, self.c1, n + 1)
                                dve.scalar_tensor_tensor(
                                    out=dst[:, e, 2:T], in0=src[:, 0:T - 2], scalar=self.prm_col(j + prev, 4 * v),
                                    in1=dst[:, e, 2:T], op0=ALU.mult, op1=ALU.add).then_inc(bank_free, 1)
                            w(dve, self.gel, j + (prev + 1))
                            w(dve, self.lo, j + (prev - 1))
                            up.freed(dve, j * 2 + (1 if self.taps == 2 else 0))
                            if self.taps == 2:
                                dve.tensor_tensor(pt[:, e, :], tg[:, e, :], tv[:, e, :],
                                                  ALU.mult).then_inc(self.prod, 1)
                            else:
                                up.unit_ready(dve, i, 2 * e + 1)
                                dve.tensor_tensor(pt[:, e, :], tg[:, e, :], bank[2 * e + 1][:],
                                                  ALU.mult).then_inc(bank_free, 1)
                            if not (isinstance(j, int) and j == 0):
                                low(j - 1, 1 - e)

                    repeat(dve, self.pairs[a] // 2, up_body)
                    low(self.pairs[a] - 1, 1)
                    onto_x = self.kind != "gelu"

                    def dn_body(i):
                        for k in range(2):
                            t = i * 2 + k
                            dn.unit_ready(dve, i, 2 * k + 1)
                            dst = (xT if onto_x else mT)[:, bass.ds(t, 1) if not isinstance(t, int) else slice(t, t + 1), :]
                            if onto_x or a == 1:
                                dve.tensor_tensor(dst, bank[k][:].unsqueeze(1), dst, ALU.add).then_inc(bank_free, 1)
                            else:
                                dve.tensor_copy(dst, bank[k][:].unsqueeze(1)).then_inc(bank_free, 1)

                    repeat(dve, 4, dn_body)

            def result_ready(self, eng, k):
                self.dn[1].freed(eng, k)

        s_tap, s_c1, s_silu = sem("conv_tap"), sem("conv_c"), sem("conv_silu")
        dt_a, dt_u, dt_w, dt_ln, dt_diff, dt_out, dt_diag = (
            sem("dt_" + s) for s in ("a", "u", "w", "ln", "diff", "out", "diag"))
        act_own, dve_own = sem("act_own"), sem("dve_own")
        tr_nat, tr_et, nat_ok, et_ok = sem("tr_nat"), sem("tr_et"), sem("nat_ok"), sem("et_ok")
        tr_x, xdt_ok, z_tanh = sem("tr_x"), sem("xdt_ok"), sem("z_tanh")
        g_cb, g_bt, g_cbm, g_bn, g_xdd, g_ds, g_ent = (
            sem("g_" + s) for s in ("cb", "bt", "cbm", "bn", "xdd", "ds", "ent"))
        p_cs, p_sub, p_min, p_ec, p_E, p_S, p_Cd, p_y, p_ev, p_g = (
            sem("p_" + s) for s in ("cs", "sub", "min", "ec", "E", "S", "Cd", "y", "ev", "g"))
        norm0 = pre("mix_pre", 0)
        gnorms = [Norm(4, (lambda k, g=g: xbc[:, 4 * g + k, :]), (lambda k, g=g: col("ssd_norm", 4 * g + k)), 512, "split",
                       (lambda k, g=g: g_hi[:, 4 * g + k, :]), (lambda k, g=g: g_lo[:, 4 * g + k, :]))
                  for g in range(SSD_G)]
        post0 = post("mix_post", 0)

        def chunk(t3, c):
            return t3[:, c * P:(c + 1) * P]

        def rhs_h(kt):
            return h_hi[:, kt, :], h_lo[:, kt, :]

        def ssd_pe(pe):
            st = stage["ssd_dt"]
            st.pe_start(pe, 0)
            st.pe_tile(pe, bank[3][:], 0, 0, rhs_h, lambda kt: norm0.lo_ready(pe, kt))
            st = stage["ssd_xbc"]

            def body(i):
                for k in range(4):
                    st.pe_start(pe, i * 4 + k)
                    st.pe_tile(pe, bank[k][:], i, k, rhs_h)

            repeat(pe, 6, body)
            pe.wait_ge(dt_out, 1)
            for n, src in enumerate((csT, dtT, dd[:, 1, :])):
                for c in range(NC):
                    last = pe.transpose(bank[4][:, (n * NC + c) * 32:(n * NC + c) * 32 + 32], src[:, c * P:(c + 1) * P],
                                        ident[0:32, 0:32])
            last.then_inc(tr_nat, 1)
            pe.wait_ge(dt_diag, 1)
            pe.matmul(bank[5][:, 0:P], ones[0:32, :], diag[:].rearrange("p a b -> p (a b)"), start=True,
                      stop=True).then_inc(tr_et, 1)
            for i in range(NX):
                pe.wait_ge(s_silu, i + 1)
                if i == 0:
                    pe.wait_ge(nat_ok, 1)
                    pe.wait_ge(et_ok, 1)
                w(pe, xdt_ok, i - 1)
                for c in range(NC):
                    last = pe.transpose(bank[4 + i % 2][:, c * P:(c + 1) * P], xbc[:, i, c * P:(c + 1) * P], ident[:])
                last.then_inc(tr_x, 1)
            zt = stage["ssd_z"]

            def z_tiles(g):
                for i in range(4 * g, 4 * g + 4):
                    zt.pe_start(pe, i)
                    zt.pe_tile(pe, bank[i % 4][:], i // 4, i % 4, rhs_h)

            def decay_rows(i):
                for e in range(2):
                    h = 2 * i + e
                    if i == 0:
                        pe.wait_ge(xdt_ok, NX)
                    w(pe, p_sub, h - 1)
                    w(pe, p_ec, h - 1)
                    pe.matmul(bank[4 + e][:], ident[0:32, h:h + 1].broadcast_to((32, P)), csT[:], start=True,
                              stop=True).then_inc(p_cs, 1)

            for g in range(SSD_G):
                w(pe, p_ev, 4 * g)
                pe.wait_ge(s_silu, 24)
                for c in range(NC):
                    last = pe.matmul(chunk(bank[7], c), chunk(xbc[:, 16 + g, :], c), chunk(xbc[:, 20 + g, :], c),
                                     start=True, stop=True)
                last.then_inc(g_cb, 1)
                for c in range(NC):
                    last = pe.transpose(chunk(bank[6], c), chunk(xbc[:, 16 + g, :], c), ident[:])
                last.then_inc(g_bt, 1)
                for z in range(3):
                    pe.wait_ge(g_xdd, 3 * g + z + 1)
                    pe.wait_ge(g_bn, g + 1)
                    if z == 0:
                        pe.wait_ge(g_cbm, g + 1)
                    if z == 2:
                        pe.wait_ge(g_ent, 3 * g + 1)
                    pe.matmul(bank[7 - z % 2][:], bn[:, z, :], xdd[:], start=True, stop=True).then_inc(g_ds, 1)
                decay_rows(4 * g)
                for q in range(4):
                    i = 4 * g + q
                    if q < 3:
                        decay_rows(i + 1)
                    y = bank[6 + i % 2]
                    if q == 0:
                        pe.wait_ge(g_ent, 3 * g + 3)
                    w(pe, p_ev, i - 1)
                    for e in range(2):
                        h = 2 * i + e
                        pe.wait_ge(p_S, h + 1)
                        pe.wait_ge(p_Cd, h + 1)
                        for c in range(NC):
                            o = y[64 * e:64 * e + 64, c * P:(c + 1) * P]
                            last = pe.matmul(o, xdt[:, c, 64 * h:64 * h + 64], chunk(t1[:, e, :], c), start=True,
                                             stop=c == 0)
                            if c:
                                last = pe.matmul(o, ent[:, c - 1, 64 * (h % 8):64 * (h % 8) + 64],
                                                 chunk(ec[:, e, :], c), start=False, stop=True)
                        last.then_inc(p_y, 1)
            z_tiles(0)
            for g in range(SSD_G):
                if g < SSD_G - 1:
                    z_tiles(g + 1)
                gnorms[g].pe(pe)
            so = stage["ssd_out"]

            def body(i):
                for k in range(2):
                    t = i * 2 + k
                    so.pe_start(pe, t)
                    ready = None
                    if isinstance(t, int) and t == 0:
                        ready = lambda kt: gnorms[kt // 4].lo_ready(pe, kt % 4)
                    so.pe_tile(pe, bank[k][:], i, 2 * k, lambda kt: (g_hi[:, kt, :], g_lo[:, kt, :]), ready)

            repeat(pe, 4, body)
            post0.pe(pe)

        def conv_start(act, st, i, k, t, prm, per, tapbuf, shift):
            act.activation(tapbuf, bank[k][:], ACT.Identity, bias=col(prm, t * per + per - 1),
                           scale=col(prm, t * per + per - 2)).then_inc(shift, 1)

        def ssd_act(act, own):
            st = stage["ssd_dt"]
            st.unit_ready(act, 0, 0)
            act.activation(dd[:, 0, :], bank[3][0:32, :], ACT.Identity, bias=col("dt_bias")[0:32, :]).then_inc(bank_free, 1)
            split_hi(0, RING)
            act.wait_ge(bank_free, 1)
            own.link(act.activation(dd[:, 1, :], dd[:, 0, :], ACT.Abs))
            act.activation(dd[:, 1, :], dd[:, 1, :], ACT.Exp, scale=-1.0).then_inc(dt_u, 1)
            act.activation(acol[:, 0:1], col("a_log")[0:32, :], ACT.Exp).then_inc(dt_a, 1)
            act.wait_ge(dt_w, 1)
            act.activation(dd[:, 3, :], dd[:, 2, :], ACT.Ln).then_inc(dt_ln, 1)
            st = stage["ssd_xbc"]

            def silu(t, e):
                st.freed(act, t)
                dst = xbc[:, t:t + 1, :] if isinstance(t, int) else xbc[:, bass.ds(t, 1), :]
                act.activation(dst, ctap[:, e:e + 1, :], ACT.Silu).then_inc(s_silu, 1)

            def body(i):
                for k in range(4):
                    t = i * 4 + k
                    st.unit_ready(act, i, k)
                    w(act, s_silu, t - 1)
                    act.activation(ctap[:, k % 2, :], bank[k][:], ACT.Identity, bias=col("ssd_conv", t * 5 + 4),
                                   scale=col("ssd_conv", t * 5 + 3)).then_inc(s_tap, 1)
                    st.split_ahead(i, k)
                    if not (isinstance(t, int) and t == 0):
                        silu(t - 1, (k - 1) % 2)

            repeat(act, 6, body)
            silu(23, 1)
            act.wait_ge(dt_diff, 1)
            act.activation(dd[:, 1, :], dd[:, 1, :], ACT.Exp).then_inc(dt_out, 1)
            act.wait_ge(tr_et, 1)
            act.activation(etot[:].rearrange("p a b -> p (a b)"), bank[5][:, 0:P], ACT.Exp).then_inc(et_ok, 1)
            zt = stage["ssd_z"]

            def z_tiles(g):
                for i in range(4 * g, 4 * g + 4):
                    zt.unit_ready(act, i // 4, i % 4)
                    w(act, p_g, i - 1)
                    act.activation(zr[:, i % 2, :], bank[i % 4][:], ACT.Tanh, scale=0.5).then_inc(z_tanh, 1)
                    zt.split_ahead(i // 4, i % 4)

            for g in range(SSD_G):
                for q in range(4):
                    i = 4 * g + q
                    for e in range(2):
                        h = 2 * i + e
                        act.wait_ge(p_sub, h + 1)
                        w(act, p_y, h - 1)
                        w(act, p_Cd, h - 1)
                        act.activation(ec[:, e, :], bank[4 + e][:], ACT.Exp).then_inc(p_ec, 1)
                        act.wait_ge(p_min, h + 1)
                        act.activation(t1[:, e, :], t1[:, e, :], ACT.Exp).then_inc(p_E, 1)
            z_tiles(0)
            for g in range(SSD_G):
                if g < SSD_G - 1:
                    z_tiles(g + 1)
                gnorms[g].act(act, lambda a, k, g=g: a.wait_ge(p_g, 4 * g + k + 1))
            so = stage["ssd_out"]

            def body(i):
                for k in range(4):
                    so.unit_ready(act, i, k)
                    so.split_ahead(i, k)

            repeat(act, 4, body)
            post0.act(act, lambda a, k: so.freed(a, k))

        def ssd_dve(dve, own):
            x, u, v, ln = (dd[:, n, :] for n in range(4))
            dve.wait_ge(dt_u, 1)
            dve.tensor_scalar(v, u, 1.0, None, ALU.add).then_inc(dt_w, 1)
            dve.wait_ge(dt_ln, 1)
            own.link(dve.tensor_scalar(v, v, -1.0, 1e-30, ALU.add, ALU.max))
            own.link(dve.reciprocal(v, v))
            own.link(dve.tensor_tensor(ln, ln, u, ALU.mult))
            own.link(dve.tensor_tensor(ln, ln, v, ALU.mult))
            own.link(dve.tensor_scalar(v, u, -0.5, 1.0, ALU.mult, ALU.add))
            own.link(dve.tensor_tensor(v, v, u, ALU.mult))
            own.link(dve.tensor_tensor(ln, ln, v, ALU.max))
            own.link(dve.scalar_tensor_tensor(out=dtT[:], in0=x, scalar=0.0, in1=ln, op0=ALU.max, op1=ALU.add))
            dve.wait_ge(dt_a, 1)
            own.link(dve.tensor_scalar(acol[:, 1:2], acol[:, 0:1], -1.0, None, ALU.mult))
            own.link(dve.tensor_scalar(x, dtT[:], acol[:, 1:2], None, ALU.mult))
            for c in range(NC):
                own(dve.tensor_tensor_scan(out=chunk(csT[:], c), data0=ones[0:32, :], data1=chunk(x, c), initial=0.0,
                                           op0=ALU.mult, op1=ALU.add))
            own.sync()
            cs3 = csT[:].rearrange("p (c l) -> p c l", c=NC)
            tot = cs3[:, :, P - 1:P]
            dve.tensor_tensor(dd[:, 1, :].rearrange("p (c l) -> p c l", c=NC), tot.broadcast_to((32, NC, P)), cs3,
                              ALU.subtract).then_inc(dt_diff, 1)
            dve.tensor_tensor(diag[:], ident[0:32, 0:32].unsqueeze(2).broadcast_to((32, 32, NC)),
                              tot.rearrange("p c l -> p l c").broadcast_to((32, 32, NC)), ALU.mult).then_inc(dt_diag, 1)
            st = stage["ssd_xbc"]

            def body(i):
                for k in range(4):
                    t = i * 4 + k
                    w(dve, s_tap, t + 1)
                    for n in range(3):
                        if n:
                            w(dve, s_c1, t * 2 + n)
                        ins = dve.scalar_tensor_tensor(
                            out=ctap[:, k % 2, n + 1:T], in0=bank[k][:, 0:T - n - 1], scalar=col("ssd_conv", t * 5 + 2 - n),
                            in1=ctap[:, k % 2, n + 1:T], op0=ALU.mult, op1=ALU.add)
                        ins.then_inc(s_c1 if n < 2 else bank_free, 1)

            repeat(dve, 6, body)
            dve.wait_ge(tr_nat, 1)
            dve.tensor_copy(nat[:].rearrange("p a b c -> p (a b c)"), bank[4][:, 0:3 * P]).then_inc(nat_ok, 1)
            dve.wait_ge(nat_ok, 1)

            def per_head(n, c, h0, heads):
                return nat[:, n, c, h0:h0 + heads].unsqueeze(2).broadcast_to((P, heads, 64))

            for i in range(NX):
                dve.wait_ge(tr_x, i + 1)
                dve.tensor_tensor(xdt[:, :, i * P:(i + 1) * P].rearrange("p c (e q) -> p c e q", e=2),
                                  bank[4 + i % 2][:].rearrange("p (c e q) -> p c e q", c=NC, e=2),
                                  nat[:, 1, :, 2 * i:2 * i + 2].unsqueeze(3).broadcast_to((P, NC, 2, 64)),
                                  ALU.mult).then_inc(xdt_ok, 1)
            zt = stage["ssd_z"]

            def z_tiles(g):
                for i in range(4 * g, 4 * g + 4):
                    dve.wait_ge(z_tanh, i + 1)
                    dve.scalar_tensor_tensor(out=zr[:, i % 2, :], in0=zr[:, i % 2, :], scalar=1.0, in1=bank[i % 4][:],
                                             op0=ALU.add, op1=ALU.mult).then_inc(bank_free, 1)
                    zt.freed(dve, i)
                    dve.scalar_tensor_tensor(out=xbc[:, i, :], in0=xbc[:, i, :], scalar=0.5, in1=zr[:, i % 2, :],
                                             op0=ALU.mult, op1=ALU.mult).then_inc(p_g, 1)

            def evacuate(i):
                dve.wait_ge(p_y, 2 * i + 2)
                dve.scalar_tensor_tensor(out=xbc[:, i, :], in0=xbc[:, i, :], scalar=col("ssd_d", i), in1=bank[6 + i % 2][:],
                                         op0=ALU.mult, op1=ALU.add).then_inc(p_ev, 1)

            for g in range(SSD_G):
                dve.wait_ge(xdt_ok, NX)
                w(dve, g_ds, 3 * g)
                for z in range(3):
                    w(dve, g_ds, 3 * g + z)
                    dve.tensor_tensor(xdd[:].rearrange("p (h q) -> p h q", q=64),
                                      xdt[:, z, 512 * g:512 * g + 512].rearrange("p (h q) -> p h q", q=64),
                                      per_head(2, z, 8 * g, 8), ALU.mult).then_inc(g_xdd, 1)
                    if z == 0:
                        dve.wait_ge(g_cb, g + 1)
                        dve.wait_ge(g_bt, g + 1)
                        b4 = xbc[:, 16 + g, :].rearrange("p (c l) -> p c l", c=NC)
                        dve.tensor_tensor(b4, bank[7][:].rearrange("p (c l) -> p c l", c=NC),
                                          causal[:].unsqueeze(1).broadcast_to((P, NC, P)), ALU.mult).then_inc(g_cbm, 1)
                        dve.tensor_copy(bn[:].rearrange("p c l -> p (c l)"), bank[6][:]).then_inc(g_bn, 1)
                    dve.wait_ge(g_ds, 3 * g + z + 1)
                    w(dve, p_y, 8 * g)
                    if z == 0:
                        dve.tensor_copy(ent[:, 0, :], bank[7][:]).then_inc(g_ent, 1)
                    else:
                        dve.wait_ge(g_ent, 3 * g + z)
                        own.link(dve.tensor_tensor(
                            ent[:, z, :].rearrange("p (h q) -> p h q", q=64),
                            ent[:, z - 1, :].rearrange("p (h q) -> p h q", q=64),
                            etot[:, 8 * g:8 * g + 8, z:z + 1].broadcast_to((P, 8, 64)), ALU.mult))
                        dve.tensor_tensor(ent[:, z, :], ent[:, z, :], bank[7 - z % 2][:], ALU.add).then_inc(g_ent, 1)
                for q in range(4):
                    i = 4 * g + q
                    for e in range(2):
                        h = 2 * i + e
                        dve.wait_ge(p_cs, h + 1)
                        w(dve, p_y, h - 1)
                        dve.tensor_tensor(t1[:, e, :].rearrange("p (c l) -> p c l", c=NC),
                                          bank[4 + e][:].rearrange("p (c l) -> p c l", c=NC),
                                          nat[:, 0, :, h:h + 1].broadcast_to((P, NC, P)), ALU.subtract).then_inc(p_sub, 1)
                        dve.wait_ge(p_sub, h + 1)
                        dve.tensor_scalar(t1[:, e, :], t1[:, e, :], 0.0, None, ALU.min).then_inc(p_min, 1)
                    if q:
                        evacuate(i - 1)
                    for e in range(2):
                        h = 2 * i + e
                        dve.wait_ge(p_E, h + 1)
                        dve.wait_ge(g_cbm, g + 1)
                        dve.tensor_tensor(t1[:, e, :], t1[:, e, :], xbc[:, 16 + g, :], ALU.mult).then_inc(p_S, 1)
                        dve.wait_ge(p_ec, h + 1)
                        dve.tensor_tensor(ec[:, e, :], ec[:, e, :], xbc[:, 20 + g, :], ALU.mult).then_inc(p_Cd, 1)
                evacuate(4 * g + 3)
            dve.wait_ge(p_ev, NX)
            z_tiles(0)
            for g in range(SSD_G):
                if g < SSD_G - 1:
                    z_tiles(g + 1)
                gnorms[g].dve(dve)
            so = stage["ssd_out"]

            def body(i):
                for k in range(2):
                    t = i * 2 + k
                    so.unit_ready(dve, i, 2 * k + 1)
                    dst = mT[:, t, :] if isinstance(t, int) else mT[:, bass.ds(t, 1), :].squeeze(1)
                    dve.tensor_copy(dst, bank[k][:]).then_inc(bank_free, 1)

            repeat(dve, 4, body)
            post0.dve(dve)

        def x_given(act, k):
            if k == 0:
                act.wait_ge(x_in, 32)

        l_in, l_x, l_c, l_t0, l_hi, l_lo = (sem("l_" + s) for s in ("in", "x", "c", "t0", "hi", "lo"))
        l_g, l_lam, l_a, l_th, l_q, l_s, l_h, l_ph, l_pl = (
            sem("l_" + s) for s in ("gates", "lam", "a", "th", "q", "s", "h", "prod_hi", "prod_lo"))
        ffn_pre0 = pre("ffn_pre", 0)
        ffn0 = FFN(0, (16, 16), "gelu", "ffn1_0", ffn_pre0)
        ffn_post0 = post("ffn_post", 0)
        norm1 = pre("mix_pre", 1)
        post1 = post("mix_post", 1)
        ffn_pre1 = pre("ffn_pre", 1)
        ffn1 = FFN(1, (16, 16), "gelu", "ffn1_1", ffn_pre1)
        ffn_post1 = post("ffn_post", 1)

        def out_pe(pe, st, hi, lo, ready):
            def body(i):
                for k in range(2):
                    t = i * 2 + k
                    st.pe_start(pe, t)
                    first = isinstance(t, int) and t == 0
                    st.pe_tile(pe, bank[k][:], i, 2 * k, lambda kt: (hi[:, kt, :], lo[:, kt, :]),
                               (lambda kt: ready(kt)) if first else None)
            repeat(pe, 4, body)

        def split_only(act, st, n4):
            def body(i):
                for k in range(4):
                    st.unit_ready(act, i, k)
                    st.split_ahead(i, k)
            repeat(act, n4, body)

        def lru_pe(pe):
            st = stage["lru_in"]

            def body(i):
                for k in range(4):
                    t = i * 4 + k
                    st.pe_start(pe, t)
                    first = isinstance(t, int) and t == 0
                    st.pe_tile(pe, bank[k][:], i, k, rhs_h, (lambda kt: norm1.lo_ready(pe, kt)) if first else None)

            repeat(pe, 5, body)
            st = stage["lru_gate"]
            for t in range(2 * NL):
                h, u = t // 2, t // 4
                st.pe_start(pe, t)
                s, b = (st.u0 + u) % RING, t % 4
                if b == 0:
                    pe.wait_ge(split_done, st.u0 + u + 1)
                pe.wait_ge(l_lo, h + 1)
                wh, wl = whi[:, s, b * P:b * P + P], wlo[:, s, b * P:b * P + P]
                pe.matmul(bank[t % 4][:], wh, xb_hi[:, h, :], start=True, stop=False)
                pe.matmul(bank[t % 4][:], wh, xb_lo[:, h, :], start=False, stop=False)
                last = pe.matmul(bank[t % 4][:], wl, xb_hi[:, h, :], start=False, stop=True)
                if b == 3:
                    last.then_inc(unit_done, 1)
                else:
                    last.then_inc(l_g, 1)
            out_pe(pe, stage["lru_out"], lo_hi, lo_lo, lambda kt: pe.wait_ge(l_pl, kt + 1))
            post1.pe(pe)

        def gate_ready(eng, t):
            st = stage["lru_gate"]
            if t % 4 == 3:
                eng.wait_ge(unit_done, st.u0 + t // 4 + 1)
            else:
                eng.wait_ge(l_g, t - t // 4 + 1)

        def lru_act(act, own):
            st = stage["lru_in"]

            def xpart(t, e, k):
                act.activation(ltap[:, e, :], bank[k][:], ACT.Identity, bias=col("lru_bx", t - NL)).then_inc(bank_free, 1)

            for t in range(20):
                i, k = t // 4, t % 4
                st.unit_ready(act, i, k)
                if t < NL:
                    act.activation(ybr[:, t, :], bank[k][:], ACT.Gelu_apprx_tanh, bias=col("lru_by", t)).then_inc(bank_free, 1)
                else:
                    j = t - NL
                    w(act, l_x, j - 1)
                    xpart(t, j % 2, k)
                    if j >= 1:
                        act.wait_ge(l_x, j)
                        act.activation(xb_hi[:, j - 1, :], xbr[:, j - 1, :], ACT.Copy).then_inc(l_hi, 1)
                st.split_ahead(i, k)
            act.wait_ge(l_x, NL)
            act.activation(xb_hi[:, NL - 1, :], xbr[:, NL - 1, :], ACT.Copy).then_inc(l_hi, 1)
            st = stage["lru_gate"]
            for t in range(2 * NL):
                h = t // 2
                gate_ready(act, t)
                dst, bias = (gx, "lru_bgx") if t % 2 == 0 else (ga, "lru_bga")
                act.activation(dst[:, h, :], bank[t % 4][:], ACT.Sigmoid, bias=col(bias, h)).then_inc(bank_free, 1)
                if t % 4 == 3:
                    split_hi(0, st.u0 + t // 4 + RING)
            lam = col("lru_lam", 0, NL)
            own.link(act.activation(lam8[:, 0, :], lam, ACT.Abs))
            act.activation(lam8[:, 1, :], lam8[:, 0, :], ACT.Exp, scale=-1.0).then_inc(l_lam, 1)
            act.wait_ge(l_lam, 2)
            act.activation(lam8[:, 3, :], lam8[:, 2, :], ACT.Ln).then_inc(l_lam, 1)
            act.wait_ge(l_lam, 4)
            for k in range(NL):
                own.link(act.activation(lth[:, k, :], ga[:, k, :], ACT.Tanh, scale=lam8[:, 1, k:k + 1]))
                act.activation(ga[:, k, :], ga[:, k, :], ACT.Exp, scale=lam8[:, 0, k:k + 1]).then_inc(l_a, 1)
            for k in range(NL):
                act.wait_ge(l_q, k + 1)
                act.activation(lth[:, k, :], lth[:, k, :], ACT.Sqrt).then_inc(l_s, 1)
                if k >= 1:
                    act.wait_ge(l_h, k)
                    act.activation(lo_hi[:, k - 1, :], lh[:, k - 1, :], ACT.Copy).then_inc(l_ph, 1)
            act.wait_ge(l_h, NL)
            act.activation(lo_hi[:, NL - 1, :], lh[:, NL - 1, :], ACT.Copy).then_inc(l_ph, 1)
            so = stage["lru_out"]
            split_only(act, so, 4)
            post1.act(act, lambda a, k: so.freed(a, k))

        def lru_dve(dve, own):
            st = stage["lru_in"]
            for j in range(NL):
                e = j % 2
                st.freed(dve, NL + j)
                src, cv = ltap[:, e, :], xbr[:, j, :]
                own.link(dve.tensor_scalar(cv, src, col("lru_conv", 5 * j + 3), col("lru_conv", 5 * j + 4), ALU.mult,
                                           ALU.add))
                for n in (1, 2, 3):
                    ins = dve.scalar_tensor_tensor(out=xbr[:, j, n:T], in0=ltap[:, e, 0:T - n],
                                                   scalar=col("lru_conv", 5 * j + 3 - n), in1=xbr[:, j, n:T],
                                                   op0=ALU.mult, op1=ALU.add)
                    if n < 3:
                        own.link(ins)
                    else:
                        ins.then_inc(l_x, 1)
                if j >= 1:
                    dve.wait_ge(l_hi, j)
                    dve.tensor_tensor(xb_lo[:, j - 1, :], xbr[:, j - 1, :], xb_hi[:, j - 1, :].bitcast(F32),
                                      ALU.subtract).then_inc(l_lo, 1)
            dve.wait_ge(l_hi, NL)
            dve.wait_ge(l_x, NL)
            dve.tensor_tensor(xb_lo[:, NL - 1, :], xbr[:, NL - 1, :], xb_hi[:, NL - 1, :].bitcast(F32),
                              ALU.subtract).then_inc(l_lo, 1)
            lam = col("lru_lam", 0, NL)
            v0, u, v, ln = (lam8[:, n, :] for n in range(4))
            dve.wait_ge(l_lam, 1)
            dve.tensor_scalar(v, u, 1.0, None, ALU.add).then_inc(l_lam, 1)
            dve.wait_ge(l_lam, 3)
            own.link(dve.tensor_scalar(v, v, -1.0, 1e-30, ALU.add, ALU.max))
            own.link(dve.reciprocal(v, v))
            own.link(dve.tensor_tensor(ln, ln, u, ALU.mult))
            own.link(dve.tensor_tensor(ln, ln, v, ALU.mult))
            own.link(dve.tensor_scalar(v, u, -0.5, 1.0, ALU.mult, ALU.add))
            own.link(dve.tensor_tensor(v, v, u, ALU.mult))
            own.link(dve.tensor_tensor(ln, ln, v, ALU.max))
            own.link(dve.scalar_tensor_tensor(out=v, in0=lam, scalar=0.0, in1=ln, op0=ALU.min, op1=ALU.subtract))
            own.link(dve.tensor_scalar(v0, v, 8.0, None, ALU.mult))
            dve.tensor_scalar(u, v, -8.0, None, ALU.mult).then_inc(l_lam, 1)
            for k in range(NL):
                dve.wait_ge(l_a, k + 1)
                own.link(dve.tensor_tensor(lh[:, k, :], ga[:, k, :], ga[:, k, :], ALU.mult))
                dve.scalar_tensor_tensor(out=lth[:, k, :], in0=lh[:, k, :], scalar=1.0, in1=lth[:, k, :], op0=ALU.add,
                                         op1=ALU.mult).then_inc(l_q, 1)
                own.link(dve.tensor_tensor(gx[:, k, :], gx[:, k, :], xbr[:, k, :], ALU.mult))
            for k in range(NL):
                dve.wait_ge(l_s, k + 1)
                own.link(dve.tensor_tensor(gx[:, k, :], gx[:, k, :], lth[:, k, :], ALU.mult))
                own.link(dve.tensor_tensor_scan(out=lh[:, k, :], data0=ga[:, k, :], data1=gx[:, k, :], initial=0.0,
                                                op0=ALU.mult, op1=ALU.add))
                dve.tensor_tensor(lh[:, k, :], lh[:, k, :], ybr[:, k, :], ALU.mult).then_inc(l_h, 1)
                if k >= 1:
                    dve.wait_ge(l_ph, k)
                    dve.tensor_tensor(lo_lo[:, k - 1, :], lh[:, k - 1, :], lo_hi[:, k - 1, :].bitcast(F32),
                                      ALU.subtract).then_inc(l_pl, 1)
            dve.wait_ge(l_ph, NL)
            dve.tensor_tensor(lo_lo[:, NL - 1, :], lh[:, NL - 1, :], lo_hi[:, NL - 1, :].bitcast(F32),
                              ALU.subtract).then_inc(l_pl, 1)
            so = stage["lru_out"]

            def body(i):
                for k in range(2):
                    t = i * 2 + k
                    so.unit_ready(dve, i, 2 * k + 1)
                    dst = mT[:, t, :] if isinstance(t, int) else mT[:, bass.ds(t, 1), :].squeeze(1)
                    dve.tensor_scalar(dst, bank[k][:], col("lru_bout", t), None, ALU.add).then_inc(bank_free, 1)

            repeat(dve, 4, body)
            post1.dve(dve)

        e_lb, e_f, e_ln, e_b, e_eb, e_q, e_enb, e_kd, e_d, e_k2e, e_k2 = (
            sem("e_" + s) for s in ("lb", "f", "ln", "b", "eb", "q", "enb", "kd", "d", "k2e", "k2"))
        e_tr, e_vn, e_at, e_am, e_ds, e_st, e_o, e_og = (sem("e_" + s) for s in ("tr", "vn", "at", "am", "ds", "st", "o", "og"))
        v_zero, v_in, v_prm, v_exp, v_bb, v_tr, v_wb, v_bu, v_cp, v_s, v_y = (
            sem("v_" + s) for s in ("zero", "in", "prm", "exp", "bb", "tr", "wb", "bu", "cp", "s", "y"))
        u_y, u_z, u_hi, u_lo, u_sg, u_o, u_ohi, u_olo = (sem("u_" + s) for s in ("y", "z", "hi", "lo", "sg", "o", "ohi", "olo"))
        norm2 = pre("mix_g2", 0)
        hnorm = [Norm(1, (lambda k, h=h: otmp[:, h % 2, :]), (lambda k, h=h: col("hgrn_g", h)), P, "split",
                      (lambda k, h=h: h_hi[:, h, :]), (lambda k, h=h: h_lo[:, h, :]),
                      squared=(lambda k, h=h: bank[2 + h % 2][:])) for h in range(HG)]
        ffn_pre2 = pre("ffn_g2", 0)
        ffn2 = FFN(2, (12, 10), "silu", "ffn2_0", ffn_pre2)
        norm3 = pre("mix_g2", 1)

        def even_pe(pe):
            st = stage["ev_in"]

            def body(i):
                for k in range(4):
                    t = i * 4 + k
                    st.pe_start(pe, t)
                    first = isinstance(t, int) and t == 0
                    st.pe_tile(pe, bank[k][:], i, k, rhs_h, (lambda kt: norm2.lo_ready(pe, kt)) if first else None)

            repeat(pe, 5, body)
            w(pe, bank_free, st.t0 + 20)
            for h in range(HG):
                w(pe, e_k2, h + 1)
                w(pe, e_vn, h)
                for c in range(NC):
                    pe.transpose(chunk(bank[4], c), chunk(ev[:, 8 + h, :], c), ident[:])
                for c in range(NC):
                    last = pe.transpose(chunk(bank[5], c), chunk(k2[:, h, :], c), ident[:])
                last.then_inc(e_tr, 1)
                w(pe, e_am, h)
                w(pe, e_kd, h + 1)
                w(pe, e_q, h + 1)
                for c in range(NC):
                    last = pe.matmul(chunk(bank[6], c), chunk(kd[:, h, :], c), chunk(ev[:, 12 + h, :], c), start=True,
                                     stop=True)
                last.then_inc(e_at, 1)
                w(pe, e_vn, h + 1)
                w(pe, e_st, 7 * h)
                for n in range(8):
                    r = slice(64 * (n % 2), 64 * (n % 2) + 64)
                    last = pe.matmul(chunk(bank[n % 2], n // 2), kN[r, h % 2, n // 2 * P:n // 2 * P + P],
                                     vN[r, h % 2, n // 2 * P:n // 2 * P + P], start=True, stop=True)
                last.then_inc(e_ds, 1)
                w(pe, e_am, h + 1)
                w(pe, e_st, 7 * h + 7)
                w(pe, e_og, h - 1)
                w(pe, n_mm, hnorm[0].sq0 + h - 1)
                o = bank[2 + h % 2]
                for c in range(NC):
                    pe.matmul(chunk(o, c), chunk(vN[:, h % 2, :], c), chunk(attT[:, h % 2, :], c), start=True, stop=False)
                    for n in (2 * c, 2 * c + 1):
                        if n:
                            last = pe.matmul(o[:, 64 * n:64 * n + 64], stS[:, h % 2, n - 1, :],
                                             ev[:, 12 + h, 64 * n:64 * n + 64], start=False, stop=n % 2 == 1)
                last.then_inc(e_o, 1)
                if h:
                    hnorm[h - 1].pe(pe)
            hnorm[HG - 1].pe(pe)
            w(pe, v_bb, 1)
            for c in range(2):
                for j in range(4):
                    last = pe.transpose(chunk(bank[4 + c], j), bbar[:, c, 4 * j:4 * j + 4, :].rearrange("p a b -> p (a b)"),
                                        ident[:])
            last.then_inc(v_tr, 1)
            w(pe, v_wb, 1)
            for i in range(S5T + 1):
                if i < S5T:
                    w(pe, v_cp, 2 * (i - 1))
                    r = slice(32 * (i % 4), 32 * (i % 4) + 32)
                    for c in range(2):
                        last = pe.matmul(bank[4 + 2 * (i % 2) + c][:], wb[r, c, i // 4, :], ev[r, i // 4, :], start=True,
                                         stop=True)
                    last.then_inc(v_bu, 1)
                if i:
                    q = i - 1
                    w(pe, v_s, q + 1)
                    o = bank[q // 4][32 * (q % 4):32 * (q % 4) + 32, :]
                    pe.matmul(o, cc[:, 0, q, :], sbuf[q % 2][1][0][:, 256:768], start=True, stop=False)
                    pe.matmul(o, cc[:, 1, q, :], sbuf[q % 2][1][1][:, 256:768], start=False, stop=True).then_inc(v_y, 1)
            st = stage["glu"]
            for t in range(4):
                s, b0 = (st.u0 + t // 2) % RING, 4 * (t % 2)
                if b0 == 0:
                    w(pe, split_done, st.u0 + t // 2 + 1)
                for kt in range(4):
                    if t == 0:
                        w(pe, u_lo, kt + 1)
                    wh, wl = (m[:, s, (b0 + kt) * P:(b0 + kt + 1) * P] for m in (whi, wlo))
                    pe.matmul(bank[t][:], wh, z_hi[:, kt, :], start=kt == 0, stop=False)
                    pe.matmul(bank[t][:], wh, z_lo[:, kt, :], start=False, stop=False)
                    last = pe.matmul(bank[t][:], wl, z_hi[:, kt, :], start=False, stop=kt == 3)
                last.then_inc(unit_done if t % 2 else g_lu, 1)
            st = stage["ev_out"]
            for t in range(8):
                st.pe_start(pe, t)
                ready = (lambda kt: w(pe, n_lo, hnorm[kt].h0 + 1) if kt < 4 else w(pe, u_olo, kt - 3)) if t == 0 else None
                st.pe_tile(pe, bank[t % 4][:], t // 4, t % 4, rhs_h, ready)

        g_lu = sem("glu_half")

        def even_act(act, own):
            st = stage["ev_in"]
            act.wait_ge(e_lb, 1)
            act.activation(lbv[:, 0:2, :], lbv[:, 0:2, :], ACT.Exp).then_inc(e_lb, 1)
            for t in range(20):
                i, k = t // 4, t % 4
                st.unit_ready(act, i, k)
                f = (ACT.Copy, ACT.Sigmoid, ACT.Copy, ACT.Copy, ACT.Silu)[t // 4]
                act.activation(ev[:, t, :], bank[k][:], f).then_inc(bank_free, 1)
                st.split_ahead(i, k)
            for h in range(HG):
                act.wait_ge(e_f, h + 1)
                act.activation(bcum[:, h, :], bcum[:, h, :], ACT.Ln).then_inc(e_ln, 1)
            for h in range(HG):
                act.wait_ge(e_b, h + 1)
                act.activation(kd[:, h, :], bcum[:, h, :], ACT.Exp).then_inc(e_eb, 1)
                own(act.activation(dec[:, h, :], bcum[:, h, 63:T:64], ACT.Exp))
                act.wait_ge(e_d, h + 1)
                act.activation(k2[:, h, :], k2[:, h, :], ACT.Exp).then_inc(e_k2e, 1)
                act.wait_ge(e_q, h + 1)
                act.activation(kd[:, h, :], bcum[:, h, :], ACT.Exp, scale=-1.0).then_inc(e_enb, 1)
            for h in range(HG):
                hnorm[h].act(act, lambda a, k, h=h: a.wait_ge(e_o, h + 1))
            act.wait_ge(v_zero, 1)
            for n, c in enumerate(("re", "im")):
                for e in range(2):
                    r = slice(64 * e, 64 * e + 64)
                    act.dma_start(braw[r, n, :, 16 * e:16 * e + 16], dram[f"s5_b_{c}"][r]).then_inc(v_in, 16)
                    act.dma_start(cc[r, n, :, 16 * e:16 * e + 16], dram[f"s5_c_{c}"][r]).then_inc(v_in, 16)
            act.wait_ge(v_prm, 1)
            own.link(act.activation(s5c[:, 0, :], col("s5_logdt", 0, S5T), ACT.Exp))
            act.activation(s5c[:, 1, :], col("s5_are", 0, S5T), ACT.Copy).then_inc(v_exp, 1)
            act.wait_ge(v_prm, 2)
            own.link(act.activation(s5c[:, 4, :], s5c[:, 2, :], ACT.Exp))
            act.activation(s5c[:, 5:7, :], s5c[:, 5:7, :], ACT.Sin).then_inc(v_exp, 1)
            for i in range(S5T):
                act.wait_ge(v_bu, i + 1)
                w(act, v_s, i - 1)
                w(act, v_y, i - 1)
                for c in range(2):
                    act.activation(sbuf[i % 2][0][c][:, 256:768], bank[4 + 2 * (i % 2) + c][:], ACT.Copy).then_inc(v_cp, 1)
            for j in range(4):
                act.wait_ge(u_y, j + 1)
                own.link(act.activation(zf[:, j, :], zf[:, j, :], ACT.Gelu_apprx_tanh))
                act.activation(z_hi[:, j, :], zf[:, j, :], ACT.Copy).then_inc(u_hi, 1)
            st = stage["glu"]

            def out_high(t):
                act.wait_ge(u_o, t + 1)
                act.activation(h_hi[:, 4 + t, :], zf[:, t, :], ACT.Copy).then_inc(u_ohi, 1)

            for t in range(4):
                if t % 2:
                    act.wait_ge(unit_done, st.u0 + t // 2 + 1)
                else:
                    act.wait_ge(g_lu, t // 2 + 1)
                w(act, u_o, t - 1)
                act.activation(otmp[:, t % 2, :], bank[t][:], ACT.Sigmoid, bias=col("b_glu", t)).then_inc(bank_free, 1)
                if t % 2:
                    split_hi(0, st.u0 + t // 2 + RING)
                if t:
                    out_high(t - 1)
            out_high(3)
            split_only(act, stage["ev_out"], 2)

        def even_dve(dve, own):
            st = stage["ev_in"]
            l0, l1 = col("lb", 0, 4), col("lb", 4, 4)
            own.link(dve.tensor_tensor(lbv[:, 2, :], l0, l1, ALU.max))
            own(dve.tensor_tensor(lbv[:, 0, :], l0, lbv[:, 2, :], ALU.subtract))
            dve.tensor_tensor(lbv[:, 1, :], l1, lbv[:, 2, :], ALU.subtract).then_inc(e_lb, 1)
            own(dve.memset(seg64[:], 1.0))
            own(dve.memset(attT[:], 0.0))
            dve.wait_ge(e_lb, 2)
            own.link(dve.tensor_tensor(lbv[:, 1, :], lbv[:, 0, :], lbv[:, 1, :], ALU.add))
            own.link(dve.reciprocal(lbv[:, 1, :], lbv[:, 1, :]))
            own.link(dve.tensor_tensor(lbv[:, 0, :], lbv[:, 0, :], lbv[:, 1, :], ALU.mult))
            own.link(dve.tensor_scalar(lbv[:, 3, :], lbv[:, 0, :], -1.0, 1.0, ALU.mult, ALU.add))
            own.link(dve.memset(seg64[:, 0:T:64], 0.0))
            for h in range(HG):
                st.freed(dve, 4 + h)
                own.link(dve.tensor_scalar(bcum[:, h, :], ev[:, 4 + h, :], lbv[:, 3, h:h + 1], lbv[:, 0, h:h + 1],
                                           ALU.mult, ALU.add))
                dve.tensor_scalar(ev[:, 4 + h, :], bcum[:, h, :], -1.0, 1.0, ALU.mult, ALU.add).then_inc(e_f, 1)
            for h in range(HG):
                dve.wait_ge(e_ln, h + 1)
                own.sync()
                dve.tensor_tensor_scan(out=bcum[:, h, :], data0=seg64[:], data1=bcum[:, h, :], initial=0.0, op0=ALU.mult,
                                       op1=ALU.add).then_inc(e_b, 1)
                dve.wait_ge(e_b, h + 1)
                b3 = bcum[:, h, :].rearrange("p (c l) -> p c l", l=64)
                dve.tensor_tensor(k2[:, h, :].rearrange("p (c l) -> p c l", l=64), b3[:, :, 63:64].broadcast_to((P, 8, 64)),
                                  b3, ALU.subtract).then_inc(e_d, 1)
            for h in range(HG):
                dve.wait_ge(e_eb, h + 1)
                st.freed(dve, 12 + h)
                dve.tensor_tensor(ev[:, 12 + h, :], ev[:, 12 + h, :], kd[:, h, :], ALU.mult).then_inc(e_q, 1)
                dve.wait_ge(e_enb, h + 1)
                dve.tensor_tensor(kd[:, h, :], kd[:, h, :], ev[:, 4 + h, :], ALU.mult).then_inc(e_kd, 1)
                dve.wait_ge(e_k2e, h + 1)
                dve.tensor_tensor(k2[:, h, :], k2[:, h, :], ev[:, 4 + h, :], ALU.mult).then_inc(e_k2, 1)
            for h in range(HG):
                dve.wait_ge(e_tr, h + 1)
                w(dve, e_o, h - 1)
                own(dve.tensor_copy(vN[:, h % 2, :], bank[4][:]))
                dve.tensor_copy(kN[:, h % 2, :], bank[5][:]).then_inc(e_vn, 1)
                dve.wait_ge(e_at, h + 1)
                dve.copy_predicated(attT[:, h % 2, :].rearrange("p (c l) -> p c l", c=NC),
                                    pair_mask[:].unsqueeze(1).broadcast_to((P, NC, P)),
                                    bank[6][:].rearrange("p (c l) -> p c l", c=NC)).then_inc(e_am, 1)
                dve.wait_ge(e_ds, h + 1)
                for n in range(7):
                    src = chunk(bank[n % 2], n // 2)
                    if n == 0:
                        dve.tensor_copy(stS[:, h % 2, 0, :], src).then_inc(e_st, 1)
                    else:
                        dve.wait_ge(e_st, 7 * h + n)
                        dve.scalar_tensor_tensor(out=stS[:, h % 2, n, :], in0=stS[:, h % 2, n - 1, :],
                                                 scalar=dec[:, h, n:n + 1], in1=src, op0=ALU.mult,
                                                 op1=ALU.add).then_inc(e_st, 1)
                if h:
                    hnorm[h - 1].dve(dve)
                dve.wait_ge(n_sq, hnorm[h].sq0 + 1)
                st.freed(dve, 16 + h)
                dve.tensor_tensor(otmp[:, h % 2, :], ev[:, 16 + h, :], bank[2 + h % 2][:], ALU.mult).then_inc(e_og, 1)
                dve.wait_ge(e_og, h + 1)
            hnorm[HG - 1].dve(dve)
            s5_prepare(dve, own)
            for i in range(S5T):
                b = sbuf[i % 2]
                dve.wait_ge(v_cp, 2 * i + 2)
                w(dve, v_y, i - 1)
                for k in range(9):
                    d = 1 << k
                    (sr, si), (dr, di) = b[k % 2], b[1 - k % 2]
                    ar, ai, nai = (apow[:, k, n, i:i + 1] for n in range(3))
                    now, ago = slice(256, 768), slice(256 - d, 768 - d)

                    def axpy(dst, src, a, plus):
                        return dve.scalar_tensor_tensor(out=dst[:, now], in0=src[:, ago], scalar=a, in1=plus[:, now],
                                                        op0=ALU.mult, op1=ALU.add)

                    own(axpy(dr, sr, ar, sr))
                    own(axpy(di, si, ar, si))
                    dve.wait_ge(dve_own, own.n - 1)
                    own(axpy(dr, si, nai, dr))
                    dve.wait_ge(dve_own, own.n - 1)
                    if k < 8:
                        own.link(axpy(di, sr, ai, di))
                    else:
                        axpy(di, sr, ai, di).then_inc(v_s, 1)
            for j in range(4):
                dve.wait_ge(v_y, 4 * j + 4)
                dve.scalar_tensor_tensor(out=zf[:, j, :], in0=ev[:, j, :], scalar=col("s5_d", j), in1=bank[j][:],
                                         op0=ALU.mult, op1=ALU.add).then_inc(u_y, 1)
            for j in range(4):
                dve.wait_ge(u_hi, j + 1)
                dve.tensor_tensor(z_lo[:, j, :], zf[:, j, :], z_hi[:, j, :].bitcast(F32), ALU.subtract).then_inc(u_lo, 1)
            st = stage["glu"]

            def out_low(t):
                dve.wait_ge(u_ohi, t + 1)
                dve.tensor_tensor(h_lo[:, 4 + t, :], zf[:, t, :], h_hi[:, 4 + t, :].bitcast(F32),
                                  ALU.subtract).then_inc(u_olo, 1)

            dve.wait_ge(u_lo, 4)
            for t in range(4):
                st.freed(dve, t)
                dve.tensor_tensor(zf[:, t, :], zf[:, t, :], otmp[:, t % 2, :], ALU.mult).then_inc(u_o, 1)
                if t:
                    out_low(t - 1)
            out_low(3)
            onto_residual(dve, stage["ev_out"])

        def onto_residual(dve, st):
            for t in range(8):
                st.unit_ready(dve, t // 4, t % 4)
                dve.tensor_tensor(xT[:, t, :], xT[:, t, :], bank[t % 4][:], ALU.add).then_inc(bank_free, 1)

        def reduced(dve, own, dst, k, src, quarter):
            own.link(dve.tensor_scalar(k, src, 1.0 / (2 * math.pi), 0.25 if quarter else 0.0, ALU.mult, ALU.add))
            own.link(dve.tensor_scalar(k, k, MAGIC, MAGIC, ALU.add, ALU.subtract))
            for n, c in enumerate(TWO_PI):
                own.link(dve.scalar_tensor_tensor(out=dst, in0=k, scalar=-c, in1=dst if n else src, op0=ALU.mult,
                                                  op1=ALU.add))
            if quarter:
                own.link(dve.tensor_scalar(dst, dst, math.pi / 2, None, ALU.add))
            own.link(dve.tensor_scalar(dst, dst, 3.1415925, -3.1415925, ALU.min, ALU.max))

        def s5_prepare(dve, own):
            q = lambda n: s5c[:, n, :]
            are, aim = col("s5_are", 0, S5T), col("s5_aim", 0, S5T)

            def tt(o, a, b, op):
                own.link(dve.tensor_tensor(o, a, b, op))

            own.sync()
            dve.wait_ge(n_lo, hnorm[-1].h0 + 1)
            own(dve.memset(braw[:], 0.0))
            own(dve.memset(cc[:], 0.0))
            for par in sbuf:
                for pair in par:
                    for one in pair:
                        own(dve.memset(one[:, 0:256], 0.0))
            own.sync()
            dve.engine_nop().then_inc(v_zero, 1)
            dve.engine_nop().then_inc(v_prm, 1)
            dve.wait_ge(v_exp, 1)
            tt(q(2), q(1), q(0), ALU.mult)
            tt(q(3), aim, q(0), ALU.mult)
            reduced(dve, own, q(5), q(7), q(3), False)
            reduced(dve, own, q(6), q(7), q(3), True)
            dve.engine_nop().then_inc(v_prm, 1)
            dve.wait_ge(v_exp, 2)
            tt(apow[:, 0, 0, :], q(4), q(6), ALU.mult)
            tt(apow[:, 0, 1, :], q(4), q(5), ALU.mult)
            xr, xi = q(8), apow[:, 0, 1, :]
            own.link(dve.tensor_scalar(xr, apow[:, 0, 0, :], -1.0, None, ALU.add))
            tt(q(9), are, are, ALU.mult)
            tt(q(10), aim, aim, ALU.mult)
            tt(q(9), q(9), q(10), ALU.add)
            own.link(dve.reciprocal(q(9), q(9)))
            tt(q(10), xr, are, ALU.mult)
            tt(q(11), xi, aim, ALU.mult)
            tt(q(10), q(10), q(11), ALU.add)
            tt(q(10), q(10), q(9), ALU.mult)
            tt(q(11), xi, are, ALU.mult)
            tt(q(12), xr, aim, ALU.mult)
            tt(q(11), q(11), q(12), ALU.subtract)
            tt(q(11), q(11), q(9), ALU.mult)
            for k in range(9):
                ar, ai, nai = (apow[:, k, n, :] for n in range(3))
                own.link(dve.tensor_scalar(nai, ai, -1.0, None, ALU.mult))
                if k < 8:
                    nr, ni = (apow[:, k + 1, n, :] for n in range(2))
                    tt(q(12), ar, ar, ALU.mult)
                    tt(q(13), ai, ai, ALU.mult)
                    tt(nr, q(12), q(13), ALU.subtract)
                    tt(q(12), ar, ai, ALU.mult)
                    own.link(dve.tensor_scalar(ni, q(12), 2.0, None, ALU.mult))
            dve.wait_ge(v_in, 16 * 8)
            wide = lambda a: a.unsqueeze(2).broadcast_to((P, S5T, 32))
            tt(bbar[:, 0], braw[:, 0], wide(q(10)), ALU.mult)
            tt(btmp[:], braw[:, 1], wide(q(11)), ALU.mult)
            tt(bbar[:, 0], bbar[:, 0], btmp[:], ALU.subtract)
            tt(bbar[:, 1], braw[:, 1], wide(q(10)), ALU.mult)
            tt(btmp[:], braw[:, 0], wide(q(11)), ALU.mult)
            tt(bbar[:, 1], bbar[:, 1], btmp[:], ALU.add)
            own.link(dve.tensor_scalar(cc[:, 1], cc[:, 1], -1.0, None, ALU.mult))
            dve.engine_nop().then_inc(v_bb, 1)
            dve.wait_ge(v_tr, 1)
            own(dve.tensor_copy(wb[:, 0].rearrange("p a b -> p (a b)"), bank[4][:]))
            dve.tensor_copy(wb[:, 1].rearrange("p a b -> p (a b)"), bank[5][:]).then_inc(v_wb, 1)

        a_pos, a_ang, a_trig, a_rot, a_kz = (sem("a_" + s) for s in ("pos", "ang", "trig", "rot", "kz"))
        a_s, a_m, a_p, a_n, a_t, a_pt, a_o, a_oh, a_ol = (
            sem("a_" + s) for s in ("s", "m", "p", "n", "t", "pt", "o", "oh", "ol"))
        qn = Norm(3, lambda k: od[:, k, :], lambda k: col("q_g", k), 384, "split", lambda k: cq_hi[:, k, :],
                  lambda k: cq_lo[:, k, :])
        kvn = Norm(2, lambda k: od[:, 3 + k, :], lambda k: col("kv_g", k), 256, "split", lambda k: ck_hi[:, k, :],
                   lambda k: ck_lo[:, k, :])
        ffn_pre3 = pre("ffn_g2", 1)
        ffn3 = FFN(3, (12, 10), "silu", "ffn2_1", ffn_pre3)
        final = Norm(KD, in_x, lambda k: col("final_g", k), D, "final")
        SCALE = 192.0 ** -0.5
        NA = MLA_H * NC

        def small_stage_pe(pe, st, tiles, per_unit, kts, operands, ready):
            for t in range(tiles):
                st.pe_start(pe, t)
                u, j = t // per_unit, t % per_unit
                s = (st.u0 + u) % RING
                if j == 0:
                    pe.wait_ge(split_done, st.u0 + u + 1)
                for kt in range(kts):
                    if t == 0:
                        ready(kt)
                    (ah, al), (bh, bl) = operands(s, j, kt, t)
                    pe.matmul(bank[t % 4][:], ah, bh, start=kt == 0, stop=False)
                    pe.matmul(bank[t % 4][:], ah, bl, start=False, stop=False)
                    last = pe.matmul(bank[t % 4][:], al, bh, start=False, stop=kt == kts - 1)
                if j == per_unit - 1:
                    last.then_inc(unit_done, 1)

        def small_stage_act(act, st, tiles, per_unit, dst):
            for t in range(tiles):
                act.wait_ge(unit_done, st.u0 + t // per_unit + 1)
                act.activation(dst(t), bank[t % 4][:], ACT.Copy).then_inc(bank_free, 1)
                if t % per_unit == per_unit - 1:
                    split_hi(0, st.u0 + t // per_unit + RING)

        def block(m, s, b):
            return m[:, s, b * P:b * P + P]

        def mla_pe(pe):
            st = stage["od_in"]
            for t in range(7):
                st.pe_start(pe, t)
                st.pe_tile(pe, bank[t % 4][:], t // 4, t % 4, rhs_h, (lambda kt: norm3.lo_ready(pe, kt)) if t == 0 else None)
            qn.pe(pe)
            kvn.pe(pe)
            small_stage_pe(pe, stage["uq"], 12, 2, 3,
                           lambda s, j, kt, t: ((block(whi, s, 3 * j + kt), block(wlo, s, 3 * j + kt)),
                                                (cq_hi[:, kt, :], cq_lo[:, kt, :])), lambda kt: qn.lo_ready(pe, kt))
            small_stage_pe(pe, stage["uk"], 8, 4, 2,
                           lambda s, j, kt, t: ((block(whi, s, 2 * j + kt), block(wlo, s, 2 * j + kt)),
                                                (ck_hi[:, kt, :], ck_lo[:, kt, :])), lambda kt: kvn.lo_ready(pe, kt))
            small_stage_pe(pe, stage["uv"], 8, 4, 2,
                           lambda s, j, kt, t: ((chunk(ck_hi[:, kt, :], t % 4), chunk(ck_lo[:, kt, :], t % 4)),
                                                (whi[:, s, 512 * kt:512 * kt + 512], wlo[:, s, 512 * kt:512 * kt + 512])),
                           lambda kt: None)
            pe.wait_ge(bank_free, TILE0["od_out"])

            def scores(n):
                h, b = n // NC, n % NC
                L = (b + 1) * P
                if n == 0:
                    pe.wait_ge(a_kz, 1)
                w(pe, a_p, n - 1)
                o = bank[4 + n % 2][:, 0:L]
                pe.matmul(o, chunk(qT[:, h, :], b), kT[:, h, 0:L], start=True, stop=False)
                pe.matmul(o, chunk(qT[:, 8 + h // 4, :], b), kz[:, 0, h % 4, 0:L], start=False, stop=False)
                pe.matmul(o, chunk(qT[:, 10 + h // 4, :], b), kz[:, 1, h % 4, 0:L], start=False, stop=True).then_inc(a_s, 1)

            def transposed(n):
                w(pe, a_n, n + 1)
                w(pe, a_pt, n - 1)
                for c in range(n % NC + 1):
                    last = pe.transpose(chunk(bank[6 + n % 2], c), chunk(prb[:, n % 2, :], c), ident[:])
                last.then_inc(a_t, 1)

            def values(n):
                h, b = n // NC, n % NC
                w(pe, a_pt, n + 1)
                if b == 0:
                    w(pe, a_oh, h - 3)
                    w(pe, a_ol, h - 3)
                for c in range(b + 1):
                    last = pe.matmul(chunk(bank[h % 4], b), vT[:, c, h * P:h * P + P], chunk(prt[:, n % 2, :], c),
                                     start=c == 0, stop=c == b)
                last.then_inc(a_o, 1)

            scores(0)
            for n in range(NA + 1):
                if n + 1 < NA:
                    scores(n + 1)
                if n:
                    values(n - 1)
                if n < NA:
                    transposed(n)
            st = stage["od_out"]
            pe.wait_ge(a_ol, MLA_H)
            for t in range(8):
                st.pe_start(pe, t)
                st.pe_tile(pe, bank[t % 4][:], t // 4, t % 4, rhs_h)

        def mla_act(act, own):
            st = stage["od_in"]
            for t in range(7):
                st.unit_ready(act, t // 4, t % 4)
                act.activation(od[:, t, :], bank[t % 4][:], ACT.Copy).then_inc(bank_free, 1)
                st.split_ahead(t // 4, t % 4)
            act.dma_start(pos_i[:], dram["positions"].broadcast_to((P, T))).then_inc(a_pos, 16)
            qn.act(act, lambda a, k: st.freed(a, k))
            kvn.act(act, lambda a, k: st.freed(a, 3 + k))
            act.wait_ge(a_ang, 1)
            act.activation(trig[:, 2:4, :], trig[:, 2:4, :], ACT.Sin).then_inc(a_trig, 1)
            small_stage_act(act, stage["uq"], 12, 2, lambda t: qT[:, t, :])
            small_stage_act(act, stage["uk"], 8, 4, lambda t: kT[:, t, :])
            small_stage_act(act, stage["uv"], 8, 4, lambda t: vT[:, t % 4, 512 * (t // 4):512 * (t // 4) + 512])

            def high(h):
                act.wait_ge(a_o, NC * h + NC)
                act.activation(h_hi[:, h, :], bank[h % 4][:], ACT.Copy).then_inc(a_oh, 1)

            for n in range(NA + 2):
                if n < NA:
                    L = (n % NC + 1) * P
                    act.wait_ge(a_m, n + 1)
                    w(act, a_t, n - 1)
                    act.activation(prb[:, n % 2, 0:L], bank[4 + n % 2][:, 0:L], ACT.Exp, bias=stat[:, 1, n:n + 1],
                                   scale=SCALE, accum_out=stat[:, 2, n:n + 1]).then_inc(a_p, 1)
                if 1 <= n <= NA:
                    L = ((n - 1) % NC + 1) * P
                    act.wait_ge(a_t, n)
                    w(act, a_o, n - 2)
                    act.activation(prt[:, (n - 1) % 2, 0:L], bank[6 + (n - 1) % 2][:, 0:L], ACT.Copy).then_inc(a_pt, 1)
                if n >= 2 and (n - 2) % NC == NC - 1:
                    high((n - 2) // NC)
            split_only(act, stage["od_out"], 2)

        def mla_dve(dve, own):
            st = stage["od_in"]
            qn.dve(dve)
            kvn.dve(dve)
            dve.wait_ge(a_pos, 16)
            own.link(dve.tensor_copy(trig[:, 0, :], pos_i[:]))
            own.link(dve.tensor_scalar(trig[:, 0, :], trig[:, 0, :], col("freq"), None, ALU.mult))
            reduced(dve, own, trig[:, 2, :], trig[:, 1, :], trig[:, 0, :], False)
            reduced(dve, own, trig[:, 3, :], trig[:, 1, :], trig[:, 0, :], True)
            dve.engine_nop().then_inc(a_ang, 1)
            dve.wait_ge(a_trig, 1)
            sin, cos = trig[:, 2, :], trig[:, 3, :]

            def rotate(o1, o2, r1, r2, in_place):
                a, b = rtmp[:, 0, :], rtmp[:, 1, :]
                own(dve.tensor_tensor(a, r1, sin, ALU.mult))
                own(dve.tensor_tensor(b, r2, sin, ALU.mult))
                own.sync()
                own(dve.tensor_tensor(o1, r1, cos, ALU.mult))
                own(dve.tensor_tensor(o2, r2, cos, ALU.mult))
                own.sync()
                own(dve.tensor_tensor(o1, o1, b, ALU.subtract))
                own(dve.tensor_tensor(o2, o2, a, ALU.add))
                own.sync()

            st.freed(dve, 6)
            rotate(krot[:, 0, :], krot[:, 1, :], od[:, 5, :], od[:, 6, :], False)
            uq = stage["uq"]
            dve.wait_ge(unit_done, uq.u0 + 6)
            own.link(dve.memset(kz[:], 0.0))
            for j in range(4):
                for n in range(2):
                    r = slice(32 * j, 32 * j + 32)
                    own(dve.tensor_copy(kz[r, n, j, :], krot[r, n, :]))
            uq.freed(dve, 11)
            for m in range(2):
                rotate(qT[:, 8 + m, :], qT[:, 10 + m, :], qT[:, 8 + m, :], qT[:, 10 + m, :], True)
            dve.engine_nop().then_inc(a_kz, 1)

            def row_max(n):
                b = n % NC
                s = bank[4 + n % 2]
                dve.wait_ge(a_s, n + 1)
                own.link(dve.tensor_tensor(chunk(s, b), chunk(s, b), neg_diag[:], ALU.add))
                own.link(dve.reduce_max(stat[:, 0, n:n + 1], s[:, 0:(b + 1) * P], axis=AX.X))
                dve.tensor_scalar(stat[:, 1, n:n + 1], stat[:, 0, n:n + 1], -SCALE, None, ALU.mult).then_inc(a_m, 1)

            def low(h):
                dve.wait_ge(a_oh, h + 1)
                dve.tensor_tensor(h_lo[:, h, :], bank[h % 4][:], h_hi[:, h, :].bitcast(F32), ALU.subtract).then_inc(a_ol, 1)

            row_max(0)
            for n in range(NA + 2):
                if n + 1 < NA:
                    row_max(n + 1)
                if n < NA:
                    L = (n % NC + 1) * P
                    dve.wait_ge(a_p, n + 1)
                    own.link(dve.reciprocal(stat[:, 3, n:n + 1], stat[:, 2, n:n + 1]))
                    dve.tensor_scalar(prb[:, n % 2, 0:L], prb[:, n % 2, 0:L], stat[:, 3, n:n + 1], None,
                                      ALU.mult).then_inc(a_n, 1)
                if n >= 2 and (n - 2) % NC == NC - 1:
                    low((n - 2) // NC)
            onto_residual(dve, stage["od_out"])

        block_ctx = ctx.enter_context(nc.Block())

        @block_ctx.sync
        def _(sp):
            sp.dma_start(cols[:], dram["columns"]).then_inc(x_in, 16)
            sp.dma_start(xT[:], dram["x"]).then_inc(x_in, 16)
            for name, units, width in SEGMENTS:
                u0 = UNIT0[name]

                def load(i, k):
                    s = (u0 + k) % RING
                    w(sp, split_done, i * RING + (u0 + k - RING + 1))
                    src = dram[name][i * RING + k] if isinstance(i, int) else dram[name][bass.ds(i * RING + k, 1)].squeeze(0)
                    sp.dma_start(raw[:, s, 0:width], src).then_inc(w_in[s], 16)

                def body(i):
                    for k in range(RING):
                        load(i, k)

                if units >= RING:
                    repeat(sp, units // RING, body)
                for k in range(units % RING):
                    load(units // RING, k)
            for k in range(KD):
                sp.wait_ge(n_t, final.t0 + k + 1)
                sp.dma_start(out_dram[:, k, :], xT[:, k, :]).then_inc(out_sem, 16)
            sp.wait_ge(out_sem, 16 * KD)

        @block_ctx.gpsimd
        def _(pool):
            pm = sqb[:, 0, 0:P]
            pool.memset(ident[:], 0.0).then_inc(consts, 1)
            pool.memset(neg_diag[:], 0.0).then_inc(consts, 1)
            pool.memset(causal[:], 1.0).then_inc(consts, 1)
            pool.memset(pm, 1.0).then_inc(consts, 1)
            pool.memset(ones[:], 1.0).then_inc(consts, 1)
            pool.memset(eps[:], EPS).then_inc(consts, 1)
            pool.wait_ge(consts, 6)
            pool.affine_select(out=ident[:], in_=ident[:], compare_op=ALU.not_equal, fill=1.0, base=0, pattern=[[-1, P]],
                               channel_multiplier=1).then_inc(consts, 1)
            pool.affine_select(out=neg_diag[:], in_=neg_diag[:], compare_op=ALU.is_ge, fill=NEG, base=0,
                               pattern=[[-1, P]], channel_multiplier=1).then_inc(consts, 1)
            pool.affine_select(out=causal[:], in_=causal[:], compare_op=ALU.is_ge, fill=0.0, base=0, pattern=[[1, P]],
                               channel_multiplier=-1).then_inc(consts, 1)
            pool.affine_select(out=pm, in_=pm, compare_op=ALU.is_ge, fill=0.0, base=0, pattern=[[1, P]],
                               channel_multiplier=-1).then_inc(consts, 1)
            pool.wait_ge(consts, 10)
            pool.memset(sqb[0:64, 0, 64:P], 0.0).then_inc(consts, 1)
            pool.wait_ge(consts, 11)
            pool.tensor_copy(pair_mask[:], pm).then_inc(consts, 1)

            def low(i, c):
                s = c % RING
                w(pool, hi_done, i * RING + (c + 1))
                pool.tensor_tensor(wlo[:, s, :], raw[:, s, :], whi[:, s, :].bitcast(F32), ALU.subtract)\
                    .then_inc(split_done, 1)

            def body(i):
                for c in range(RING):
                    low(i, c)

            repeat(pool, UNITS // RING, body)
            for c in range(UNITS % RING):
                low(UNITS // RING, c)

        @block_ctx.tensor
        def _(pe):
            pe.wait_ge(consts, 12)
            norm0.pe(pe)
            ssd_pe(pe)
            ffn_pre0.pe(pe)
            ffn0.pe(pe)
            ffn_post0.pe(pe)
            norm1.pe(pe)
            lru_pe(pe)
            ffn_pre1.pe(pe)
            ffn1.pe(pe)
            ffn_post1.pe(pe)
            norm2.pe(pe)
            even_pe(pe)
            ffn_pre2.pe(pe)
            ffn2.pe(pe)
            norm3.pe(pe)
            mla_pe(pe)
            ffn_pre3.pe(pe)
            ffn3.pe(pe)
            final.pe(pe)

        def residual_ready(norm):
            return lambda eng, k: w(eng, x_new, norm.x0 + k + 1)

        @block_ctx.scalar
        def _(act):
            own = Chain(act, act_own)
            act.wait_ge(consts, 12)
            act.wait_ge(x_in, 32)
            for c in range(RING):
                split_hi(0, c)
            norm0.act(act, x_given)
            ssd_act(act, own)
            ffn_pre0.act(act, residual_ready(post0))
            ffn0.act(act)
            ffn_post0.act(act, ffn0.result_ready)
            norm1.act(act, residual_ready(ffn_post0))
            lru_act(act, own)
            ffn_pre1.act(act, residual_ready(post1))
            ffn1.act(act)
            ffn_post1.act(act, ffn1.result_ready)
            norm2.act(act, residual_ready(ffn_post1))
            even_act(act, own)
            ffn_pre2.act(act, stage["ev_out"].freed)
            ffn2.act(act)
            norm3.act(act, ffn2.result_ready)
            mla_act(act, own)
            ffn_pre3.act(act, stage["od_out"].freed)
            ffn3.act(act)
            final.act(act, ffn3.result_ready)

        @block_ctx.vector
        def _(dve):
            own = Chain(dve, dve_own)
            dve.wait_ge(consts, 12)
            dve.wait_ge(x_in, 32)
            norm0.dve(dve)
            ssd_dve(dve, own)
            ffn_pre0.dve(dve)
            ffn0.dve(dve)
            ffn_post0.dve(dve)
            norm1.dve(dve)
            lru_dve(dve, own)
            ffn_pre1.dve(dve)
            ffn1.dve(dve)
            ffn_post1.dve(dve)
            norm2.dve(dve)
            even_dve(dve, own)
            ffn_pre2.dve(dve)
            ffn2.dve(dve)
            norm3.dve(dve)
            mla_dve(dve, own)
            ffn_pre3.dve(dve)
            ffn3.dve(dve)
            final.dve(dve)


def _pack(wt, ks):
    K, N = wt.shape
    a, n, q = ks[0], N // P, len(ks)
    t = wt.reshape(q, a, P, n, P).transpose(3, 0, 2, 1, 4)
    return np.ascontiguousarray(t.reshape(n * q, P, a * P))


def _group(units, g):
    n, p, c = units.shape
    return np.ascontiguousarray(units.reshape(n // g, g, p, c).transpose(0, 2, 1, 3).reshape(n // g, p, g * c))


def _cols(v):
    return v.reshape(-1, P).T


def _taps(wt, b):
    k = wt.shape[0]
    t = np.concatenate([wt, b[None]], axis=0).reshape(k + 1, -1, P)
    return t.transpose(2, 1, 0)


def _layout(a):
    seg, c = {}, {}
    win = a["ssd_w_in"][0]
    seg["ssd_dt"] = _pack(np.tile(win[:, 5120:5152], (1, 4)), (8,))
    seg["ssd_xbc"] = _pack(win[:, 2048:5120], (8,))
    seg["ssd_z"] = _pack(win[:, 0:2048], (8,))
    seg["ssd_out"] = _pack(a["ssd_w_out"][0], (8, 8))
    for f in range(2):
        up = a["ffn_w_up"][f].reshape(D, 2, 32, P).transpose(0, 2, 1, 3)
        down = a["ffn_w_down"][f]
        for h in range(2):
            seg[f"f{f}_up{h}"] = _pack(up[:, 16 * h:16 * h + 16].reshape(D, -1), (8,))
            seg[f"f{f}_dn{h}"] = _pack(down[2048 * h:2048 * h + 2048], (8, 8))
        up2 = a["ffn_w_in_2"][f].reshape(D, 2, 22, P).transpose(0, 2, 1, 3)
        down2 = a["ffn_w_out_2"][f]
        for h, (lo, hi) in enumerate(((0, 12), (12, 22))):
            seg[f"f{f + 2}_up{h}"] = _pack(up2[:, lo:hi].reshape(D, -1), (8,))
            seg[f"f{f + 2}_dn{h}"] = _pack(down2[P * lo:P * hi], ((hi - lo) // 2,) * 2)
        t = _taps(a["ffn_conv_w"][f], a["ffn_conv_b"][f]).reshape(P, 2, 32, 4).transpose(0, 2, 1, 3)
        c[f"ffn1_{f}"] = t.reshape(P, -1)
        c[f"ffn2_{f}"] = _taps(a["ffn_conv_w_2"][f], a["ffn_conv_b_2"][f]).reshape(P, -1)
    seg["lru_in"] = _pack(a["lru_w_in"][0], (8,))
    gates = np.stack([a["lru_w_gx"][0], a["lru_w_ga"][0]], axis=1).reshape(20, P, P)
    seg["lru_gate"] = _group(gates, 4)
    seg["lru_out"] = _pack(a["lru_w_out"][0], (5, 5))
    ein = a["even_w_in_2"][0].reshape(D, 5, 512)
    seg["ev_in"] = _pack(np.concatenate([ein[:, n] for n in (4, 1, 2, 0, 3)], axis=1), (8,))
    seg["glu"] = _group(_pack(a["s5_w_glu_2"][0], (4,)), 2)
    seg["ev_out"] = _pack(a["even_w_out_2"][0], (8,))
    oin = a["odd_w_in_2"][0]
    r1, r2 = oin[:, 640:672], oin[:, 672:704]
    seg["od_in"] = _pack(np.concatenate([oin[:, 0:640]] + [r1] * 4 + [r2] * 4, axis=1), (8,))
    uq = a["mla_w_uq_2"][0].reshape(384, 8, 192)
    seg["uq"] = _group(_pack(np.concatenate([uq[:, :, 0:128].reshape(384, -1), uq[:, :, 128:160].reshape(384, -1),
                                             uq[:, :, 160:192].reshape(384, -1)], axis=1), (3,)), 2)
    ukv = a["mla_w_ukv_2"][0].reshape(256, 8, 256)
    seg["uk"] = _group(_pack(ukv[:, :, 0:128].reshape(256, -1), (2,)), 4)
    uv = ukv[:, :, 128:256].reshape(2, P, 2, 512).transpose(2, 1, 0, 3)
    seg["uv"] = np.ascontiguousarray(uv.reshape(2, P, 1024))
    seg["od_out"] = _pack(a["odd_w_out_2"][0], (8,))

    for name, key in (("mix_pre", "norm_mix_pre"), ("mix_post", "norm_mix_post"), ("ffn_pre", "norm_ffn_pre"),
                      ("ffn_post", "norm_ffn_post"), ("mix_g2", "norm_mix_g_2"), ("ffn_g2", "norm_ffn_g_2"),
                      ("final_g", "final_norm_g_2"), ("ssd_norm", "ssd_norm"), ("lru_bgx", "lru_b_gx"),
                      ("lru_bga", "lru_b_ga"), ("lru_lam", "lru_lambda"), ("lru_bout", "lru_b_out"),
                      ("lb", "hgrn_lb_logits_2"), ("hgrn_g", "hgrn_norm_g_2"), ("s5_d", "s5_d_2"),
                      ("b_glu", "s5_b_glu_2"), ("q_g", "mla_q_norm_g_2"), ("kv_g", "mla_kv_norm_g_2")):
        c[name] = _cols(a[key])
    c["ssd_conv"] = _taps(a["ssd_conv_w"][0], a["ssd_conv_b"][0]).reshape(P, -1)
    c["lru_conv"] = _taps(a["lru_conv_w"][0], a["lru_conv_b"][0]).reshape(P, -1)
    c["ssd_d"] = _cols(np.repeat(a["ssd_d"][0], 64))
    c["dt_bias"] = np.tile(a["ssd_dt_bias"][0], 4)[:, None]
    c["a_log"] = np.tile(a["ssd_a_log"][0], 4)[:, None]
    c["lru_by"] = _cols(a["lru_b_in"][0, 0:LRU_W])
    c["lru_bx"] = _cols(a["lru_b_in"][0, LRU_W:])
    c["s5_are"] = _cols(a["s5_a_re_2"][0])
    c["s5_aim"] = _cols(a["s5_a_im_2"][0])
    c["s5_logdt"] = _cols(np.repeat(a["s5_log_dt_2"][0], 64))
    freqs = np.power(np.float32(10000.0), -np.arange(0, 64, 2, dtype=np.float32) / np.float32(64))
    c["freq"] = np.tile(freqs.astype(np.float32), 4)[:, None]
    seg["columns"] = np.ascontiguousarray(np.concatenate([c[n] for n, _ in COLUMNS], axis=1))
    seg["x"] = np.ascontiguousarray(a["x"][0].T.reshape(KD, P, T).transpose(1, 0, 2))
    seg["positions"] = np.ascontiguousarray(a["positions_2"])
    for name in ("b_re", "b_im"):
        seg["s5_" + name] = np.ascontiguousarray(
            a[f"s5_{name}_2"][0].reshape(16, 2, 64, 16).transpose(1, 2, 0, 3).reshape(P, 16, 16))
    for name in ("c_re", "c_im"):
        seg["s5_" + name] = np.ascontiguousarray(
            a[f"s5_{name}_2"][0].reshape(16, 2, 16, 64).transpose(1, 3, 0, 2).reshape(P, 16, 16))
    return seg


def kernel(**inputs):
    import concourse.bacc as bacc
    from concourse.bass_utils import run_bass_kernel_spmd

    arrays = _layout({k: np.asarray(v) for k, v in inputs.items()})
    nc = bacc.Bacc("TRN2", target_bir_lowering=False, num_devices=1)
    dram = {}
    for name, v in arrays.items():
        dram[name] = nc.dram_tensor(f"in_{name}", v.shape, mybir.dt.from_np(v.dtype), kind="ExternalInput").ap()
    out = nc.dram_tensor("out_x", (P, KD, T), F32, kind="ExternalOutput").ap()
    build_program(nc, dram, out)
    r = run_bass_kernel_spmd(nc, [{f"in_{k}": v for k, v in arrays.items()}], core_ids=[0])
    y = r.results[0]["out_x"]
    return np.ascontiguousarray(y.transpose(2, 1, 0).reshape(1, T, D))
```

```python
import math
from contextlib import ExitStack

import numpy as np
import concourse.bass as bass
from concourse import mybir
from concourse.alu_op_type import AluOpType as ALU

ACT = mybir.ActivationFunctionType
F32 = mybir.dt.float32
F32R = mybir.dt.float32r
I32 = mybir.dt.int32
AX = mybir.AxisListType

P = 128
T = 512
D = 1024
KD = D // P
NC = T // P
EPS = 1e-6
SSD_CH = 2048
NX = SSD_CH // P
SSD_H = 32
SSD_G = 4
LRU_W = 1280
NL = LRU_W // P
FF1 = 4096
FF2 = 2816
HG = 4
S5T = 16
S5L = 64
S5M = T // 2 // S5L
MLA_H = 8
RING = 4
BPU = 8
MAGIC = 1.5 * 2.0 ** 23
TWO_PI = (6.28125, 1.93500518798828125e-03, 2 * math.pi - 6.28125 - 1.93500518798828125e-03)
NEG = -3.0e38

COLUMNS = [
    ("mix_pre", 16), ("mix_post", 16), ("ffn_pre", 16), ("ffn_post", 16), ("mix_g2", 16), ("ffn_g2", 16),
    ("final_g", 8), ("ssd_conv", 24 * 5), ("ssd_d", 16), ("ssd_norm", 16), ("dt_bias", 1), ("a_log", 1),
    ("lru_bx", 10), ("lru_by", 10), ("lru_conv", 10 * 5), ("lru_bgx", 10), ("lru_bga", 10), ("lru_lam", 10),
    ("lru_bout", 8), ("ffn1_0", 32 * 8), ("ffn1_1", 32 * 8), ("ffn2_0", 22 * 4), ("ffn2_1", 22 * 4),
    ("lb", 8), ("hgrn_g", 4), ("s5_are", 16), ("s5_aim", 16), ("s5_logdt", 16), ("s5_d", 4), ("b_glu", 4),
    ("q_g", 3), ("kv_g", 2), ("freq", 1),
]
COL, _n = {}, 0
for _name, _w in COLUMNS:
    COL[_name] = _n
    _n += _w
NCOL = _n

SEGMENTS = [
    ("ssd_dt", 1, 1024), ("ssd_xbc", 24, 1024), ("ssd_z", 16, 1024), ("ssd_out", 16, 1024),
    ("f0_up0", 32, 1024), ("f0_dn0", 16, 1024), ("f0_up1", 32, 1024), ("f0_dn1", 16, 1024),
    ("lru_in", 20, 1024), ("lru_gate", 5, 512), ("lru_out", 16, 640),
    ("f1_up0", 32, 1024), ("f1_dn0", 16, 1024), ("f1_up1", 32, 1024), ("f1_dn1", 16, 1024),
    ("ev_in", 20, 1024), ("glu", 2, 1024), ("ev_out", 8, 1024),
    ("f2_up0", 24, 1024), ("f2_dn0", 16, 768), ("f2_up1", 20, 1024), ("f2_dn1", 16, 640),
    ("od_in", 7, 1024), ("uq", 6, 768), ("uk", 2, 1024), ("uv", 2, 1024), ("od_out", 8, 1024),
    ("f3_up0", 24, 1024), ("f3_dn0", 16, 768), ("f3_up1", 20, 1024), ("f3_dn1", 16, 640),
]
UNIT0, _n = {}, 0
for _name, _k, _w in SEGMENTS:
    UNIT0[_name] = _n
    _n += _k
UNITS = _n

TILES = [
    ("ssd_dt", 1), ("ssd_xbc", 24), ("ssd_z", 16), ("ssd_out", 8),
    ("f0_up0", 32), ("f0_dn0", 8), ("f0_up1", 32), ("f0_dn1", 8),
    ("lru_in", 20), ("lru_gate", 20), ("lru_out", 8),
    ("f1_up0", 32), ("f1_dn0", 8), ("f1_up1", 32), ("f1_dn1", 8),
    ("ev_in", 20), ("glu", 4), ("ev_out", 8),
    ("f2_up0", 24), ("f2_dn0", 8), ("f2_up1", 20), ("f2_dn1", 8),
    ("od_in", 7), ("uq", 12), ("uk", 8), ("uv", 8), ("od_out", 8),
    ("f3_up0", 24), ("f3_dn0", 8), ("f3_up1", 20), ("f3_dn1", 8),
]
TILE0, _n = {}, 0
for _name, _k in TILES:
    TILE0[_name] = _n
    _n += _k


def wait(eng, sem, value):
    if not isinstance(value, int) or value > 0:
        eng.wait_ge(sem, value)


def repeat(eng, n, body, peel_last=False):
    body(0)
    if n - peel_last > 1:
        with eng.Fori(1, n - peel_last) as i:
            body(i)
    if peel_last:
        body(n - 1)


class Chain:

    def __init__(self, eng, sem, n=0):
        self.eng, self.sem, self.n = eng, sem, n

    def __call__(self, ins):
        ins.then_inc(self.sem, 1)
        self.n += 1
        return self.n

    def sync(self):
        self.eng.wait_ge(self.sem, self.n)

    def link(self, ins):
        self(ins)
        self.sync()
        return self.n


def build_program(nc, dram, out_dram):
    ctx = ExitStack()
    with ctx:
        KB = 1024
        base = 16512
        place = {}
        for name, size in (("cols", NCOL * 4 + (-NCOL * 4) % 32), ("ident", 512), ("ones", 512), ("causal", 512),
                           ("neg_diag", 512), ("pair_mask", 512), ("eps", 32), ("x", 16 * KB), ("h", 32 * KB),
                           ("m", 16 * KB), ("raw", 16 * KB), ("whi", 16 * KB), ("wlo", 16 * KB), ("big", 88 * KB)):
            place[name] = base
            base += size
        assert base <= nc.sbuf_usable_end, base
        BIG, M_, H_ = place["big"], place["m"], place["h"]

        def at(name, offset, shape, dt=F32):
            return nc.alloc_sbuf_tensor_at(name, list(shape), dt, offset=offset)

        cols = at("cols", place["cols"], [P, NCOL])
        ident = at("ident", place["ident"], [P, P])
        ones = at("ones", place["ones"], [P, P])
        causal = at("causal", place["causal"], [P, P])
        neg_diag = at("neg_diag", place["neg_diag"], [P, P])
        pair_mask = at("pair_mask", place["pair_mask"], [P, P], I32)
        eps = at("eps", place["eps"], [P, 1])
        xT = at("xT", place["x"], [P, KD, T])
        h_hi = at("h_hi", H_, [P, KD, T], F32R)
        h_lo = at("h_lo", H_ + 16 * KB, [P, KD, T], F32R)
        mT = at("mT", M_, [P, KD, T])
        raw = at("raw", place["raw"], [P, RING, 1024])
        whi = at("whi", place["whi"], [P, RING, 1024], F32R)
        wlo = at("wlo", place["wlo"], [P, RING, 1024], F32R)
        SCR = BIG + 76 * KB
        sqb = at("sqb", SCR, [P, 2, T])
        ntmp = at("ntmp", SCR + 4 * KB, [P, 2, T])
        rms = at("rms", SCR + 8 * KB, [P, T])
        inv = at("inv", SCR + 10 * KB, [P, T])
        act_hi = at("act_hi", BIG, [P, 16, T], F32R)
        act_lo = at("act_lo", BIG + 32 * KB, [P, 16, T], F32R)
        tg = at("tg", BIG + 64 * KB, [P, 2, T])
        tv = at("tv", BIG + 68 * KB, [P, 2, T])
        pt = at("pt", BIG + 72 * KB, [P, 2, T])
        zr = at("zr", M_ + 14 * KB, [P, T])
        g_hi = at("g_hi", BIG, [P, NX, T], F32R)
        xbc = at("xbc", BIG + 32 * KB, [P, 24, T])
        g_lo = at("g_lo", BIG + 32 * KB, [P, NX, T], F32R)
        ctap = at("ctap", BIG + 80 * KB, [P, 2, T])
        t1 = at("t1", BIG + 80 * KB, [P, 2, T])
        ec = at("ec", BIG + 84 * KB, [P, 2, T])
        xdt = at("xdt", BIG, [P, NC, SSD_CH])
        dd = at("dd", M_, [32, 4, T])
        dtT = at("dtT", M_ + 8 * KB, [32, T])
        csT = at("csT", M_ + 10 * KB, [32, T])
        nat = at("nat", M_ + 12 * KB, [P, 3, NC, 32])
        etot = at("etot", M_ + 12 * KB + 1536, [P, 32, NC])
        diag = at("diag", M_ + 14 * KB, [32, 32, NC])
        acol = at("acol", M_ + 14 * KB + 512, [32, 2])
        seg128 = at("seg128", M_ + 15 * KB, [32, 2])
        bn = at("bn", M_, [P, NC, P])
        ent = at("ent", M_ + 2 * KB, [P, 3, 512])
        xdd = at("xdd", M_ + 8 * KB, [P, 512])
        xb_hi = at("xb_hi", BIG, [P, NL, T], F32R)
        xb_lo = at("xb_lo", BIG + 20 * KB, [P, NL, T], F32R)
        ybr = at("ybr", BIG + 40 * KB, [P, NL, T])
        xbr = at("xbr", BIG + 60 * KB, [P, NL, T])
        ltap = at("ltap", BIG + 80 * KB, [P, 2, T])
        lcv = at("lcv", BIG + 84 * KB, [P, 2, T])
        gx = at("gx", H_, [P, NL, T])
        ga = at("ga", H_ + 20 * KB, [P, NL, T])
        lth = at("lth", BIG, [P, NL, T])
        lh = at("lh", BIG + 20 * KB, [P, NL, T])
        lo_hi = at("lo_hi", BIG, [P, NL, T], F32R)
        lo_lo = at("lo_lo", BIG + 40 * KB, [P, NL, T], F32R)
        lam8 = at("lam8", M_ + 15 * KB, [P, 4, NL])
        ev = at("ev", BIG, [P, 20, T])
        lbv = at("lbv", M_ + 15 * KB, [P, 6, 4])
        seg64 = at("seg64", M_ + 12 * KB, [P, T])
        bcum = at("bcum", BIG + 40 * KB, [P, 4, T])
        kd = at("kd", BIG + 48 * KB, [P, 4, T])
        k2 = at("k2", BIG + 56 * KB, [P, 4, T])
        attT = at("attT", BIG + 64 * KB, [P, 2, T])
        vN = at("vN", BIG + 68 * KB, [P, 2, T])
        kN = at("kN", BIG + 72 * KB, [P, 2, T])
        stS = at("stS", M_, [P, 2, 7, P])
        dec = at("dec", M_ + 7 * KB, [P, 4, 8])
        otmp = at("otmp", M_ + 8 * KB, [P, 2, T])
        s5c = at("s5c", M_ + 14 * KB, [P, 16, S5T])
        tab = at("tab", H_ + 8 * KB, [P, 2, S5T, S5L])
        cc = at("cc", H_ + 24 * KB, [P, 2, S5T, 32])
        cca = at("cca", H_ + 28 * KB, [P, 2, S5T, 32])
        ptmp = at("ptmp", H_ + 28 * KB, [P, 2, S5T, 32])
        magt = at("magt", BIG + 8 * KB, [P, 4, 2, 4, S5L])
        bbara = at("bbara", BIG + 48 * KB, [P, 2, S5T, 32])
        mm = at("mm", BIG + 16 * KB, [P, 2, 2, 2, 4, S5L])
        sv = at("sv", BIG + 24 * KB, [P, 2, 2, 4, S5L])
        sw = at("sw", BIG + 28 * KB, [P, 2, 2, 4, S5L])
        zf = at("zf", BIG + 32 * KB, [P, 4, T])
        braw = at("braw", BIG + 40 * KB, [P, 2, S5T, 32])
        ptmp2 = at("ptmp2", BIG + 40 * KB, [P, 2, S5T, 32])
        bbar = at("bbar", BIG + 44 * KB, [P, 2, S5T, 32])
        z_hi = at("z_hi", BIG + 40 * KB, [P, 4, T], F32R)
        z_lo = at("z_lo", BIG + 48 * KB, [P, 4, T], F32R)
        om = at("om", BIG + 48 * KB, [P, 2, 2, 2, 4, S5L])
        ss = at("ss", BIG + 72 * KB, [P, 4, 2, 4, 2, S5L])
        wb = at("wb", BIG + 64 * KB, [P, 2, 2, 4, P])
        k0 = at("k0", BIG + 56 * KB, [P, 4, P])
        s5k = at("s5k", BIG + 58 * KB, [P, 2, 2, 4])
        od = at("od", BIG, [P, 7, T])
        cq_hi = at("cq_hi", BIG + 14 * KB, [P, 3, T], F32R)
        cq_lo = at("cq_lo", BIG + 20 * KB, [P, 3, T], F32R)
        ck_hi = at("ck_hi", BIG + 26 * KB, [P, 2, T], F32R)
        ck_lo = at("ck_lo", BIG + 30 * KB, [P, 2, T], F32R)
        qT = at("qT", BIG + 34 * KB, [P, 12, T])
        kT = at("kT", BIG + 60 * KB, [P, 8, T])
        pos_i = at("pos_i", M_, [P, T], I32)
        ang = at("ang", M_ + 2 * KB, [P, 2, T])
        trig = at("trig", M_ + 12 * KB, [P, 2, T])
        rtmp = at("rtmp", H_ + 14 * KB, [P, 2, T])
        krot = at("krot", H_ + 18 * KB, [P, 2, T])
        kz = at("kz", BIG, [P, 2, 4, T])
        vT = at("vT", M_, [P, NC, 1024])
        prb = at("prb", SCR, [P, 2, T])
        prt = at("prt", SCR + 4 * KB, [P, 2, T])
        stat = at("stat", SCR + 8 * KB, [P, 4, 32])

        bank = [ctx.enter_context(nc.psum_tensor(f"bank{b}", [P, T], F32)) for b in range(8)]

        def sem(name):
            return ctx.enter_context(nc.semaphore(name))

        w_in = [sem(f"w_in{s}") for s in range(RING)]
        hi_done = sem("hi_done")
        split_done = sem("split_done")
        unit_done = sem("unit_done")
        bank_free = sem("bank_free")
        x_in = sem("x_in")
        consts = sem("consts")
        out_sem = sem("out_sem")
        n_sq, n_mm, n_rms, n_inv, n_t, n_hi, n_lo = (sem("n_" + s) for s in ("sq", "mm", "rms", "inv", "t", "hi", "lo"))
        x_new = sem("x_new")
        m_new = sem("m_new")

        def w(eng, s, v):
            wait(eng, s, v)

        def split_hi(i, c):
            act = nc.scalar
            s = c % RING
            u = i * RING + c
            if isinstance(u, int) and u >= UNITS:
                return
            w(act, w_in[s], (i + c // RING + 1) * 16)
            w(act, unit_done, u - RING + 1)
            act.activation(whi[:, s, :], raw[:, s, :], ACT.Copy).then_inc(hi_done, 1)

        class Stage:

            def __init__(self, name, ks=(8,)):
                self.name, self.ks = name, ks
                self.u0, self.t0 = UNIT0[name], TILE0[name]
                self.banks = 4 if len(ks) == 1 else 2

            def split_ahead(self, i, k):
                split_hi(i, self.u0 + k + RING)

            def unit_ready(self, eng, i, k):
                w(eng, unit_done, i * RING + (self.u0 + k + 1))

            def pe_start(self, pe, t):
                if isinstance(t, int) and t < self.banks:
                    if t == 0:
                        w(pe, bank_free, self.t0)
                else:
                    w(pe, bank_free, t + (self.t0 - self.banks + 1))

            def freed(self, eng, t):
                w(eng, bank_free, t + (self.t0 + 1))

            def pe_tile(self, pe, out, i, k, rhs, ready=None):
                kt = 0
                n = sum(self.ks)
                for q, blocks in enumerate(self.ks):
                    s = (self.u0 + k + q) % RING
                    w(pe, split_done, i * RING + (self.u0 + k + q + 1))
                    for b in range(blocks):
                        if ready is not None:
                            ready(kt)
                        hi, lo = rhs(kt)
                        wh, wl = whi[:, s, b * P:b * P + P], wlo[:, s, b * P:b * P + P]
                        pe.matmul(out, wh, hi, start=kt == 0, stop=False)
                        pe.matmul(out, wh, lo, start=False, stop=False)
                        last = pe.matmul(out, wl, hi, start=False, stop=kt == n - 1)
                        kt += 1
                    last.then_inc(unit_done, 1)

            def pe_first_two(self, pe, rhs, ready):
                n, per = sum(self.ks), len(self.ks)
                self.pe_start(pe, 0)
                self.pe_start(pe, 1)
                q = b = 0
                for kt in range(n):
                    ready(kt)
                    hi, lo = rhs(kt)
                    for t in range(2):
                        s = (self.u0 + t * per + q) % RING
                        w(pe, split_done, self.u0 + t * per + q + 1)
                        wh, wl = whi[:, s, b * P:b * P + P], wlo[:, s, b * P:b * P + P]
                        pe.matmul(bank[t][:], wh, hi, start=kt == 0, stop=False)
                        pe.matmul(bank[t][:], wh, lo, start=False, stop=False)
                        last = pe.matmul(bank[t][:], wl, hi, start=False, stop=kt == n - 1)
                        if per == 1 and kt == n - 1:
                            last.then_inc(unit_done, 1)
                    b += 1
                    if b == self.ks[q]:
                        q, b = q + 1, 0
                if per > 1:
                    last.then_inc(unit_done, 2 * per)

        stage = {}
        for name, ks in (("ssd_dt", (8,)), ("ssd_xbc", (8,)), ("ssd_z", (8,)), ("ssd_out", (8, 8)),
                         ("lru_in", (8,)), ("lru_gate", (1,)), ("lru_out", (5, 5)), ("ev_in", (8,)), ("glu", (4,)),
                         ("ev_out", (8,)), ("od_in", (8,)), ("uq", (3,)), ("uk", (2,)), ("uv", (2,)), ("od_out", (8,)),
                         *((f"f{f}_up{a}", (8,)) for f in range(4) for a in range(2)),
                         ("f0_dn0", (8, 8)), ("f0_dn1", (8, 8)), ("f1_dn0", (8, 8)), ("f1_dn1", (8, 8)),
                         ("f2_dn0", (6, 6)), ("f2_dn1", (5, 5)), ("f3_dn0", (6, 6)), ("f3_dn1", (5, 5))):
            stage[name] = Stage(name, ks)

        def col(name, k=0, n=1):
            c = COL[name] + k
            if isinstance(c, int):
                return cols[:, c:c + n]
            return cols[:, bass.ds(c, n)]

        class Norm:
            count = dict(sq=0, rms=0, t=0, hi=0, x=0)

            def __init__(self, K, src, gain, n, mode, hi=None, lo=None, squared=None):
                c = Norm.count
                self.squared = squared or src
                self.K, self.src, self.gain, self.n, self.mode = K, src, gain, n, mode
                self.hi, self.lo = hi, lo
                self.sq0, self.r0, self.t0, self.h0, self.x0 = c["sq"], c["rms"], c["t"], c["hi"], c["x"]
                c["sq"] += K
                c["rms"] += 1
                c["t"] += K
                if mode == "split":
                    c["hi"] += K
                elif mode == "residual":
                    c["x"] += K

            def act(self, act, ready):
                for k in range(self.K):
                    ready(act, k)
                    w(act, n_mm, self.sq0 + k - 1)
                    act.activation(sqb[:, (self.sq0 + k) % 2, :], self.squared(k), ACT.Square).then_inc(n_sq, 1)
                w(act, n_mm, self.sq0 + self.K)
                w(act, n_inv, self.r0)
                act.activation(rms[:], bank[7][:], ACT.Sqrt, bias=eps[:], scale=1.0 / self.n).then_inc(n_rms, 1)
                if self.mode == "split":
                    for k in range(self.K):
                        w(act, n_t, self.t0 + k + 1)
                        act.activation(self.hi(k), ntmp[:, (self.t0 + k) % 2, :], ACT.Copy).then_inc(n_hi, 1)

            def pe(self, pe):
                for k in range(self.K):
                    w(pe, n_sq, self.sq0 + k + 1)
                    pe.matmul(bank[7][:], ones[:], sqb[:, (self.sq0 + k) % 2, :], start=k == 0,
                              stop=k == self.K - 1).then_inc(n_mm, 1)

            def dve(self, dve):
                w(dve, n_rms, self.r0 + 1)
                w(dve, n_t, self.t0)
                dve.reciprocal(inv[:], rms[:]).then_inc(n_inv, 1)
                w(dve, n_inv, self.r0 + 1)

                def low(k):
                    w(dve, n_hi, self.h0 + k + 1)
                    dve.tensor_tensor(self.lo(k), ntmp[:, (self.t0 + k) % 2, :], self.hi(k).bitcast(F32),
                                      ALU.subtract).then_inc(n_lo, 1)

                for k in range(self.K):
                    b = (self.t0 + k) % 2
                    if self.mode == "split" and k >= 2:
                        w(dve, n_lo, self.h0 + k - 1)
                    if self.mode == "split" and k < 2:
                        w(dve, n_lo, self.h0)
                        w(dve, x_new, self.x0)
                    if self.mode == "residual":
                        w(dve, x_new, self.x0 + k - 1 if k >= 2 else self.x0)
                        w(dve, n_lo, self.h0)
                    if self.mode == "final":
                        w(dve, x_new, self.x0)
                    dst = self.src(k) if self.mode == "final" else ntmp[:, b, :]
                    dve.scalar_tensor_tensor(out=dst, in0=self.src(k), scalar=self.gain(k), in1=inv[:],
                                             op0=ALU.mult, op1=ALU.mult).then_inc(n_t, 1)
                    if self.mode == "residual":
                        w(dve, n_t, self.t0 + k + 1)
                        dve.tensor_tensor(xT[:, k, :], xT[:, k, :], ntmp[:, b, :], ALU.add).then_inc(x_new, 1)
                    if self.mode == "split" and k >= 1:
                        low(k - 1)
                if self.mode == "split":
                    low(self.K - 1)

            def lo_ready(self, pe, k):
                w(pe, n_lo, self.h0 + k + 1)

        def in_x(k):
            return xT[:, k, :]

        def in_m(k):
            return mT[:, k, :]

        def out_h(k):
            return h_hi[:, k, :]

        def out_hl(k):
            return h_lo[:, k, :]

        def pre(name, layer):
            return Norm(KD, in_x, lambda k: col(name, layer * KD + k), D, "split", out_h, out_hl)

        def post(name, layer):
            return Norm(KD, in_m, lambda k: col(name, layer * KD + k), D, "residual")

        class FFN:

            def __init__(self, f, pairs, kind, prm, pre_norm):
                self.f, self.pairs, self.kind, self.prm, self.norm = f, pairs, kind, prm, pre_norm
                self.up = [stage[f"f{f}_up{a}"] for a in range(2)]
                self.dn = [stage[f"f{f}_dn{a}"] for a in range(2)]
                self.tap, self.gel, self.prod, self.hi, self.lo, self.c1 = (
                    sem(f"f{f}_{s}") for s in ("tap", "gate", "prod", "hi", "lo", "c1"))
                self.taps = 2 if kind == "gelu" else 1
                self.prev = [0, pairs[0]]
                self.per = 4 * self.taps

            def prm_col(self, j, c):
                return col(self.prm, j * self.per + c)

            def product(self, eng, up, j, prev):
                if self.taps == 2:
                    w(eng, self.prod, j + (prev + 1))
                else:
                    up.freed(eng, j * 2 + 1)

            def pe(self, pe):
                for a in range(2):
                    up, dn, prev = self.up[a], self.dn[a], self.prev[a]

                    def up_body(i):
                        for k in range(4):
                            t = i * 4 + k
                            if a == 0 and isinstance(t, int) and t < 2:
                                if t == 0:
                                    up.pe_first_two(pe, rhs_h, lambda kt: self.norm.lo_ready(pe, kt))
                                continue
                            up.pe_start(pe, t)
                            up.pe_tile(pe, bank[k][:], i, k, rhs_h)

                    def dn_body(i):
                        for k in range(2):
                            t = i * 2 + k
                            dn.pe_start(pe, t)
                            first = isinstance(t, int) and t == 0
                            ready = (lambda kt: w(pe, self.lo, prev + kt + 1)) if first else None
                            dn.pe_tile(pe, bank[k][:], i, 2 * k,
                                       lambda kt: (act_hi[:, kt, :], act_lo[:, kt, :]), ready)

                    repeat(pe, self.pairs[a] // 2, up_body)
                    repeat(pe, 4, dn_body)

            def act(self, act):
                func = ACT.Gelu_apprx_tanh if self.kind == "gelu" else ACT.Silu
                for a in range(2):
                    up, dn, prev = self.up[a], self.dn[a], self.prev[a]

                    def high(j, e):
                        self.product(act, up, j, prev)
                        act.activation(act_hi[:, j, :] if isinstance(j, int) else act_hi[:, bass.ds(j, 1), :],
                                       pt[:, e, :], ACT.Copy).then_inc(self.hi, 1)

                    def up_body(i):
                        for e in range(2):
                            j = i * 2 + e
                            t = j * 2
                            for v in range(2):
                                up.unit_ready(act, i, 2 * e + v)
                                if v < self.taps:
                                    if v == 0:
                                        if not isinstance(j, int) or j >= 2:
                                            self.product(act, up, j - 2, prev)
                                    act.activation((tg, tv)[v][:, e, :], bank[2 * e + v][:], ACT.Identity,
                                                   bias=self.prm_col(j + prev, 4 * v + 3),
                                                   scale=self.prm_col(j + prev, 4 * v + 2)).then_inc(self.tap, 1)
                                up.split_ahead(i, 2 * e + v)
                            if not (isinstance(j, int) and j == 0):
                                high(j - 1, 1 - e)
                            up.freed(act, t)
                            act.activation(tg[:, e, :], tg[:, e, :], func).then_inc(self.gel, 1)

                    repeat(act, self.pairs[a] // 2, up_body)
                    high(self.pairs[a] - 1, 1)
                    last = self.f == 3 and a == 1

                    def dn_body(i):
                        for k in range(4):
                            dn.unit_ready(act, i, k)
                            dn.split_ahead(i, k)

                    repeat(act, 4, dn_body, peel_last=last)

            def dve(self, dve):
                for a in range(2):
                    up, dn, prev = self.up[a], self.dn[a], self.prev[a]

                    def low(j, e):
                        w(dve, self.hi, j + (prev + 1))
                        hi = act_hi[:, j, :] if isinstance(j, int) else act_hi[:, bass.ds(j, 1), :]
                        lo = act_lo[:, j, :] if isinstance(j, int) else act_lo[:, bass.ds(j, 1), :]
                        dve.tensor_tensor(lo, pt[:, e, :], hi.bitcast(F32), ALU.subtract).then_inc(self.lo, 1)

                    def up_body(i):
                        for e in range(2):
                            j = i * 2 + e
                            for v in range(self.taps):
                                dst, src = (tg, tv)[v], bank[2 * e + v]
                                n = (j + prev) * self.taps + v
                                w(dve, self.tap, n + 1)
                                dve.scalar_tensor_tensor(
                                    out=dst[:, e, 1:T], in0=src[:, 0:T - 1], scalar=self.prm_col(j + prev, 4 * v + 1),
                                    in1=dst[:, e, 1:T], op0=ALU.mult, op1=ALU.add).then_inc(self.c1, 1)
                                w(dve, self.c1, n + 1)
                                dve.scalar_tensor_tensor(
                                    out=dst[:, e, 2:T], in0=src[:, 0:T - 2], scalar=self.prm_col(j + prev, 4 * v),
                                    in1=dst[:, e, 2:T], op0=ALU.mult, op1=ALU.add).then_inc(bank_free, 1)
                            w(dve, self.gel, j + (prev + 1))
                            w(dve, self.lo, j + (prev - 1))
                            up.freed(dve, j * 2 + (1 if self.taps == 2 else 0))
                            if self.taps == 2:
                                dve.tensor_tensor(pt[:, e, :], tg[:, e, :], tv[:, e, :],
                                                  ALU.mult).then_inc(self.prod, 1)
                            else:
                                up.unit_ready(dve, i, 2 * e + 1)
                                dve.tensor_tensor(pt[:, e, :], tg[:, e, :], bank[2 * e + 1][:],
                                                  ALU.mult).then_inc(bank_free, 1)
                            if not (isinstance(j, int) and j == 0):
                                low(j - 1, 1 - e)

                    repeat(dve, self.pairs[a] // 2, up_body)
                    low(self.pairs[a] - 1, 1)
                    onto_x = self.kind != "gelu"

                    def dn_body(i):
                        for k in range(2):
                            t = i * 2 + k
                            dn.unit_ready(dve, i, 2 * k + 1)
                            dst = (xT if onto_x else mT)[:, bass.ds(t, 1) if not isinstance(t, int) else slice(t, t + 1), :]
                            if onto_x or a == 1:
                                dve.tensor_tensor(dst, bank[k][:].unsqueeze(1), dst, ALU.add).then_inc(bank_free, 1)
                            else:
                                dve.tensor_copy(dst, bank[k][:].unsqueeze(1)).then_inc(bank_free, 1)

                    repeat(dve, 4, dn_body)

            def result_ready(self, eng, k):
                self.dn[1].freed(eng, k)

        s_tap, s_c1, s_silu = sem("conv_tap"), sem("conv_c"), sem("conv_silu")
        dt_a, dt_u, dt_w, dt_ln, dt_diff, dt_out, dt_diag = (
            sem("dt_" + s) for s in ("a", "u", "w", "ln", "diff", "out", "diag"))
        act_own, dve_own = sem("act_own"), sem("dve_own")
        tr_nat, tr_et, nat_ok, et_ok = sem("tr_nat"), sem("tr_et"), sem("nat_ok"), sem("et_ok")
        tr_x, xdt_ok, z_tanh = sem("tr_x"), sem("xdt_ok"), sem("z_tanh")
        g_cb, g_bt, g_cbm, g_bn, g_xdd, g_ds, g_ent = (
            sem("g_" + s) for s in ("cb", "bt", "cbm", "bn", "xdd", "ds", "ent"))
        p_cs, p_sub, p_min, p_ec, p_E, p_S, p_Cd, p_y, p_ev, p_g = (
            sem("p_" + s) for s in ("cs", "sub", "min", "ec", "E", "S", "Cd", "y", "ev", "g"))
        norm0 = pre("mix_pre", 0)
        gnorms = [Norm(4, (lambda k, g=g: xbc[:, 4 * g + k, :]), (lambda k, g=g: col("ssd_norm", 4 * g + k)), 512, "split",
                       (lambda k, g=g: g_hi[:, 4 * g + k, :]), (lambda k, g=g: g_lo[:, 4 * g + k, :]))
                  for g in range(SSD_G)]
        post0 = post("mix_post", 0)

        def chunk(t3, c):
            return t3[:, c * P:(c + 1) * P]

        def rhs_h(kt):
            return h_hi[:, kt, :], h_lo[:, kt, :]

        def ssd_pe(pe):
            st = stage["ssd_dt"]
            st.pe_start(pe, 0)
            st.pe_tile(pe, bank[3][:], 0, 0, rhs_h, lambda kt: norm0.lo_ready(pe, kt))
            st = stage["ssd_xbc"]

            def body(i):
                for k in range(4):
                    st.pe_start(pe, i * 4 + k)
                    st.pe_tile(pe, bank[k][:], i, k, rhs_h)

            repeat(pe, 6, body)
            pe.wait_ge(dt_out, 1)
            for n, src in enumerate((csT, dtT, dd[:, 1, :])):
                for c in range(NC):
                    last = pe.transpose(bank[4][:, (n * NC + c) * 32:(n * NC + c) * 32 + 32], src[:, c * P:(c + 1) * P],
                                        ident[0:32, 0:32])
            last.then_inc(tr_nat, 1)
            pe.wait_ge(dt_diag, 1)
            pe.matmul(bank[5][:, 0:P], ones[0:32, :], diag[:].rearrange("p a b -> p (a b)"), start=True,
                      stop=True).then_inc(tr_et, 1)
            for i in range(NX):
                pe.wait_ge(s_silu, i + 1)
                if i == 0:
                    pe.wait_ge(nat_ok, 1)
                    pe.wait_ge(et_ok, 1)
                w(pe, xdt_ok, i - 1)
                for c in range(NC):
                    last = pe.transpose(bank[4 + i % 2][:, c * P:(c + 1) * P], xbc[:, i, c * P:(c + 1) * P], ident[:])
                last.then_inc(tr_x, 1)
            zt = stage["ssd_z"]

            z_next = iter(range(NX * BPU))

            def z_blocks(n):
                for _, b in zip(range(n), z_next):
                    t, kt = b // BPU, b % BPU
                    s = (zt.u0 + t) % RING
                    if kt == 0:
                        zt.pe_start(pe, t)
                        w(pe, split_done, zt.u0 + t + 1)
                    hi, lo = rhs_h(kt)
                    wh, wl = whi[:, s, kt * P:kt * P + P], wlo[:, s, kt * P:kt * P + P]
                    o = bank[t % 4][:]
                    pe.matmul(o, wh, hi, start=kt == 0, stop=False)
                    pe.matmul(o, wh, lo, start=False, stop=False)
                    last = pe.matmul(o, wl, hi, start=False, stop=kt == BPU - 1)
                    if kt == BPU - 1:
                        last.then_inc(unit_done, 1)

            def decay_rows(i):
                for e in range(2):
                    h = 2 * i + e
                    if i == 0:
                        pe.wait_ge(xdt_ok, NX)
                    w(pe, p_sub, h - 1)
                    w(pe, p_ec, h - 1)
                    pe.matmul(bank[4 + e][:], ident[0:32, h:h + 1].broadcast_to((32, P)), csT[:], start=True,
                              stop=True).then_inc(p_cs, 1)

            for g in range(SSD_G):
                w(pe, p_ev, 4 * g)
                pe.wait_ge(s_silu, 24)
                for c in range(NC):
                    last = pe.matmul(chunk(bank[7], c), chunk(xbc[:, 16 + g, :], c), chunk(xbc[:, 20 + g, :], c),
                                     start=True, stop=True)
                last.then_inc(g_cb, 1)
                for c in range(NC):
                    last = pe.transpose(chunk(bank[6], c), chunk(xbc[:, 16 + g, :], c), ident[:])
                last.then_inc(g_bt, 1)
                for z in range(3):
                    z_blocks(4)
                    pe.wait_ge(g_xdd, 3 * g + z + 1)
                    pe.wait_ge(g_bn, g + 1)
                    if z == 0:
                        pe.wait_ge(g_cbm, g + 1)
                    if z == 2:
                        pe.wait_ge(g_ent, 3 * g + 1)
                    pe.matmul(bank[7 - z % 2][:], bn[:, z, :], xdd[:], start=True, stop=True).then_inc(g_ds, 1)
                decay_rows(4 * g)
                for q in range(4):
                    i = 4 * g + q
                    if q < 3:
                        decay_rows(i + 1)
                    z_blocks(5)
                    y = bank[6 + i % 2]
                    if q == 0:
                        pe.wait_ge(g_ent, 3 * g + 3)
                    w(pe, p_ev, i - 1)
                    for e in range(2):
                        h = 2 * i + e
                        pe.wait_ge(p_S, h + 1)
                        pe.wait_ge(p_Cd, h + 1)
                        for c in range(NC):
                            o = y[64 * e:64 * e + 64, c * P:(c + 1) * P]
                            last = pe.matmul(o, xdt[:, c, 64 * h:64 * h + 64], chunk(t1[:, e, :], c), start=True,
                                             stop=c == 0)
                            if c:
                                last = pe.matmul(o, ent[:, c - 1, 64 * (h % 8):64 * (h % 8) + 64],
                                                 chunk(ec[:, e, :], c), start=False, stop=True)
                        last.then_inc(p_y, 1)
            w(pe, p_ev, NX)
            gnorms[0].pe(pe)

            def g_ready(kt):
                if kt % 4 == 0 and kt // 4 + 1 < SSD_G:
                    gnorms[kt // 4 + 1].pe(pe)
                gnorms[kt // 4].lo_ready(pe, kt % 4)

            out_pe(pe, stage["ssd_out"], g_hi, g_lo, g_ready)
            post0.pe(pe)

        def conv_start(act, st, i, k, t, prm, per, tapbuf, shift):
            act.activation(tapbuf, bank[k][:], ACT.Identity, bias=col(prm, t * per + per - 1),
                           scale=col(prm, t * per + per - 2)).then_inc(shift, 1)

        def ssd_act(act, own):
            st = stage["ssd_dt"]
            st.unit_ready(act, 0, 0)
            act.activation(dd[:, 0, :], bank[3][0:32, :], ACT.Identity, bias=col("dt_bias")[0:32, :]).then_inc(bank_free, 1)
            split_hi(0, RING)
            act.wait_ge(bank_free, 1)
            own.link(act.activation(dd[:, 1, :], dd[:, 0, :], ACT.Abs))
            act.activation(dd[:, 1, :], dd[:, 1, :], ACT.Exp, scale=-1.0).then_inc(dt_u, 1)
            act.activation(acol[:, 0:1], col("a_log")[0:32, :], ACT.Exp).then_inc(dt_a, 1)
            act.wait_ge(dt_w, 1)
            act.activation(dd[:, 3, :], dd[:, 2, :], ACT.Ln).then_inc(dt_ln, 1)
            st = stage["ssd_xbc"]

            def silu(t, e):
                st.freed(act, t)
                dst = xbc[:, t:t + 1, :] if isinstance(t, int) else xbc[:, bass.ds(t, 1), :]
                act.activation(dst, ctap[:, e:e + 1, :], ACT.Silu).then_inc(s_silu, 1)

            def body(i):
                for k in range(4):
                    t = i * 4 + k
                    st.unit_ready(act, i, k)
                    w(act, s_silu, t - 1)
                    act.activation(ctap[:, k % 2, :], bank[k][:], ACT.Identity, bias=col("ssd_conv", t * 5 + 4),
                                   scale=col("ssd_conv", t * 5 + 3)).then_inc(s_tap, 1)
                    st.split_ahead(i, k)
                    if not (isinstance(t, int) and t == 0):
                        silu(t - 1, (k - 1) % 2)

            repeat(act, 6, body)
            silu(23, 1)
            act.wait_ge(dt_diff, 1)
            act.activation(dd[:, 1, :], dd[:, 1, :], ACT.Exp).then_inc(dt_out, 1)
            act.wait_ge(tr_et, 1)
            act.activation(etot[:].rearrange("p a b -> p (a b)"), bank[5][:, 0:P], ACT.Exp).then_inc(et_ok, 1)
            zt = stage["ssd_z"]

            def z_tanh_of(i):
                zt.unit_ready(act, i // 4, i % 4)
                w(act, p_g, i)
                act.activation(zr[:], bank[i % 4][:], ACT.Tanh, scale=0.5).then_inc(z_tanh, 1)
                zt.split_ahead(i // 4, i % 4)

            for g in range(SSD_G):
                for q in range(4):
                    i = 4 * g + q
                    for e in range(2):
                        h = 2 * i + e
                        act.wait_ge(p_sub, h + 1)
                        w(act, p_y, h - 1)
                        w(act, p_Cd, h - 1)
                        act.activation(ec[:, e, :], bank[4 + e][:], ACT.Exp).then_inc(p_ec, 1)
                        act.wait_ge(p_min, h + 1)
                        act.activation(t1[:, e, :], t1[:, e, :], ACT.Exp).then_inc(p_E, 1)
                    if q:
                        z_tanh_of(i - 1)
                z_tanh_of(4 * g + 3)
            act.wait_ge(p_g, NX)
            for g in range(SSD_G):
                gnorms[g].act(act, lambda a, k: None)
            so = stage["ssd_out"]

            def body(i):
                for k in range(4):
                    so.unit_ready(act, i, k)
                    so.split_ahead(i, k)

            repeat(act, 4, body)
            post0.act(act, lambda a, k: so.freed(a, k))

        def ssd_dve(dve, own):
            x, u, v, ln = (dd[:, n, :] for n in range(4))
            dve.wait_ge(dt_u, 1)
            dve.tensor_scalar(v, u, 1.0, None, ALU.add).then_inc(dt_w, 1)
            dve.wait_ge(dt_ln, 1)
            own.link(dve.tensor_scalar(v, v, -1.0, 1e-30, ALU.add, ALU.max))
            own.link(dve.reciprocal(v, v))
            own.link(dve.tensor_tensor(ln, ln, u, ALU.mult))
            own.link(dve.tensor_tensor(ln, ln, v, ALU.mult))
            own.link(dve.tensor_scalar(v, u, -0.5, 1.0, ALU.mult, ALU.add))
            own.link(dve.tensor_tensor(v, v, u, ALU.mult))
            own.link(dve.tensor_tensor(ln, ln, v, ALU.max))
            own.link(dve.scalar_tensor_tensor(out=dtT[:], in0=x, scalar=0.0, in1=ln, op0=ALU.max, op1=ALU.add))
            dve.wait_ge(dt_a, 1)
            own.link(dve.tensor_scalar(acol[:, 1:2], acol[:, 0:1], -1.0, None, ALU.mult))
            own.link(dve.tensor_scalar(x, dtT[:], acol[:, 1:2], None, ALU.mult))
            for c in range(NC):
                own(dve.tensor_tensor_scan(out=chunk(csT[:], c), data0=ones[0:32, :], data1=chunk(x, c), initial=0.0,
                                           op0=ALU.mult, op1=ALU.add))
            own.sync()
            cs3 = csT[:].rearrange("p (c l) -> p c l", c=NC)
            tot = cs3[:, :, P - 1:P]
            dve.tensor_tensor(dd[:, 1, :].rearrange("p (c l) -> p c l", c=NC), tot.broadcast_to((32, NC, P)), cs3,
                              ALU.subtract).then_inc(dt_diff, 1)
            dve.tensor_tensor(diag[:], ident[0:32, 0:32].unsqueeze(2).broadcast_to((32, 32, NC)),
                              tot.rearrange("p c l -> p l c").broadcast_to((32, 32, NC)), ALU.mult).then_inc(dt_diag, 1)
            st = stage["ssd_xbc"]

            def body(i):
                for k in range(4):
                    t = i * 4 + k
                    w(dve, s_tap, t + 1)
                    for n in range(3):
                        if n:
                            w(dve, s_c1, t * 2 + n)
                        ins = dve.scalar_tensor_tensor(
                            out=ctap[:, k % 2, n + 1:T], in0=bank[k][:, 0:T - n - 1], scalar=col("ssd_conv", t * 5 + 2 - n),
                            in1=ctap[:, k % 2, n + 1:T], op0=ALU.mult, op1=ALU.add)
                        ins.then_inc(s_c1 if n < 2 else bank_free, 1)

            repeat(dve, 6, body)
            dve.wait_ge(tr_nat, 1)
            dve.tensor_copy(nat[:].rearrange("p a b c -> p (a b c)"), bank[4][:, 0:3 * P]).then_inc(nat_ok, 1)
            dve.wait_ge(nat_ok, 1)

            def per_head(n, c, h0, heads):
                return nat[:, n, c, h0:h0 + heads].unsqueeze(2).broadcast_to((P, heads, 64))

            for i in range(NX):
                dve.wait_ge(tr_x, i + 1)
                dve.tensor_tensor(xdt[:, :, i * P:(i + 1) * P].rearrange("p c (e q) -> p c e q", e=2),
                                  bank[4 + i % 2][:].rearrange("p (c e q) -> p c e q", c=NC, e=2),
                                  nat[:, 1, :, 2 * i:2 * i + 2].unsqueeze(3).broadcast_to((P, NC, 2, 64)),
                                  ALU.mult).then_inc(xdt_ok, 1)
            zt = stage["ssd_z"]

            def gate(i):
                dve.wait_ge(z_tanh, i + 1)
                dve.scalar_tensor_tensor(out=zr[:], in0=zr[:], scalar=1.0, in1=bank[i % 4][:], op0=ALU.add,
                                         op1=ALU.mult).then_inc(bank_free, 1)
                zt.freed(dve, i)
                dve.wait_ge(p_ev, i + 1)
                dve.scalar_tensor_tensor(out=xbc[:, i, :], in0=xbc[:, i, :], scalar=0.5, in1=zr[:], op0=ALU.mult,
                                         op1=ALU.mult).then_inc(p_g, 1)

            def evacuate(i):
                dve.wait_ge(p_y, 2 * i + 2)
                dve.scalar_tensor_tensor(out=xbc[:, i, :], in0=xbc[:, i, :], scalar=col("ssd_d", i), in1=bank[6 + i % 2][:],
                                         op0=ALU.mult, op1=ALU.add).then_inc(p_ev, 1)

            for g in range(SSD_G):
                dve.wait_ge(xdt_ok, NX)
                w(dve, g_ds, 3 * g)
                for z in range(3):
                    w(dve, g_ds, 3 * g + z)
                    dve.tensor_tensor(xdd[:].rearrange("p (h q) -> p h q", q=64),
                                      xdt[:, z, 512 * g:512 * g + 512].rearrange("p (h q) -> p h q", q=64),
                                      per_head(2, z, 8 * g, 8), ALU.mult).then_inc(g_xdd, 1)
                    if z == 0:
                        dve.wait_ge(g_cb, g + 1)
                        dve.wait_ge(g_bt, g + 1)
                        b4 = xbc[:, 16 + g, :].rearrange("p (c l) -> p c l", c=NC)
                        dve.tensor_tensor(b4, bank[7][:].rearrange("p (c l) -> p c l", c=NC),
                                          causal[:].unsqueeze(1).broadcast_to((P, NC, P)), ALU.mult).then_inc(g_cbm, 1)
                        dve.tensor_copy(bn[:].rearrange("p c l -> p (c l)"), bank[6][:]).then_inc(g_bn, 1)
                    dve.wait_ge(g_ds, 3 * g + z + 1)
                    w(dve, p_y, 8 * g)
                    if z == 0:
                        dve.tensor_copy(ent[:, 0, :], bank[7][:]).then_inc(g_ent, 1)
                    else:
                        dve.wait_ge(g_ent, 3 * g + z)
                        own.link(dve.tensor_tensor(
                            ent[:, z, :].rearrange("p (h q) -> p h q", q=64),
                            ent[:, z - 1, :].rearrange("p (h q) -> p h q", q=64),
                            etot[:, 8 * g:8 * g + 8, z:z + 1].broadcast_to((P, 8, 64)), ALU.mult))
                        dve.tensor_tensor(ent[:, z, :], ent[:, z, :], bank[7 - z % 2][:], ALU.add).then_inc(g_ent, 1)
                for q in range(4):
                    i = 4 * g + q
                    for e in range(2):
                        h = 2 * i + e
                        dve.wait_ge(p_cs, h + 1)
                        w(dve, p_y, h - 1)
                        dve.tensor_tensor(t1[:, e, :].rearrange("p (c l) -> p c l", c=NC),
                                          bank[4 + e][:].rearrange("p (c l) -> p c l", c=NC),
                                          nat[:, 0, :, h:h + 1].broadcast_to((P, NC, P)), ALU.subtract).then_inc(p_sub, 1)
                        dve.wait_ge(p_sub, h + 1)
                        dve.tensor_scalar(t1[:, e, :], t1[:, e, :], 0.0, None, ALU.min).then_inc(p_min, 1)
                    for e in range(2):
                        h = 2 * i + e
                        dve.wait_ge(p_E, h + 1)
                        dve.wait_ge(g_cbm, g + 1)
                        dve.tensor_tensor(t1[:, e, :], t1[:, e, :], xbc[:, 16 + g, :], ALU.mult).then_inc(p_S, 1)
                        dve.wait_ge(p_ec, h + 1)
                        dve.tensor_tensor(ec[:, e, :], ec[:, e, :], xbc[:, 20 + g, :], ALU.mult).then_inc(p_Cd, 1)
                    if q:
                        evacuate(i - 1)
                        gate(i - 1)
                evacuate(4 * g + 3)
                gate(4 * g + 3)
            for g in range(SSD_G):
                gnorms[g].dve(dve)
            so = stage["ssd_out"]

            def body(i):
                for k in range(2):
                    t = i * 2 + k
                    so.unit_ready(dve, i, 2 * k + 1)
                    dst = mT[:, t, :] if isinstance(t, int) else mT[:, bass.ds(t, 1), :].squeeze(1)
                    dve.tensor_copy(dst, bank[k][:]).then_inc(bank_free, 1)

            repeat(dve, 4, body)
            post0.dve(dve)

        def x_given(act, k):
            if k == 0:
                act.wait_ge(x_in, 32)

        l_in, l_x, l_c, l_t0, l_hi, l_lo = (sem("l_" + s) for s in ("in", "x", "c", "t0", "hi", "lo"))
        l_g, l_lam, l_a, l_th, l_q, l_s, l_h, l_ph, l_pl = (
            sem("l_" + s) for s in ("gates", "lam", "a", "th", "q", "s", "h", "prod_hi", "prod_lo"))
        ffn_pre0 = pre("ffn_pre", 0)
        ffn0 = FFN(0, (16, 16), "gelu", "ffn1_0", ffn_pre0)
        ffn_post0 = post("ffn_post", 0)
        norm1 = pre("mix_pre", 1)
        post1 = post("mix_post", 1)
        ffn_pre1 = pre("ffn_pre", 1)
        ffn1 = FFN(1, (16, 16), "gelu", "ffn1_1", ffn_pre1)
        ffn_post1 = post("ffn_post", 1)

        def out_pe(pe, st, hi, lo, ready):
            def body(i):
                for k in range(2):
                    t = i * 2 + k
                    st.pe_start(pe, t)
                    st.pe_tile(pe, bank[k][:], i, 2 * k, rhs)

            def rhs(kt):
                return hi[:, kt, :], lo[:, kt, :]

            st.pe_first_two(pe, rhs, ready)
            with pe.Fori(1, 4) as i:
                body(i)

        def split_only(act, st, n4):
            def body(i):
                for k in range(4):
                    st.unit_ready(act, i, k)
                    st.split_ahead(i, k)
            repeat(act, n4, body)

        def lru_pe(pe):
            st = stage["lru_in"]

            def body(i):
                for k in range(4):
                    t = i * 4 + k
                    if isinstance(t, int) and t < 2:
                        if t == 0:
                            st.pe_first_two(pe, rhs_h, lambda kt: norm1.lo_ready(pe, kt))
                        continue
                    st.pe_start(pe, t)
                    st.pe_tile(pe, bank[k][:], i, k, rhs_h)

            repeat(pe, 5, body)
            st = stage["lru_gate"]
            for t in range(2 * NL):
                h, u = t // 2, t // 4
                st.pe_start(pe, t)
                s, b = (st.u0 + u) % RING, t % 4
                if b == 0:
                    pe.wait_ge(split_done, st.u0 + u + 1)
                pe.wait_ge(l_lo, h + 1)
                wh, wl = whi[:, s, b * P:b * P + P], wlo[:, s, b * P:b * P + P]
                pe.matmul(bank[t % 4][:], wh, xb_hi[:, h, :], start=True, stop=False)
                pe.matmul(bank[t % 4][:], wh, xb_lo[:, h, :], start=False, stop=False)
                last = pe.matmul(bank[t % 4][:], wl, xb_hi[:, h, :], start=False, stop=True)
                if b == 3:
                    last.then_inc(unit_done, 1)
                else:
                    last.then_inc(l_g, 1)
            out_pe(pe, stage["lru_out"], lo_hi, lo_lo, lambda kt: pe.wait_ge(l_pl, kt + 1))
            post1.pe(pe)

        def gate_ready(eng, t):
            st = stage["lru_gate"]
            if t % 4 == 3:
                eng.wait_ge(unit_done, st.u0 + t // 4 + 1)
            else:
                eng.wait_ge(l_g, t - t // 4 + 1)

        def lru_act(act, own):
            lam = col("lru_lam", 0, NL)
            own.link(act.activation(lam8[:, 0, :], lam, ACT.Abs))
            act.activation(lam8[:, 1, :], lam8[:, 0, :], ACT.Exp, scale=-1.0).then_inc(l_lam, 1)
            act.wait_ge(l_lam, 2)
            act.activation(lam8[:, 3, :], lam8[:, 2, :], ACT.Ln).then_inc(l_lam, 1)
            st = stage["lru_in"]

            def xpart(t, e, k):
                act.activation(ltap[:, e, :], bank[k][:], ACT.Identity, bias=col("lru_bx", t - NL)).then_inc(bank_free, 1)

            for t in range(20):
                i, k = t // 4, t % 4
                st.unit_ready(act, i, k)
                if t < NL:
                    act.activation(ybr[:, t, :], bank[k][:], ACT.Gelu_apprx_tanh, bias=col("lru_by", t)).then_inc(bank_free, 1)
                else:
                    j = t - NL
                    w(act, l_x, j - 1)
                    xpart(t, j % 2, k)
                    if j >= 1:
                        act.wait_ge(l_x, j)
                        act.activation(xb_hi[:, j - 1, :], xbr[:, j - 1, :], ACT.Copy).then_inc(l_hi, 1)
                st.split_ahead(i, k)
            act.wait_ge(l_x, NL)
            act.activation(xb_hi[:, NL - 1, :], xbr[:, NL - 1, :], ACT.Copy).then_inc(l_hi, 1)
            st = stage["lru_gate"]
            for t in range(2 * NL):
                h = t // 2
                gate_ready(act, t)
                dst, bias = (gx, "lru_bgx") if t % 2 == 0 else (ga, "lru_bga")
                act.activation(dst[:, h, :], bank[t % 4][:], ACT.Sigmoid, bias=col(bias, h)).then_inc(bank_free, 1)
                if t % 4 == 3:
                    split_hi(0, st.u0 + t // 4 + RING)
            act.wait_ge(l_lam, 4)
            for k in range(NL):
                own.link(act.activation(lth[:, k, :], ga[:, k, :], ACT.Tanh, scale=lam8[:, 1, k:k + 1]))
                own.link(act.activation(ga[:, k, :], ga[:, k, :], ACT.Exp, scale=lam8[:, 0, k:k + 1]))
                act.activation(lh[:, k, :], ga[:, k, :], ACT.Square).then_inc(l_a, 1)
            for k in range(NL):
                act.wait_ge(l_q, k + 1)
                act.activation(lth[:, k, :], lth[:, k, :], ACT.Sqrt).then_inc(l_s, 1)
                if k >= 1:
                    act.wait_ge(l_h, k)
                    act.activation(lo_hi[:, k - 1, :], lh[:, k - 1, :], ACT.Copy).then_inc(l_ph, 1)
            act.wait_ge(l_h, NL)
            act.activation(lo_hi[:, NL - 1, :], lh[:, NL - 1, :], ACT.Copy).then_inc(l_ph, 1)
            so = stage["lru_out"]
            split_only(act, so, 4)
            post1.act(act, lambda a, k: so.freed(a, k))

        def lru_dve(dve, own):
            lam = col("lru_lam", 0, NL)
            v0, u, v, ln = (lam8[:, n, :] for n in range(4))
            dve.wait_ge(l_lam, 1)
            dve.tensor_scalar(v, u, 1.0, None, ALU.add).then_inc(l_lam, 1)
            dve.wait_ge(l_lam, 3)
            own.link(dve.tensor_scalar(v, v, -1.0, 1e-30, ALU.add, ALU.max))
            own.link(dve.reciprocal(v, v))
            own.link(dve.tensor_tensor(ln, ln, u, ALU.mult))
            own.link(dve.tensor_tensor(ln, ln, v, ALU.mult))
            own.link(dve.tensor_scalar(v, u, -0.5, 1.0, ALU.mult, ALU.add))
            own.link(dve.tensor_tensor(v, v, u, ALU.mult))
            own.link(dve.tensor_tensor(ln, ln, v, ALU.max))
            own.link(dve.scalar_tensor_tensor(out=v, in0=lam, scalar=0.0, in1=ln, op0=ALU.min, op1=ALU.subtract))
            own.link(dve.tensor_scalar(v0, v, 8.0, None, ALU.mult))
            dve.tensor_scalar(u, v, -8.0, None, ALU.mult).then_inc(l_lam, 1)
            st = stage["lru_in"]
            for j in range(NL):
                e = j % 2
                st.freed(dve, NL + j)
                src, cv = ltap[:, e, :], xbr[:, j, :]
                own.link(dve.tensor_scalar(cv, src, col("lru_conv", 5 * j + 3), col("lru_conv", 5 * j + 4), ALU.mult,
                                           ALU.add))
                for n in (1, 2, 3):
                    ins = dve.scalar_tensor_tensor(out=xbr[:, j, n:T], in0=ltap[:, e, 0:T - n],
                                                   scalar=col("lru_conv", 5 * j + 3 - n), in1=xbr[:, j, n:T],
                                                   op0=ALU.mult, op1=ALU.add)
                    if n < 3:
                        own.link(ins)
                    else:
                        ins.then_inc(l_x, 1)
                if j >= 1:
                    dve.wait_ge(l_hi, j)
                    dve.tensor_tensor(xb_lo[:, j - 1, :], xbr[:, j - 1, :], xb_hi[:, j - 1, :].bitcast(F32),
                                      ALU.subtract).then_inc(l_lo, 1)
            dve.wait_ge(l_hi, NL)
            dve.wait_ge(l_x, NL)
            dve.tensor_tensor(xb_lo[:, NL - 1, :], xbr[:, NL - 1, :], xb_hi[:, NL - 1, :].bitcast(F32),
                              ALU.subtract).then_inc(l_lo, 1)
            for k in range(NL):
                gate = stage["lru_gate"]
                gate.freed(dve, 2 * k)
                dve.tensor_tensor(gx[:, k, :], gx[:, k, :], xbr[:, k, :], ALU.mult).then_inc(l_c, 1)
            for k in range(NL):
                dve.wait_ge(l_a, k + 1)
                dve.scalar_tensor_tensor(out=lth[:, k, :], in0=lh[:, k, :], scalar=1.0, in1=lth[:, k, :], op0=ALU.add,
                                         op1=ALU.mult).then_inc(l_q, 1)
            for k in range(NL):
                dve.wait_ge(l_s, k + 1)
                w(dve, l_c, k + 1)
                own.link(dve.tensor_tensor(gx[:, k, :], gx[:, k, :], lth[:, k, :], ALU.mult))
                own.link(dve.tensor_tensor_scan(out=lh[:, k, :], data0=ga[:, k, :], data1=gx[:, k, :], initial=0.0,
                                                op0=ALU.mult, op1=ALU.add))
                dve.tensor_tensor(lh[:, k, :], lh[:, k, :], ybr[:, k, :], ALU.mult).then_inc(l_h, 1)
                if k >= 1:
                    dve.wait_ge(l_ph, k)
                    dve.tensor_tensor(lo_lo[:, k - 1, :], lh[:, k - 1, :], lo_hi[:, k - 1, :].bitcast(F32),
                                      ALU.subtract).then_inc(l_pl, 1)
            dve.wait_ge(l_ph, NL)
            dve.tensor_tensor(lo_lo[:, NL - 1, :], lh[:, NL - 1, :], lo_hi[:, NL - 1, :].bitcast(F32),
                              ALU.subtract).then_inc(l_pl, 1)
            so = stage["lru_out"]

            def body(i):
                for k in range(2):
                    t = i * 2 + k
                    so.unit_ready(dve, i, 2 * k + 1)
                    dst = mT[:, t, :] if isinstance(t, int) else mT[:, bass.ds(t, 1), :].squeeze(1)
                    dve.tensor_scalar(dst, bank[k][:], col("lru_bout", t), None, ALU.add).then_inc(bank_free, 1)

            repeat(dve, 4, body)
            post1.dve(dve)

        e_lb, e_f, e_ln, e_b, e_eb, e_q, e_enb, e_kd, e_d, e_k2e, e_k2 = (
            sem("e_" + s) for s in ("lb", "f", "ln", "b", "eb", "q", "enb", "kd", "d", "k2e", "k2"))
        e_tr, e_vn, e_at, e_am, e_ds, e_st, e_o, e_og = (sem("e_" + s) for s in ("tr", "vn", "at", "am", "ds", "st", "o", "og"))
        v_in, v_prm, v_exp, v_bb, v_ca, v_tr, v_wb, v_k0p, v_k0 = (
            sem("v_" + s) for s in ("in", "prm", "exp", "bb", "ca", "tr", "wb", "k0p", "k0"))
        v_bu, v_mm, v_v, v_ct, v_v0, v_w, v_om, v_s, v_y = (
            sem("v_" + s) for s in ("bu", "mm", "v", "ct", "v0", "w", "om", "s", "y"))
        pool_own = sem("pool_own")
        u_y, u_z, u_hi, u_lo, u_sg, u_o, u_ohi, u_olo = (sem("u_" + s) for s in ("y", "z", "hi", "lo", "sg", "o", "ohi", "olo"))
        norm2 = pre("mix_g2", 0)
        hnorm = [Norm(1, (lambda k, h=h: otmp[:, h % 2, :]), (lambda k, h=h: col("hgrn_g", h)), P, "split",
                      (lambda k, h=h: h_hi[:, h, :]), (lambda k, h=h: h_lo[:, h, :]),
                      squared=(lambda k, h=h: bank[2 + h % 2][:])) for h in range(HG)]
        ffn_pre2 = pre("ffn_g2", 0)
        ffn2 = FFN(2, (12, 10), "silu", "ffn2_0", ffn_pre2)
        norm3 = pre("mix_g2", 1)

        def even_pe(pe):
            st = stage["ev_in"]

            def body(i):
                for k in range(4):
                    t = i * 4 + k
                    if isinstance(t, int) and t < 2:
                        if t == 0:
                            st.pe_first_two(pe, rhs_h, lambda kt: norm2.lo_ready(pe, kt))
                        continue
                    st.pe_start(pe, t)
                    st.pe_tile(pe, bank[k][:], i, k, rhs_h)

            repeat(pe, 5, body)

            def head_in(h):
                w(pe, e_k2, h + 1)
                w(pe, e_vn, h)
                for c in range(NC):
                    pe.transpose(chunk(bank[4], c), chunk(ev[:, 8 + h, :], c), ident[:])
                for c in range(NC):
                    last = pe.transpose(chunk(bank[5], c), chunk(k2[:, h, :], c), ident[:])
                last.then_inc(e_tr, 1)
                w(pe, e_am, h)
                w(pe, e_kd, h + 1)
                w(pe, e_q, h + 1)
                for c in range(NC):
                    last = pe.matmul(chunk(bank[6], c), chunk(kd[:, h, :], c), chunk(ev[:, 12 + h, :], c), start=True,
                                     stop=True)
                last.then_inc(e_at, 1)
                if h == 0:
                    w(pe, bank_free, st.t0 + 20)
                w(pe, e_vn, h + 1)
                w(pe, e_st, 7 * h)
                for n in range(8):
                    r = slice(64 * (n % 2), 64 * (n % 2) + 64)
                    last = pe.matmul(chunk(bank[n % 2], n // 2), kN[r, h % 2, n // 2 * P:n // 2 * P + P],
                                     vN[r, h % 2, n // 2 * P:n // 2 * P + P], start=True, stop=True)
                last.then_inc(e_ds, 1)

            head_in(0)
            head_in(1)
            for h in range(HG):
                w(pe, e_am, h + 1)
                w(pe, e_st, 7 * h + 7)
                w(pe, e_og, h - 1)
                w(pe, n_mm, hnorm[0].sq0 + h - 1)
                o = bank[2 + h % 2]
                for c in range(NC):
                    pe.matmul(chunk(o, c), chunk(vN[:, h % 2, :], c), chunk(attT[:, h % 2, :], c), start=True, stop=False)
                    for n in (2 * c, 2 * c + 1):
                        if n:
                            last = pe.matmul(o[:, 64 * n:64 * n + 64], stS[:, h % 2, n - 1, :],
                                             ev[:, 12 + h, 64 * n:64 * n + 64], start=False, stop=n % 2 == 1)
                last.then_inc(e_o, 1)
                hnorm[h].pe(pe)
                if h + 2 < HG:
                    head_in(h + 2)
            w(pe, v_bb, 2)
            w(pe, n_rms, hnorm[-1].r0 + 1)
            for n, mat in enumerate((bbar, bbara)):
                for c in range(2):
                    for j in range(4):
                        last = pe.transpose(chunk(bank[4 + 2 * n + c], j),
                                            mat[:, c, 4 * j:4 * j + 4, :].rearrange("p a b -> p (a b)"), ident[:])
            last.then_inc(v_tr, 1)
            for i in range(S5T):
                r, j = i % 4, i // 4
                o = bank[0][32 * r:32 * r + 32, P * j + 32 * r:P * j + 32 * r + 32]
                pe.matmul(o, bbar[:, 0, i, :], cc[:, 0, i, :], start=True, stop=False)
                last = pe.matmul(o, bbar[:, 1, i, :], cc[:, 1, i, :], start=False, stop=True)
            last.then_inc(v_k0p, 1)

            def s5_in(m, r):
                rows = slice(32 * r, 32 * r + 32)
                for j in range(4):
                    for c in range(2):
                        o = bank[4 + r][:, (4 * c + j) * S5L:(4 * c + j + 1) * S5L]
                        for n in (1, 0):
                            last = pe.matmul(o, wb[rows, n, c, j, :], steps(ev[rows, j, :], m, 1 - n), start=n == 1,
                                             stop=n == 0)
                last.then_inc(v_bu, 1)

            def s5_out(m, r, n_even):
                t0 = (m - 1) * S5L
                for j in range(4):
                    odd = bank[j][32 * r:32 * r + 32, 256 + t0:256 + t0 + 2 * S5L]
                    even = bank[j][32 * r:32 * r + 32, t0 + 1:t0 + 1 + n_even]
                    for c in range(2):
                        states = ss[:, r, c, j].rearrange("p h l -> p (h l)")
                        pe.matmul(odd, cc[:, c, 4 * j + r, :], states, start=False, stop=False)
                        last = pe.matmul(even, cca[:, c, 4 * j + r, :], states[:, 0:n_even], start=False,
                                         stop=n_even < 2 * S5L and c == 1)
                last.then_inc(v_y, 1)

            w(pe, v_wb, 4)
            for r in range(4):
                s5_in(0, r)
            w(pe, v_k0, 4)
            w(pe, v_ca, 1)
            for j in range(4):
                pe.matmul(bank[j][:, 0:256], k0[:, j, :], ev[:, j, 0:T:2], start=True, stop=False)

            for m in range(S5M):
                for r in range(4):
                    if m + 1 < S5M:
                        w(pe, v_mm, (4 * m + r) * 2 + 2)
                        s5_in(m + 1, r)
                    if m % 2:
                        w(pe, v_s, (4 * m + r) * 2 + 2)
                        s5_out(m, r, 2 * S5L - (m == S5M - 1))
            st = stage["glu"]
            for t in range(4):
                s, b0 = (st.u0 + t // 2) % RING, 4 * (t % 2)
                if b0 == 0:
                    w(pe, split_done, st.u0 + t // 2 + 1)
                for kt in range(4):
                    if t == 0:
                        w(pe, u_lo, kt + 1)
                    wh, wl = (m[:, s, (b0 + kt) * P:(b0 + kt + 1) * P] for m in (whi, wlo))
                    pe.matmul(bank[t][:], wh, z_hi[:, kt, :], start=kt == 0, stop=False)
                    pe.matmul(bank[t][:], wh, z_lo[:, kt, :], start=False, stop=False)
                    last = pe.matmul(bank[t][:], wl, z_hi[:, kt, :], start=False, stop=kt == 3)
                last.then_inc(unit_done if t % 2 else g_lu, 1)
            st = stage["ev_out"]
            for t in range(8):
                st.pe_start(pe, t)
                ready = (lambda kt: w(pe, n_lo, hnorm[kt].h0 + 1) if kt < 4 else w(pe, u_olo, kt - 3)) if t == 0 else None
                st.pe_tile(pe, bank[t % 4][:], t // 4, t % 4, rhs_h, ready)

        g_lu = sem("glu_half")

        def steps(tokens, m, odd):
            return tokens.rearrange("p (t two) -> p t two", two=2)[:, m * S5L:(m + 1) * S5L, odd]

        def even_act(act, own):
            st = stage["ev_in"]
            act.wait_ge(e_lb, 1)
            act.activation(lbv[:, 0:2, :], lbv[:, 0:2, :], ACT.Exp).then_inc(e_lb, 1)
            act.activation(s5c[:, 0, :], col("s5_logdt", 0, S5T), ACT.Exp).then_inc(v_exp, 1)
            for t in range(20):
                i, k = t // 4, t % 4
                st.unit_ready(act, i, k)
                f = (ACT.Copy, ACT.Sigmoid, ACT.Copy, ACT.Copy, ACT.Silu)[t // 4]
                act.activation(ev[:, t, :], bank[k][:], f).then_inc(bank_free, 1)
                st.split_ahead(i, k)
                if t == 11:
                    for h in range(HG):
                        act.wait_ge(e_f, h + 1)
                        act.activation(bcum[:, h, :], bcum[:, h, :], ACT.Ln).then_inc(e_ln, 1)
                if t == 15:
                    for h in range(HG):
                        act.wait_ge(e_b, h + 1)
                        act.activation(kd[:, h, :], bcum[:, h, :], ACT.Exp).then_inc(e_eb, 1)
                        own(act.activation(dec[:, h, :], bcum[:, h, 63:T:64], ACT.Exp))
                        act.wait_ge(e_d, h + 1)
                        act.activation(k2[:, h, :], k2[:, h, :], ACT.Exp).then_inc(e_k2e, 1)
                        act.wait_ge(e_q, h + 1)
                        act.activation(kd[:, h, :], bcum[:, h, :], ACT.Exp, scale=-1.0).then_inc(e_enb, 1)
                if t == 3:
                    act.wait_ge(v_prm, 1)
                    act.activation(s5c[:, 4, :], s5c[:, 2, :], ACT.Exp).then_inc(v_exp, 1)
                    act.activation(s5c[:, 5:7, :], s5c[:, 5:7, :], ACT.Sin).then_inc(v_exp, 1)
            act.wait_ge(e_enb, HG)
            act.dma_start(braw[:], dram["s5_b"]).then_inc(v_in, 16)
            act.dma_start(cc[:], dram["s5_c"]).then_inc(v_in, 16)
            for h in range(HG):
                hnorm[h].act(act, lambda a, k, h=h: a.wait_ge(e_o, h + 1))
            act.wait_ge(v_tr, 1)
            for c in range(2):
                act.activation(wb[:, 0, c].rearrange("p a b -> p (a b)"), bank[4 + c][:], ACT.Copy).then_inc(v_wb, 1)
            for j in range(4):
                act.wait_ge(u_y, 2 * j + 2)
                own.link(act.activation(zf[:, j, :], zf[:, j, :], ACT.Gelu_apprx_tanh))
                act.activation(z_hi[:, j, :], zf[:, j, :], ACT.Copy).then_inc(u_hi, 1)
            st = stage["glu"]

            def out_high(t):
                act.wait_ge(u_o, t + 1)
                act.activation(h_hi[:, 4 + t, :], zf[:, t, :], ACT.Copy).then_inc(u_ohi, 1)

            for t in range(4):
                if t % 2:
                    act.wait_ge(unit_done, st.u0 + t // 2 + 1)
                else:
                    act.wait_ge(g_lu, t // 2 + 1)
                w(act, u_o, t - 1)
                act.activation(otmp[:, t % 2, :], bank[t][:], ACT.Sigmoid, bias=col("b_glu", t)).then_inc(bank_free, 1)
                if t % 2:
                    split_hi(0, st.u0 + t // 2 + RING)
                if t:
                    out_high(t - 1)
            out_high(3)
            split_only(act, stage["ev_out"], 2)

        def even_dve(dve, own):
            st = stage["ev_in"]
            l0, l1 = col("lb", 0, 4), col("lb", 4, 4)
            own.sync()
            own.link(dve.tensor_tensor(lbv[:, 2, :], l0, l1, ALU.max))
            own(dve.tensor_tensor(lbv[:, 0, :], l0, lbv[:, 2, :], ALU.subtract))
            dve.tensor_tensor(lbv[:, 1, :], l1, lbv[:, 2, :], ALU.subtract).then_inc(e_lb, 1)
            own(dve.memset(seg64[:], 1.0))
            own(dve.memset(attT[:], 0.0))
            dve.wait_ge(e_lb, 2)
            own.link(dve.tensor_tensor(lbv[:, 1, :], lbv[:, 0, :], lbv[:, 1, :], ALU.add))
            own.link(dve.reciprocal(lbv[:, 1, :], lbv[:, 1, :]))
            own.link(dve.tensor_tensor(lbv[:, 0, :], lbv[:, 0, :], lbv[:, 1, :], ALU.mult))
            own.link(dve.tensor_scalar(lbv[:, 3, :], lbv[:, 0, :], -1.0, 1.0, ALU.mult, ALU.add))
            own.link(dve.memset(seg64[:, 0:T:64], 0.0))
            s5_angles(dve, own)
            for h in range(HG):
                st.freed(dve, 4 + h)
                own.link(dve.tensor_scalar(bcum[:, h, :], ev[:, 4 + h, :], lbv[:, 3, h:h + 1], lbv[:, 0, h:h + 1],
                                           ALU.mult, ALU.add))
                dve.tensor_scalar(ev[:, 4 + h, :], bcum[:, h, :], -1.0, 1.0, ALU.mult, ALU.add).then_inc(e_f, 1)
            s5_coefficients(dve, own)
            for h in range(HG):
                dve.wait_ge(e_ln, h + 1)
                own.sync()
                dve.tensor_tensor_scan(out=bcum[:, h, :], data0=seg64[:], data1=bcum[:, h, :], initial=0.0, op0=ALU.mult,
                                       op1=ALU.add).then_inc(e_b, 1)
                dve.wait_ge(e_b, h + 1)
                b3 = bcum[:, h, :].rearrange("p (c l) -> p c l", l=64)
                dve.tensor_tensor(k2[:, h, :].rearrange("p (c l) -> p c l", l=64), b3[:, :, 63:64].broadcast_to((P, 8, 64)),
                                  b3, ALU.subtract).then_inc(e_d, 1)
            for h in range(HG):
                dve.wait_ge(e_eb, h + 1)
                st.freed(dve, 12 + h)
                dve.tensor_tensor(ev[:, 12 + h, :], ev[:, 12 + h, :], kd[:, h, :], ALU.mult).then_inc(e_q, 1)
                dve.wait_ge(e_enb, h + 1)
                dve.tensor_tensor(kd[:, h, :], kd[:, h, :], ev[:, 4 + h, :], ALU.mult).then_inc(e_kd, 1)
                dve.wait_ge(e_k2e, h + 1)
                dve.tensor_tensor(k2[:, h, :], k2[:, h, :], ev[:, 4 + h, :], ALU.mult).then_inc(e_k2, 1)
            dve.wait_ge(e_k2, HG)
            for c in range(2):
                own(dve.tensor_copy(magt[:, :, c], s5c[:, 7, :].rearrange("p (j r) -> p r j", r=4).unsqueeze(3)
                                    .broadcast_to((P, 4, 4, S5L))))
            own.sync()
            own.link(dve.memset(magt[:, :, :, :, 0:1], 0.0))

            def head_states(h):
                dve.wait_ge(e_tr, h + 1)
                w(dve, e_o, h - 1)
                own(dve.tensor_copy(vN[:, h % 2, :], bank[4][:]))
                dve.tensor_copy(kN[:, h % 2, :], bank[5][:]).then_inc(e_vn, 1)
                dve.wait_ge(e_at, h + 1)
                dve.copy_predicated(attT[:, h % 2, :].rearrange("p (c l) -> p c l", c=NC),
                                    pair_mask[:].unsqueeze(1).broadcast_to((P, NC, P)),
                                    bank[6][:].rearrange("p (c l) -> p c l", c=NC)).then_inc(e_am, 1)
                dve.wait_ge(e_ds, h + 1)
                for n in range(7):
                    src = chunk(bank[n % 2], n // 2)
                    if n == 0:
                        dve.tensor_copy(stS[:, h % 2, 0, :], src).then_inc(e_st, 1)
                    else:
                        dve.wait_ge(e_st, 7 * h + n)
                        dve.scalar_tensor_tensor(out=stS[:, h % 2, n, :], in0=stS[:, h % 2, n - 1, :],
                                                 scalar=dec[:, h, n:n + 1], in1=src, op0=ALU.mult,
                                                 op1=ALU.add).then_inc(e_st, 1)

            head_states(0)
            for h in range(HG):
                if h + 1 < HG:
                    head_states(h + 1)
                dve.wait_ge(n_sq, hnorm[h].sq0 + 1)
                st.freed(dve, 16 + h)
                dve.tensor_tensor(otmp[:, h % 2, :], ev[:, 16 + h, :], bank[2 + h % 2][:], ALU.mult).then_inc(e_og, 1)
                dve.wait_ge(e_og, h + 1)
                hnorm[h].dve(dve)
            own.link(dve.memset(k0[:], 0.0))
            dve.wait_ge(v_tr, 1)
            for c in range(2):
                dve.tensor_copy(wb[:, 1, c].rearrange("p a b -> p (a b)"), bank[6 + c][:]).then_inc(v_wb, 1)
            dve.wait_ge(v_k0p, 1)
            for r in range(4):
                rows, c4 = slice(32 * r, 32 * r + 32), slice(32 * r, 32 * r + 32)
                dve.tensor_copy(k0[rows, :, c4], bank[0][rows, :].rearrange("p (j n) -> p j n", j=4)[:, :, c4])\
                    .then_inc(v_k0, 1)

            def wide(t):
                return t.unsqueeze(1).broadcast_to((P, 2, 4, S5L))

            def flat(t):
                return t.rearrange("p c j l -> p (c j l)")

            def turn_out(u, r):
                b = r % 2
                w(dve, v_w, u + 1)
                w(dve, v_s, u * 2 - 2)
                for n in range(2):
                    dve.tensor_tensor(om[:, b, n], wide(tab[:, n, r:S5T:4, :]), sw[:, b], ALU.mult).then_inc(v_om, 1)

            def states(u, m, r):
                b = r % 2
                w(dve, v_om, u * 2 + 2)
                if m >= 2:
                    w(dve, v_y, (m // 2 - 1) * 4 + r + 1)
                dve.tensor_tensor(ss[:, r, 0, :, m % 2], om[:, b, 0, 0], om[:, b, 1, 1], ALU.subtract).then_inc(v_s, 1)
                dve.tensor_tensor(ss[:, r, 1, :, m % 2], om[:, b, 0, 1], om[:, b, 1, 0], ALU.add).then_inc(v_s, 1)

            def s5_body(m):
                first = m == 0
                for r in range(4):
                    u, b = m * 4 + r, r % 2
                    src = bank[4 + r][:].rearrange("p (c j l) -> p c j l", c=2, j=4)
                    w(dve, v_bu, u + 1)
                    w(dve, v_v, u * 2 - 2)
                    for n in range(2):
                        dve.tensor_tensor(mm[:, b, n], wide(tab[:, n, r:S5T:4, :]), src, ALU.mult).then_inc(v_mm, 1)
                    if not (first and r == 0):
                        turn_out(u - 1, (r - 1) % 4)
                    w(dve, v_mm, u * 2 + 2)
                    w(dve, v_w, u - 1)
                    dve.tensor_tensor(sv[:, b, 0], mm[:, b, 0, 0], mm[:, b, 1, 1], ALU.add).then_inc(v_v, 1)
                    dve.tensor_tensor(sv[:, b, 1], mm[:, b, 0, 1], mm[:, b, 1, 0], ALU.subtract).then_inc(v_v, 1)
                    if not first:
                        w(dve, v_s, u * 2 - 6)
                        dve.tensor_tensor(s5k[:, b], ss[:, r, :, :, (m - 1) % 2, S5L - 1],
                                          s5c[:, 7, r:S5T:4].unsqueeze(1).broadcast_to((P, 2, 4)),
                                          ALU.mult).then_inc(v_ct, 1)
                    if not (first and r == 0):
                        if not first:
                            w(dve, v_ct, u - 4)
                        states(u - 1, (u - 1) // 4, (r - 1) % 4)
                    w(dve, v_v, u * 2 + 2)
                    if not first:
                        w(dve, v_ct, u - 3)
                        dve.tensor_tensor(sv[:, b, :, :, 0], sv[:, b, :, :, 0], s5k[:, b], ALU.add).then_inc(v_v0, 1)
                        w(dve, v_v0, u - 3)
                    w(dve, v_om, u * 2 - 2)
                    dve.tensor_tensor_scan(out=flat(sw[:, b]), data0=flat(magt[:, r]), data1=flat(sv[:, b]),
                                           initial=0.0, op0=ALU.mult, op1=ALU.add).then_inc(v_w, 1)

            dve.wait_ge(v_ca, 1)
            for m in range(S5M):
                s5_body(m)
            turn_out(4 * S5M - 1, 3)
            states(4 * S5M - 1, S5M - 1, 3)
            dve.wait_ge(v_y, 2 * S5M)
            for j in range(4):
                for odd in range(2):
                    dve.scalar_tensor_tensor(out=steps_of(zf[:, j, :], odd), in0=steps_of(ev[:, j, :], odd),
                                             scalar=col("s5_d", j), in1=bank[j][:, 256 * odd:256 * odd + 256],
                                             op0=ALU.mult, op1=ALU.add).then_inc(u_y, 1)
            for j in range(4):
                dve.wait_ge(u_hi, j + 1)
                dve.tensor_tensor(z_lo[:, j, :], zf[:, j, :], z_hi[:, j, :].bitcast(F32), ALU.subtract).then_inc(u_lo, 1)
            st = stage["glu"]

            def out_low(t):
                dve.wait_ge(u_ohi, t + 1)
                dve.tensor_tensor(h_lo[:, 4 + t, :], zf[:, t, :], h_hi[:, 4 + t, :].bitcast(F32),
                                  ALU.subtract).then_inc(u_olo, 1)

            dve.wait_ge(u_lo, 4)
            for t in range(4):
                st.freed(dve, t)
                dve.tensor_tensor(zf[:, t, :], zf[:, t, :], otmp[:, t % 2, :], ALU.mult).then_inc(u_o, 1)
                if t:
                    out_low(t - 1)
            out_low(3)
            onto_residual(dve, stage["ev_out"])

        def onto_residual(dve, st):
            for t in range(8):
                st.unit_ready(dve, t // 4, t % 4)
                dve.tensor_tensor(xT[:, t, :], xT[:, t, :], bank[t % 4][:], ALU.add).then_inc(bank_free, 1)

        def reduced(dve, own, dst, k, src, quarter):
            own.link(dve.tensor_scalar(k, src, 1.0 / (2 * math.pi), 0.25 if quarter else 0.0, ALU.mult, ALU.add))
            own.link(dve.tensor_scalar(k, k, MAGIC, MAGIC, ALU.add, ALU.subtract))
            for n, c in enumerate(TWO_PI):
                own.link(dve.scalar_tensor_tensor(out=dst, in0=k, scalar=-c, in1=dst if n else src, op0=ALU.mult,
                                                  op1=ALU.add))
            if quarter:
                own.link(dve.tensor_scalar(dst, dst, math.pi / 2, None, ALU.add))
            own.link(dve.tensor_scalar(dst, dst, 3.1415925, -3.1415925, ALU.min, ALU.max))

        def steps_of(tokens, odd):
            return tokens.rearrange("p (t two) -> p t two", two=2)[:, :, odd]

        def s5_row(n):
            return s5c[:, n, :]

        def s5_angles(dve, own):
            q = s5_row
            own.link(dve.tensor_scalar(q(1), col("s5_aim", 0, S5T), -1.0, None, ALU.mult))
            dve.wait_ge(v_exp, 1)
            own.link(dve.tensor_tensor(q(2), col("s5_are", 0, S5T), q(0), ALU.mult))
            own.link(dve.tensor_tensor(q(3), q(1), q(0), ALU.mult))
            reduced(dve, own, q(5), q(7), q(3), False)
            reduced(dve, own, q(6), q(7), q(3), True)
            dve.engine_nop().then_inc(v_prm, 1)

        def s5_coefficients(dve, own):
            q = s5_row
            are, aim = col("s5_are", 0, S5T), q(1)

            def tt(o, a, b, op):
                own.link(dve.tensor_tensor(o, a, b, op))

            dve.wait_ge(v_exp, 3)
            tt(q(7), q(4), q(4), ALU.mult)
            tt(q(8), q(4), q(6), ALU.mult)
            tt(q(9), q(4), q(5), ALU.mult)
            own.link(dve.tensor_scalar(q(12), q(8), -1.0, None, ALU.add))
            tt(q(13), are, are, ALU.mult)
            tt(q(14), aim, aim, ALU.mult)
            tt(q(13), q(13), q(14), ALU.add)
            own.link(dve.reciprocal(q(13), q(13)))
            tt(q(14), q(12), are, ALU.mult)
            tt(q(15), q(9), aim, ALU.mult)
            tt(q(14), q(14), q(15), ALU.add)
            tt(q(10), q(14), q(13), ALU.mult)
            tt(q(14), q(9), are, ALU.mult)
            tt(q(15), q(12), aim, ALU.mult)
            tt(q(14), q(14), q(15), ALU.subtract)
            tt(q(11), q(14), q(13), ALU.mult)
            dve.engine_nop().then_inc(v_prm, 1)

        def s5_pool(pool):
            own = Chain(pool, pool_own)
            q = s5_row

            def products(*ops):
                for o, a, b in ops:
                    own(pool.tensor_tensor(o, a, b, ALU.mult))
                own.sync()

            def sums(*ops):
                for o, a, b, op in ops:
                    own(pool.tensor_tensor(o, a, b, op))
                own.sync()

            st = stage["ev_in"]
            pool.wait_ge(unit_done, st.u0 + 20)
            pool.wait_ge(v_prm, 2)
            cos, sin = tab[:, 0], tab[:, 1]
            first = [t[:, :, 0] for t in (cos, sin)]
            t0, t1_ = ptmp[:, 0], ptmp[:, 1]
            products((t0[:, :, 0], q(5), q(5)), (first[0], q(6), q(6)), (first[1], q(5), q(6)))
            sums((first[0], first[0], t0[:, :, 0], ALU.subtract), (first[1], first[1], first[1], ALU.add))
            d = 1
            while d < S5L:
                now, nxt, td = slice(0, d), slice(d, 2 * d), slice(0, d)
                cd, sd = (t[:, :, d - 1:d].broadcast_to((P, S5T, d)) for t in (cos, sin))
                products((t0[:, :, td], sin[:, :, now], sd), (t1_[:, :, td], cos[:, :, now], sd),
                         (cos[:, :, nxt], cos[:, :, now], cd), (sin[:, :, nxt], sin[:, :, now], cd))
                sums((cos[:, :, nxt], cos[:, :, nxt], t0[:, :, td], ALU.subtract),
                     (sin[:, :, nxt], sin[:, :, nxt], t1_[:, :, td], ALU.add))
                d *= 2

            def wide(n):
                return q(n).unsqueeze(2).broadcast_to((P, S5T, 32))

            pool.wait_ge(v_in, 32)
            products((bbar[:, 0], braw[:, 0], wide(10)), (t0, braw[:, 1], wide(11)), (bbar[:, 1], braw[:, 0], wide(11)),
                     (t1_, braw[:, 1], wide(10)))
            sums((bbar[:, 0], bbar[:, 0], t0, ALU.add), (bbar[:, 1], bbar[:, 1], t1_, ALU.subtract))
            pool.wait_ge(e_at, 2)
            products((bbara[:, 0], bbar[:, 0], wide(8)), (t0, bbar[:, 1], wide(9)), (bbara[:, 1], bbar[:, 1], wide(8)),
                     (t1_, bbar[:, 0], wide(9)))
            pool.tensor_tensor(bbara[:, 0], bbara[:, 0], t0, ALU.subtract).then_inc(v_bb, 1)
            pool.tensor_tensor(bbara[:, 1], bbara[:, 1], t1_, ALU.add).then_inc(v_bb, 1)
            pool.wait_ge(v_bb, 2)
            t0, t1_ = ptmp2[:, 0], ptmp2[:, 1]
            products((cca[:, 0], cc[:, 0], wide(8)), (t0, cc[:, 1], wide(9)), (cca[:, 1], cc[:, 1], wide(8)),
                     (t1_, cc[:, 0], wide(9)))
            sums((cca[:, 0], cca[:, 0], t0, ALU.add), (cca[:, 1], cca[:, 1], t1_, ALU.subtract))
            own.sync()
            pool.engine_nop().then_inc(v_ca, 1)

        a_pos, a_ang, a_trig, a_rot, a_kz = (sem("a_" + s) for s in ("pos", "ang", "trig", "rot", "kz"))
        a_s, a_m, a_p, a_n, a_t, a_pt, a_o, a_oh, a_ol = (
            sem("a_" + s) for s in ("s", "m", "p", "n", "t", "pt", "o", "oh", "ol"))
        qn = Norm(3, lambda k: od[:, k, :], lambda k: col("q_g", k), 384, "split", lambda k: cq_hi[:, k, :],
                  lambda k: cq_lo[:, k, :])
        kvn = Norm(2, lambda k: od[:, 3 + k, :], lambda k: col("kv_g", k), 256, "split", lambda k: ck_hi[:, k, :],
                   lambda k: ck_lo[:, k, :])
        ffn_pre3 = pre("ffn_g2", 1)
        ffn3 = FFN(3, (12, 10), "silu", "ffn2_1", ffn_pre3)
        final = Norm(KD, in_x, lambda k: col("final_g", k), D, "final")
        SCALE = 192.0 ** -0.5
        NA = MLA_H * NC

        def small_stage_pe(pe, st, tiles, per_unit, kts, operands, ready):
            for t in range(tiles):
                st.pe_start(pe, t)
                u, j = t // per_unit, t % per_unit
                s = (st.u0 + u) % RING
                if j == 0:
                    pe.wait_ge(split_done, st.u0 + u + 1)
                for kt in range(kts):
                    if t == 0:
                        ready(kt)
                    (ah, al), (bh, bl) = operands(s, j, kt, t)
                    pe.matmul(bank[t % 4][:], ah, bh, start=kt == 0, stop=False)
                    pe.matmul(bank[t % 4][:], ah, bl, start=False, stop=False)
                    last = pe.matmul(bank[t % 4][:], al, bh, start=False, stop=kt == kts - 1)
                if j == per_unit - 1:
                    last.then_inc(unit_done, 1)

        def small_stage_act(act, st, tiles, per_unit, dst, before=None):
            for t in range(tiles):
                act.wait_ge(unit_done, st.u0 + t // per_unit + 1)
                if before is not None:
                    before(t)
                act.activation(dst(t), bank[t % 4][:], ACT.Copy).then_inc(bank_free, 1)
                if t % per_unit == per_unit - 1:
                    split_hi(0, st.u0 + t // per_unit + RING)

        def block(m, s, b):
            return m[:, s, b * P:b * P + P]

        def mla_pe(pe):
            st = stage["od_in"]
            st.pe_first_two(pe, rhs_h, lambda kt: norm3.lo_ready(pe, kt))
            for t in range(2, 7):
                st.pe_start(pe, t)
                st.pe_tile(pe, bank[t % 4][:], t // 4, t % 4, rhs_h)
                if t == 4:
                    qn.pe(pe)
            kvn.pe(pe)
            small_stage_pe(pe, stage["uq"], 12, 2, 3,
                           lambda s, j, kt, t: ((block(whi, s, 3 * j + kt), block(wlo, s, 3 * j + kt)),
                                                (cq_hi[:, kt, :], cq_lo[:, kt, :])), lambda kt: qn.lo_ready(pe, kt))
            small_stage_pe(pe, stage["uk"], 8, 4, 2,
                           lambda s, j, kt, t: ((block(whi, s, 2 * j + kt), block(wlo, s, 2 * j + kt)),
                                                (ck_hi[:, kt, :], ck_lo[:, kt, :])), lambda kt: kvn.lo_ready(pe, kt))
            small_stage_pe(pe, stage["uv"], 8, 4, 2,
                           lambda s, j, kt, t: ((chunk(ck_hi[:, kt, :], t % 4), chunk(ck_lo[:, kt, :], t % 4)),
                                                (whi[:, s, 512 * kt:512 * kt + 512], wlo[:, s, 512 * kt:512 * kt + 512])),
                           lambda kt: None)
            pe.wait_ge(bank_free, TILE0["od_out"])

            def scores(n):
                h, b = n // NC, n % NC
                L = (b + 1) * P
                if n == 0:
                    pe.wait_ge(a_kz, 1)
                w(pe, a_p, n - 3)
                o = bank[2 + n % 4][:, 0:L]
                pe.matmul(o, chunk(qT[:, h, :], b), kT[:, h, 0:L], start=True, stop=False)
                pe.matmul(o, chunk(qT[:, 8 + h // 4, :], b), kz[:, 0, h % 4, 0:L], start=False, stop=False)
                pe.matmul(o, chunk(qT[:, 10 + h // 4, :], b), kz[:, 1, h % 4, 0:L], start=False, stop=True).then_inc(a_s, 1)

            def transposed(n):
                w(pe, a_n, n + 1)
                w(pe, a_pt, n - 1)
                for c in range(n % NC + 1):
                    last = pe.transpose(chunk(bank[6 + n % 2], c), chunk(prb[:, n % 2, :], c), ident[:])
                last.then_inc(a_t, 1)

            def values(n):
                h, b = n // NC, n % NC
                w(pe, a_pt, n + 1)
                if b == 0:
                    w(pe, a_oh, h - 1)
                    w(pe, a_ol, h - 1)
                for c in range(b + 1):
                    last = pe.matmul(chunk(bank[h % 2], b), vT[:, c, h * P:h * P + P], chunk(prt[:, n % 2, :], c),
                                     start=c == 0, stop=c == b)
                last.then_inc(a_o, 1)

            scores(0)
            scores(1)
            for n in range(NA + 1):
                if n + 2 < NA:
                    scores(n + 2)
                if n:
                    values(n - 1)
                if n < NA:
                    transposed(n)
            st = stage["od_out"]
            pe.wait_ge(a_ol, MLA_H)
            for t in range(8):
                st.pe_start(pe, t)
                st.pe_tile(pe, bank[t % 4][:], t // 4, t % 4, rhs_h)

        def mla_act(act, own):
            st = stage["od_in"]
            act.dma_start(pos_i[:], dram["positions"].broadcast_to((P, T))).then_inc(a_pos, 16)
            for t in range(7):
                st.unit_ready(act, t // 4, t % 4)
                act.activation(od[:, t, :], bank[t % 4][:], ACT.Copy).then_inc(bank_free, 1)
                st.split_ahead(t // 4, t % 4)
                if t == 2:
                    act.wait_ge(a_ang, 1)
                    act.activation(trig[:], trig[:], ACT.Sin).then_inc(a_trig, 1)
                if t == 3:
                    qn.act(act, lambda a, k: st.freed(a, k))
            kvn.act(act, lambda a, k: st.freed(a, 3 + k))
            small_stage_act(act, stage["uq"], 12, 2, lambda t: qT[:, t, :])
            small_stage_act(act, stage["uk"], 8, 4, lambda t: kT[:, t, :])
            small_stage_act(act, stage["uv"], 8, 4, lambda t: vT[:, t % 4, 512 * (t // 4):512 * (t // 4) + 512],
                            lambda t: act.wait_ge(a_kz, 1) if t == 3 else None)

            def high(h):
                act.wait_ge(a_o, NC * h + NC)
                act.activation(h_hi[:, h, :], bank[h % 2][:], ACT.Copy).then_inc(a_oh, 1)

            for n in range(NA + 2):
                if n < NA:
                    L = (n % NC + 1) * P
                    act.wait_ge(a_m, n + 1)
                    w(act, a_t, n - 1)
                    act.activation(prb[:, n % 2, 0:L], bank[2 + n % 4][:, 0:L], ACT.Exp, bias=stat[:, 1, n:n + 1],
                                   scale=SCALE, accum_out=stat[:, 2, n:n + 1]).then_inc(a_p, 1)
                if 1 <= n <= NA:
                    L = ((n - 1) % NC + 1) * P
                    act.wait_ge(a_t, n)
                    w(act, a_o, n - 2)
                    act.activation(prt[:, (n - 1) % 2, 0:L], bank[6 + (n - 1) % 2][:, 0:L], ACT.Copy).then_inc(a_pt, 1)
                if n >= 2 and (n - 2) % NC == NC - 1:
                    high((n - 2) // NC)
            split_only(act, stage["od_out"], 2)

        def mla_dve(dve, own):
            st = stage["od_in"]
            dve.wait_ge(a_pos, 16)
            own.link(dve.tensor_copy(ang[:, 0, :], pos_i[:]))
            own.link(dve.tensor_scalar(ang[:, 0, :], ang[:, 0, :], col("freq"), None, ALU.mult))
            reduced(dve, own, trig[:, 0, :], ang[:, 1, :], ang[:, 0, :], False)
            reduced(dve, own, trig[:, 1, :], ang[:, 1, :], ang[:, 0, :], True)
            dve.engine_nop().then_inc(a_ang, 1)
            qn.dve(dve)
            kvn.dve(dve)
            dve.wait_ge(a_trig, 1)
            sin, cos = trig[:, 0, :], trig[:, 1, :]

            def rotate(o1, o2, r1, r2, in_place):
                a, b = rtmp[:, 0, :], rtmp[:, 1, :]
                own(dve.tensor_tensor(a, r1, sin, ALU.mult))
                own(dve.tensor_tensor(b, r2, sin, ALU.mult))
                own.sync()
                own(dve.tensor_tensor(o1, r1, cos, ALU.mult))
                own(dve.tensor_tensor(o2, r2, cos, ALU.mult))
                own.sync()
                own(dve.tensor_tensor(o1, o1, b, ALU.subtract))
                own(dve.tensor_tensor(o2, o2, a, ALU.add))
                own.sync()

            st.freed(dve, 6)
            rotate(krot[:, 0, :], krot[:, 1, :], od[:, 5, :], od[:, 6, :], False)
            uq = stage["uq"]
            dve.wait_ge(unit_done, uq.u0 + 6)
            own.link(dve.memset(kz[:], 0.0))
            for j in range(4):
                for n in range(2):
                    r = slice(32 * j, 32 * j + 32)
                    own(dve.tensor_copy(kz[r, n, j, :], krot[r, n, :]))
            uq.freed(dve, 11)
            for m in range(2):
                rotate(qT[:, 8 + m, :], qT[:, 10 + m, :], qT[:, 8 + m, :], qT[:, 10 + m, :], True)
            dve.engine_nop().then_inc(a_kz, 1)

            def row_max(n):
                b = n % NC
                s = bank[2 + n % 4]
                dve.wait_ge(a_s, n + 1)
                own.link(dve.tensor_tensor(chunk(s, b), chunk(s, b), neg_diag[:], ALU.add))
                own.link(dve.reduce_max(stat[:, 0, n:n + 1], s[:, 0:(b + 1) * P], axis=AX.X))
                dve.tensor_scalar(stat[:, 1, n:n + 1], stat[:, 0, n:n + 1], -SCALE, None, ALU.mult).then_inc(a_m, 1)

            def low(h):
                dve.wait_ge(a_oh, h + 1)
                dve.tensor_tensor(h_lo[:, h, :], bank[h % 2][:], h_hi[:, h, :].bitcast(F32), ALU.subtract).then_inc(a_ol, 1)

            row_max(0)
            for n in range(NA + 2):
                if n + 1 < NA:
                    row_max(n + 1)
                if n < NA:
                    L = (n % NC + 1) * P
                    dve.wait_ge(a_p, n + 1)
                    own.link(dve.reciprocal(stat[:, 3, n:n + 1], stat[:, 2, n:n + 1]))
                    dve.tensor_scalar(prb[:, n % 2, 0:L], prb[:, n % 2, 0:L], stat[:, 3, n:n + 1], None,
                                      ALU.mult).then_inc(a_n, 1)
                if n >= 2 and (n - 2) % NC == NC - 1:
                    low((n - 2) // NC)
            onto_residual(dve, stage["od_out"])

        block_ctx = ctx.enter_context(nc.Block())

        @block_ctx.sync
        def _(sp):
            sp.dma_start(cols[:], dram["columns"]).then_inc(x_in, 16)
            sp.dma_start(xT[:], dram["x"]).then_inc(x_in, 16)
            for name, units, width in SEGMENTS:
                u0 = UNIT0[name]

                def load(i, k):
                    s = (u0 + k) % RING
                    w(sp, split_done, i * RING + (u0 + k - RING + 1))
                    src = dram[name][i * RING + k] if isinstance(i, int) else dram[name][bass.ds(i * RING + k, 1)].squeeze(0)
                    sp.dma_start(raw[:, s, 0:width], src).then_inc(w_in[s], 16)

                def body(i):
                    for k in range(RING):
                        load(i, k)

                if units >= RING:
                    repeat(sp, units // RING, body)
                for k in range(units % RING):
                    load(units // RING, k)
            for k in range(KD):
                sp.wait_ge(n_t, final.t0 + k + 1)
                sp.dma_start(out_dram[:, k, :], xT[:, k, :]).then_inc(out_sem, 16)
            sp.wait_ge(out_sem, 16 * KD)

        @block_ctx.gpsimd
        def _(pool):
            pm = sqb[:, 0, 0:P]
            pool.memset(ident[:], 0.0).then_inc(consts, 1)
            pool.memset(neg_diag[:], 0.0).then_inc(consts, 1)
            pool.memset(causal[:], 1.0).then_inc(consts, 1)
            pool.memset(pm, 1.0).then_inc(consts, 1)
            pool.memset(ones[:], 1.0).then_inc(consts, 1)
            pool.memset(eps[:], EPS).then_inc(consts, 1)
            pool.wait_ge(consts, 6)
            pool.affine_select(out=ident[:], in_=ident[:], compare_op=ALU.not_equal, fill=1.0, base=0, pattern=[[-1, P]],
                               channel_multiplier=1).then_inc(consts, 1)
            pool.affine_select(out=neg_diag[:], in_=neg_diag[:], compare_op=ALU.is_ge, fill=NEG, base=0,
                               pattern=[[-1, P]], channel_multiplier=1).then_inc(consts, 1)
            pool.affine_select(out=causal[:], in_=causal[:], compare_op=ALU.is_ge, fill=0.0, base=0, pattern=[[1, P]],
                               channel_multiplier=-1).then_inc(consts, 1)
            pool.affine_select(out=pm, in_=pm, compare_op=ALU.is_ge, fill=0.0, base=0, pattern=[[1, P]],
                               channel_multiplier=-1).then_inc(consts, 1)
            pool.wait_ge(consts, 10)
            pool.memset(sqb[0:64, 0, 64:P], 0.0).then_inc(consts, 1)
            pool.wait_ge(consts, 11)
            pool.tensor_copy(pair_mask[:], pm).then_inc(consts, 1)

            def low(i, c):
                s = c % RING
                w(pool, hi_done, i * RING + (c + 1))
                pool.tensor_tensor(wlo[:, s, :], raw[:, s, :], whi[:, s, :].bitcast(F32), ALU.subtract)\
                    .then_inc(split_done, 1)

            def lows(first, end):
                while first < end and first % RING:
                    low(first // RING, first % RING)
                    first += 1
                with pool.Fori(first // RING, end // RING) as i:
                    for c in range(RING):
                        low(i, c)
                for c in range(end % RING):
                    low(end // RING, c)

            for c in range(RING):
                low(0, c)
            lows(RING, UNIT0["glu"] + RING)
            s5_pool(pool)
            lows(UNIT0["glu"] + RING, UNITS)

        @block_ctx.tensor
        def _(pe):
            pe.wait_ge(consts, 12)
            norm0.pe(pe)
            ssd_pe(pe)
            ffn_pre0.pe(pe)
            ffn0.pe(pe)
            ffn_post0.pe(pe)
            norm1.pe(pe)
            lru_pe(pe)
            ffn_pre1.pe(pe)
            ffn1.pe(pe)
            ffn_post1.pe(pe)
            norm2.pe(pe)
            even_pe(pe)
            ffn_pre2.pe(pe)
            ffn2.pe(pe)
            norm3.pe(pe)
            mla_pe(pe)
            ffn_pre3.pe(pe)
            ffn3.pe(pe)
            final.pe(pe)

        def residual_ready(norm):
            return lambda eng, k: w(eng, x_new, norm.x0 + k + 1)

        @block_ctx.scalar
        def _(act):
            own = Chain(act, act_own)
            act.wait_ge(consts, 12)
            act.wait_ge(x_in, 32)
            for c in range(RING):
                split_hi(0, c)
            norm0.act(act, x_given)
            ssd_act(act, own)
            ffn_pre0.act(act, residual_ready(post0))
            ffn0.act(act)
            ffn_post0.act(act, ffn0.result_ready)
            norm1.act(act, residual_ready(ffn_post0))
            lru_act(act, own)
            ffn_pre1.act(act, residual_ready(post1))
            ffn1.act(act)
            ffn_post1.act(act, ffn1.result_ready)
            norm2.act(act, residual_ready(ffn_post1))
            even_act(act, own)
            ffn_pre2.act(act, stage["ev_out"].freed)
            ffn2.act(act)
            norm3.act(act, ffn2.result_ready)
            mla_act(act, own)
            ffn_pre3.act(act, stage["od_out"].freed)
            ffn3.act(act)
            final.act(act, ffn3.result_ready)

        @block_ctx.vector
        def _(dve):
            own = Chain(dve, dve_own)
            dve.wait_ge(consts, 12)
            dve.wait_ge(x_in, 32)
            norm0.dve(dve)
            ssd_dve(dve, own)
            ffn_pre0.dve(dve)
            ffn0.dve(dve)
            ffn_post0.dve(dve)
            norm1.dve(dve)
            lru_dve(dve, own)
            ffn_pre1.dve(dve)
            ffn1.dve(dve)
            ffn_post1.dve(dve)
            norm2.dve(dve)
            even_dve(dve, own)
            ffn_pre2.dve(dve)
            ffn2.dve(dve)
            norm3.dve(dve)
            mla_dve(dve, own)
            ffn_pre3.dve(dve)
            ffn3.dve(dve)
            final.dve(dve)


def _pack(wt, ks):
    K, N = wt.shape
    a, n, q = ks[0], N // P, len(ks)
    t = wt.reshape(q, a, P, n, P).transpose(3, 0, 2, 1, 4)
    return np.ascontiguousarray(t.reshape(n * q, P, a * P))


def _group(units, g):
    n, p, c = units.shape
    return np.ascontiguousarray(units.reshape(n // g, g, p, c).transpose(0, 2, 1, 3).reshape(n // g, p, g * c))


def _cols(v):
    return v.reshape(-1, P).T


def _taps(wt, b):
    k = wt.shape[0]
    t = np.concatenate([wt, b[None]], axis=0).reshape(k + 1, -1, P)
    return t.transpose(2, 1, 0)


def _layout(a):
    seg, c = {}, {}
    win = a["ssd_w_in"][0]
    seg["ssd_dt"] = _pack(np.tile(win[:, 5120:5152], (1, 4)), (8,))
    seg["ssd_xbc"] = _pack(win[:, 2048:5120], (8,))
    seg["ssd_z"] = _pack(win[:, 0:2048], (8,))
    seg["ssd_out"] = _pack(a["ssd_w_out"][0], (8, 8))
    for f in range(2):
        up = a["ffn_w_up"][f].reshape(D, 2, 32, P).transpose(0, 2, 1, 3)
        down = a["ffn_w_down"][f]
        for h in range(2):
            seg[f"f{f}_up{h}"] = _pack(up[:, 16 * h:16 * h + 16].reshape(D, -1), (8,))
            seg[f"f{f}_dn{h}"] = _pack(down[2048 * h:2048 * h + 2048], (8, 8))
        up2 = a["ffn_w_in_2"][f].reshape(D, 2, 22, P).transpose(0, 2, 1, 3)
        down2 = a["ffn_w_out_2"][f]
        for h, (lo, hi) in enumerate(((0, 12), (12, 22))):
            seg[f"f{f + 2}_up{h}"] = _pack(up2[:, lo:hi].reshape(D, -1), (8,))
            seg[f"f{f + 2}_dn{h}"] = _pack(down2[P * lo:P * hi], ((hi - lo) // 2,) * 2)
        t = _taps(a["ffn_conv_w"][f], a["ffn_conv_b"][f]).reshape(P, 2, 32, 4).transpose(0, 2, 1, 3)
        c[f"ffn1_{f}"] = t.reshape(P, -1)
        c[f"ffn2_{f}"] = _taps(a["ffn_conv_w_2"][f], a["ffn_conv_b_2"][f]).reshape(P, -1)
    seg["lru_in"] = _pack(a["lru_w_in"][0], (8,))
    gates = np.stack([a["lru_w_gx"][0], a["lru_w_ga"][0]], axis=1).reshape(20, P, P)
    seg["lru_gate"] = _group(gates, 4)
    seg["lru_out"] = _pack(a["lru_w_out"][0], (5, 5))
    ein = a["even_w_in_2"][0].reshape(D, 5, 512)
    seg["ev_in"] = _pack(np.concatenate([ein[:, n] for n in (4, 1, 2, 0, 3)], axis=1), (8,))
    seg["glu"] = _group(_pack(a["s5_w_glu_2"][0], (4,)), 2)
    seg["ev_out"] = _pack(a["even_w_out_2"][0], (8,))
    oin = a["odd_w_in_2"][0]
    r1, r2 = oin[:, 640:672], oin[:, 672:704]
    seg["od_in"] = _pack(np.concatenate([oin[:, 0:640]] + [r1] * 4 + [r2] * 4, axis=1), (8,))
    uq = a["mla_w_uq_2"][0].reshape(384, 8, 192)
    seg["uq"] = _group(_pack(np.concatenate([uq[:, :, 0:128].reshape(384, -1), uq[:, :, 128:160].reshape(384, -1),
                                             uq[:, :, 160:192].reshape(384, -1)], axis=1), (3,)), 2)
    ukv = a["mla_w_ukv_2"][0].reshape(256, 8, 256)
    seg["uk"] = _group(_pack(ukv[:, :, 0:128].reshape(256, -1), (2,)), 4)
    uv = ukv[:, :, 128:256].reshape(2, P, 2, 512).transpose(2, 1, 0, 3)
    seg["uv"] = np.ascontiguousarray(uv.reshape(2, P, 1024))
    seg["od_out"] = _pack(a["odd_w_out_2"][0], (8,))

    for name, key in (("mix_pre", "norm_mix_pre"), ("mix_post", "norm_mix_post"), ("ffn_pre", "norm_ffn_pre"),
                      ("ffn_post", "norm_ffn_post"), ("mix_g2", "norm_mix_g_2"), ("ffn_g2", "norm_ffn_g_2"),
                      ("final_g", "final_norm_g_2"), ("ssd_norm", "ssd_norm"), ("lru_bgx", "lru_b_gx"),
                      ("lru_bga", "lru_b_ga"), ("lru_lam", "lru_lambda"), ("lru_bout", "lru_b_out"),
                      ("lb", "hgrn_lb_logits_2"), ("hgrn_g", "hgrn_norm_g_2"), ("s5_d", "s5_d_2"),
                      ("b_glu", "s5_b_glu_2"), ("q_g", "mla_q_norm_g_2"), ("kv_g", "mla_kv_norm_g_2")):
        c[name] = _cols(a[key])
    c["ssd_conv"] = _taps(a["ssd_conv_w"][0], a["ssd_conv_b"][0]).reshape(P, -1)
    c["lru_conv"] = _taps(a["lru_conv_w"][0], a["lru_conv_b"][0]).reshape(P, -1)
    c["ssd_d"] = _cols(np.repeat(a["ssd_d"][0], 64))
    c["dt_bias"] = np.tile(a["ssd_dt_bias"][0], 4)[:, None]
    c["a_log"] = np.tile(a["ssd_a_log"][0], 4)[:, None]
    c["lru_by"] = _cols(a["lru_b_in"][0, 0:LRU_W])
    c["lru_bx"] = _cols(a["lru_b_in"][0, LRU_W:])
    c["s5_are"] = _cols(a["s5_a_re_2"][0])
    c["s5_aim"] = _cols(a["s5_a_im_2"][0])
    c["s5_logdt"] = _cols(np.repeat(a["s5_log_dt_2"][0], 64))
    freqs = np.power(np.float32(10000.0), -np.arange(0, 64, 2, dtype=np.float32) / np.float32(64))
    c["freq"] = np.tile(freqs.astype(np.float32), 4)[:, None]
    seg["columns"] = np.ascontiguousarray(np.concatenate([c[n] for n, _ in COLUMNS], axis=1))
    seg["x"] = np.ascontiguousarray(a["x"][0].T.reshape(KD, P, T).transpose(1, 0, 2))
    seg["positions"] = np.ascontiguousarray(a["positions_2"])
    b = np.stack([a["s5_b_re_2"][0], a["s5_b_im_2"][0]])
    c2 = np.stack([a["s5_c_re_2"][0], a["s5_c_im_2"][0]]).transpose(0, 1, 3, 2)
    for name, m in (("s5_b", b), ("s5_c", c2)):
        m = m.reshape(2, S5T, 2, 64, 16)
        wide = np.zeros((2, 64, 2, S5T, 2, 16), dtype=m.dtype)
        for e in range(2):
            wide[e, :, :, :, e, :] = m[:, :, e].transpose(2, 0, 1, 3)
        seg[name] = wide.reshape(P, 2, S5T, 32)
    return seg


def kernel(**inputs):
    import concourse.bacc as bacc
    from concourse.bass_utils import run_bass_kernel_spmd

    arrays = _layout({k: np.asarray(v) for k, v in inputs.items()})
    nc = bacc.Bacc("TRN2", target_bir_lowering=False, num_devices=1)
    dram = {}
    for name, v in arrays.items():
        dram[name] = nc.dram_tensor(f"in_{name}", v.shape, mybir.dt.from_np(v.dtype), kind="ExternalInput").ap()
    out = nc.dram_tensor("out_x", (P, KD, T), F32, kind="ExternalOutput").ap()
    build_program(nc, dram, out)
    r = run_bass_kernel_spmd(nc, [{f"in_{k}": v for k, v in arrays.items()}], core_ids=[0])
    y = r.results[0]["out_x"]
    return np.ascontiguousarray(y.transpose(2, 1, 0).reshape(1, T, D))
```
